# Optimizing a Trainium2 kernel written in Bass

```python
import jax, jax.numpy as jnp
from jax import lax
import numpy as np

D_MODEL = 1024
BATCH = 1
SEQ = 2048
DEPTH = 1

HEAD_DIM = 64
MIX_WIDTH = D_MODEL
ATTN_WIDTH = MIX_WIDTH // 2
ATTN_Q_HEADS = ATTN_WIDTH // HEAD_DIM
ATTN_KV_HEADS = 2
KV_WIDTH = ATTN_KV_HEADS * HEAD_DIM
WINDOW = 128
ATTN_BLOCK = 128
RWKV_WIDTH = MIX_WIDTH // 4
RWKV_HEADS = RWKV_WIDTH // HEAD_DIM
DECAY_LORA = 64
ICLR_LORA = 64
RWKV_LN_EPS = 64e-5
GLA_VAL_WIDTH = MIX_WIDTH // 4
GLA_HEADS = 4
GLA_VAL_DIM = GLA_VAL_WIDTH // GLA_HEADS
GLA_KEY_WIDTH = GLA_VAL_WIDTH // 2
GLA_KEY_DIM = GLA_KEY_WIDTH // GLA_HEADS
GLA_GATE_LORA = 16
GLA_GATE_NORMALIZER = 16.0
GLA_CHUNK = 64
IN_SPLITS = (ATTN_WIDTH, KV_WIDTH, KV_WIDTH, ATTN_WIDTH,
             3 * RWKV_WIDTH, RWKV_WIDTH,
             GLA_KEY_WIDTH, GLA_KEY_WIDTH, GLA_VAL_WIDTH, GLA_VAL_WIDTH)
IN_WIDTH = 2 * ATTN_WIDTH + 2 * KV_WIDTH + 4 * RWKV_WIDTH + 2 * GLA_KEY_WIDTH + 2 * GLA_VAL_WIDTH
NORM_EPS = 1e-6


def _rmsnorm(x, g):
    xf = x.astype(jnp.float32)
    y = xf * lax.rsqrt(jnp.mean(xf * xf, axis=-1, keepdims=True) + NORM_EPS)
    return (y * g.astype(jnp.float32)).astype(x.dtype)

def _shift(z):
    return jnp.pad(z, ((0, 0), (1, 0), (0, 0)))[:, :-1]

def _sliding_window_attention(q, k, v, sinks):
    B, T, Hq, D = q.shape
    Hkv = k.shape[2]
    G = Hq // Hkv
    nb = T // ATTN_BLOCK
    qb = q.reshape(B, nb, ATTN_BLOCK, Hkv, G, D)

    def band(z):
        zb = z.reshape(B, nb, ATTN_BLOCK, Hkv, D)
        prev = jnp.concatenate([jnp.zeros_like(zb[:, :1]), zb[:, :-1]], axis=1)
        return jnp.concatenate([prev, zb], axis=2)

    kb, vb = band(k), band(v)
    s = jnp.einsum('bnqhgd,bnkhd->bnhgqk', qb, kb,
                   preferred_element_type=jnp.float32) * (D ** -0.5)
    qi = jnp.arange(ATTN_BLOCK)[:, None]
    kj = jnp.arange(2 * ATTN_BLOCK)[None, :]
    dist = qi - kj + ATTN_BLOCK
    key_pos = jnp.arange(nb)[:, None, None] * ATTN_BLOCK + kj[None] - ATTN_BLOCK
    valid = (dist >= 0) & (dist < WINDOW) & (key_pos >= 0)
    slopes = 2.0 ** (-8.0 * jnp.arange(1, Hq + 1, dtype=jnp.float32) / Hq)
    s = s - slopes.reshape(Hkv, G)[:, :, None, None] * dist.astype(jnp.float32)
    s = jnp.where(valid[None, :, None, None], s, -jnp.inf)
    sink = jnp.broadcast_to(sinks.astype(jnp.float32).reshape(Hkv, G)[:, :, None, None],
                            s.shape[:-1] + (1,))
    p = jax.nn.softmax(jnp.concatenate([s, sink], axis=-1), axis=-1)[..., :-1]
    o = jnp.einsum('bnhgqk,bnkhd->bnqhgd', p.astype(v.dtype), vb)
    return o.reshape(B, T, Hq * D)

def _rwkv7_mixer(h, r, k, v, mu_w, mu_a, w0, w1, w2, a0, a1, a2, k_k, k_a, r_k, ln_w, ln_b):
    B, T, _ = h.shape
    f32 = jnp.float32
    h_prev = _shift(h)
    xw = h + (h_prev - h) * mu_w
    xa = h + (h_prev - h) * mu_a
    w = -jax.nn.softplus(-(w0 + jnp.tanh(xw @ w1) @ w2).astype(f32)) - 0.5
    decay = jnp.exp(-jnp.exp(w))
    a = jax.nn.sigmoid((a0 + (xa @ a1) @ a2).astype(f32))
    r, k, v = r.astype(f32), k.astype(f32), v.astype(f32)
    heads = lambda z: z.reshape(B, T, RWKV_HEADS, HEAD_DIM)
    kk = heads(k * k_k.astype(f32))
    kk = kk / jnp.maximum(jnp.linalg.norm(kk, axis=-1, keepdims=True), 1e-12)
    k = k * (1.0 + (a - 1.0) * k_a.astype(f32))

    def step(S, inp):
        r_t, w_t, k_t, v_t, kk_t, a_t = inp
        sa = jnp.einsum('bhvk,bhk->bhv', S, -kk_t)
        S = (S * w_t[:, :, None, :] + sa[..., None] * (kk_t * a_t)[:, :, None, :]
             + v_t[..., None] * k_t[:, :, None, :])
        return S, jnp.einsum('bhvk,bhk->bhv', S, r_t)

    tm = lambda z: jnp.moveaxis(z, 1, 0)
    S0 = jnp.zeros((B, RWKV_HEADS, HEAD_DIM, HEAD_DIM), f32)
    _, y = lax.scan(step, S0, (tm(heads(r)), tm(heads(decay)), tm(heads(k)), tm(heads(v)),
                               tm(kk), tm(heads(a))))
    y = jnp.moveaxis(y, 0, 1)
    mean = jnp.mean(y, axis=-1, keepdims=True)
    var = jnp.mean(jnp.square(y - mean), axis=-1, keepdims=True)
    y = ((y - mean) * lax.rsqrt(var + RWKV_LN_EPS)).reshape(B, T, RWKV_WIDTH)
    y = y * ln_w.astype(f32) + ln_b.astype(f32)
    bonus = jnp.sum(heads(r) * heads(k) * r_k.astype(f32), axis=-1, keepdims=True) * heads(v)
    return (y + bonus.reshape(B, T, RWKV_WIDTH)).astype(h.dtype)

def _gla_mixer(h, q, k, v, gk1, gk2, gk_b, norm_w):
    B, T, _ = h.shape
    f32 = jnp.float32
    n = T // GLA_CHUNK
    gk = jax.nn.log_sigmoid(((h @ gk1) @ gk2 + gk_b).astype(f32)) / GLA_GATE_NORMALIZER

    def chunks(z, d):
        return z.reshape(B, n, GLA_CHUNK, GLA_HEADS, d).transpose(1, 0, 3, 2, 4).astype(f32)

    qc = chunks(q, GLA_KEY_DIM) * (GLA_KEY_DIM ** -0.5)
    kc = chunks(k, GLA_KEY_DIM)
    vc = chunks(v, GLA_VAL_DIM)
    gc = chunks(gk, GLA_KEY_DIM)
    causal = jnp.tril(jnp.ones((GLA_CHUNK, GLA_CHUNK), bool))

    def step(S, inp):
        q_c, k_c, v_c, g_c = inp
        b = jnp.cumsum(g_c, axis=2)
        diff = b[:, :, :, None, :] - b[:, :, None, :, :]
        diff = jnp.where(causal[:, :, None], diff, -jnp.inf)
        A = jnp.einsum('bhid,bhjd,bhijd->bhij', q_c, k_c, jnp.exp(diff))
        o = A @ v_c + jnp.einsum('bhid,bhdv->bhiv', q_c * jnp.exp(b), S)
        b_last = b[:, :, -1:, :]
        S = (jnp.exp(b_last[:, :, 0, :])[..., None] * S
             + jnp.einsum('bhjd,bhjv->bhdv', k_c * jnp.exp(b_last - b), v_c))
        return S, o

    S0 = jnp.zeros((B, GLA_HEADS, GLA_KEY_DIM, GLA_VAL_DIM), f32)
    _, o = lax.scan(step, S0, (qc, kc, vc, gc))
    o = o.transpose(1, 0, 3, 2, 4).reshape(B, T, GLA_HEADS, GLA_VAL_DIM)
    o = o * lax.rsqrt(jnp.mean(o * o, axis=-1, keepdims=True) + 1e-5) * norm_w.astype(f32)
    return o.reshape(B, T, GLA_VAL_WIDTH).astype(h.dtype)

def _hybrid_layer(x, c_act, ada_w, ada_b, g_pre, g_post, w_in, w_out, sinks,
                  mu_rkv, mu_w, mu_a, w0, w1, w2, a0, a1, a2, k_k, k_a, r_k, ln_w, ln_b,
                  gk1, gk2, gk_b, gla_norm_w):
    B, T, _ = x.shape
    shift, scale, gate = jnp.split(c_act @ ada_w + ada_b, 3, axis=-1)
    h = _rmsnorm(x, g_pre) * (1.0 + scale[:, None]) + shift[:, None]
    proj = h @ w_in
    aq, ak, av, ag, rkv, rg, gq, gkk, gv, gg = jnp.split(proj, list(np.cumsum(IN_SPLITS)[:-1]), axis=-1)
    attn = _sliding_window_attention(aq.reshape(B, T, ATTN_Q_HEADS, HEAD_DIM),
                                     ak.reshape(B, T, ATTN_KV_HEADS, HEAD_DIM),
                                     av.reshape(B, T, ATTN_KV_HEADS, HEAD_DIM), sinks)
    attn = attn * jax.nn.silu(ag)
    rkv = rkv + (_shift(rkv) - rkv) * mu_rkv
    rr, rk, rv = jnp.split(rkv, 3, axis=-1)
    rwkv = _rwkv7_mixer(h, rr, rk, rv, mu_w, mu_a, w0, w1, w2, a0, a1, a2, k_k, k_a, r_k, ln_w, ln_b)
    rwkv = rwkv * jax.nn.silu(rg)
    gla = _gla_mixer(h, gq, gkk, gv, gk1, gk2, gk_b, gla_norm_w) * jax.nn.silu(gg)
    y = jnp.concatenate([attn, rwkv, gla], axis=-1) @ w_out
    return x + gate[:, None] * _rmsnorm(y, g_post)

def first_inputs(seed: int = 0) -> dict:
    key = jax.random.key(seed)
    ks = jax.random.split(key, 32)
    nrm = lambda k, shape, s: s * jax.random.normal(k, shape, jnp.float32)
    uni = lambda k, shape, lo, hi: jax.random.uniform(k, shape, jnp.float32, lo, hi)
    D, L = D_MODEL, DEPTH
    return {
        "x": nrm(ks[0], (BATCH, SEQ, D), 1.0),
        "c": nrm(ks[1], (BATCH, D), 1.0),
        "ada_w": nrm(ks[2], (L, D, 3 * D), 0.5 * D ** -0.5),
        "ada_b": nrm(ks[3], (L, 3 * D), 0.02),
        "norm_pre": 1.0 + nrm(ks[4], (L, D), 0.05),
        "norm_post": 1.0 + nrm(ks[5], (L, D), 0.05),
        "w_in": nrm(ks[6], (L, D, IN_WIDTH), D ** -0.5),
        "w_out": nrm(ks[7], (L, MIX_WIDTH, D), MIX_WIDTH ** -0.5),
        "attn_sinks": nrm(ks[8], (L, ATTN_Q_HEADS), 0.5),
        "rwkv_mu_rkv": uni(ks[9], (L, 3 * RWKV_WIDTH), 0.0, 1.0),
        "rwkv_mu_w": uni(ks[10], (L, D), 0.0, 1.0),
        "rwkv_mu_a": uni(ks[11], (L, D), 0.0, 1.0),
        "rwkv_w0": uni(ks[12], (L, RWKV_WIDTH), -4.0, 1.0),
        "rwkv_w1": nrm(ks[13], (L, D, DECAY_LORA), D ** -0.5),
        "rwkv_w2": nrm(ks[14], (L, DECAY_LORA, RWKV_WIDTH), 0.5 * DECAY_LORA ** -0.5),
        "rwkv_a0": nrm(ks[15], (L, RWKV_WIDTH), 0.1),
        "rwkv_a1": nrm(ks[16], (L, D, ICLR_LORA), D ** -0.5),
        "rwkv_a2": nrm(ks[17], (L, ICLR_LORA, RWKV_WIDTH), 0.5 * ICLR_LORA ** -0.5),
        "rwkv_k_k": 0.85 + nrm(ks[18], (L, RWKV_WIDTH), 0.05),
        "rwkv_k_a": 1.0 + nrm(ks[19], (L, RWKV_WIDTH), 0.05),
        "rwkv_r_k": nrm(ks[20], (L, RWKV_HEADS, HEAD_DIM), 0.1),
        "rwkv_ln_w": 1.0 + nrm(ks[21], (L, RWKV_WIDTH), 0.05),
        "rwkv_ln_b": nrm(ks[22], (L, RWKV_WIDTH), 0.02),
        "gla_gk1": nrm(ks[23], (L, D, GLA_GATE_LORA), D ** -0.5),
        "gla_gk2": nrm(ks[24], (L, GLA_GATE_LORA, GLA_KEY_WIDTH), GLA_GATE_LORA ** -0.5),
        "gla_gk_b": nrm(ks[25], (L, GLA_KEY_WIDTH), 0.1),
        "gla_norm_w": 1.0 + nrm(ks[26], (L, GLA_VAL_DIM), 0.05),
    }

def first_block(x, c, ada_w, ada_b, norm_pre, norm_post, w_in, w_out, attn_sinks,
              rwkv_mu_rkv, rwkv_mu_w, rwkv_mu_a, rwkv_w0, rwkv_w1, rwkv_w2,
              rwkv_a0, rwkv_a1, rwkv_a2, rwkv_k_k, rwkv_k_a, rwkv_r_k, rwkv_ln_w, rwkv_ln_b,
              gla_gk1, gla_gk2, gla_gk_b, gla_norm_w):
    c_act = jax.nn.silu(c)
    for l in range(DEPTH):
        x = _hybrid_layer(x, c_act, ada_w[l], ada_b[l], norm_pre[l], norm_post[l], w_in[l], w_out[l],
                          attn_sinks[l], rwkv_mu_rkv[l], rwkv_mu_w[l], rwkv_mu_a[l],
                          rwkv_w0[l], rwkv_w1[l], rwkv_w2[l], rwkv_a0[l], rwkv_a1[l], rwkv_a2[l],
                          rwkv_k_k[l], rwkv_k_a[l], rwkv_r_k[l], rwkv_ln_w[l], rwkv_ln_b[l],
                          gla_gk1[l], gla_gk2[l], gla_gk_b[l], gla_norm_w[l])
    return x


CHUNK = 64
Q_BLOCK = 128
EPS = 1e-6

N_HEADS_A = 8
N_KV_A = 2
ROT_DIM = HEAD_DIM // 4
ROPE_THETA = 500000.0
N_IDX_HEADS = 8
IDX_DIM = 32
IDX_ROT_DIM = IDX_DIM // 4
TOPK_MAX = 256
WIDTH_A = N_HEADS_A * HEAD_DIM

POOL_WINDOWS = (2, 4, 8, 16)
N_POOL_GROUPS = 4
POOL_GROUP_DIM = 128
WIDTH_B = N_POOL_GROUPS * POOL_GROUP_DIM

N_BRANCHES = 2

SPLIT_SIZES = (
    WIDTH_A,
    N_KV_A * HEAD_DIM,
    N_KV_A * HEAD_DIM,
    N_IDX_HEADS * IDX_DIM,
    IDX_DIM,
    N_IDX_HEADS,
    WIDTH_A,
    WIDTH_B,
    WIDTH_B,
    N_BRANCHES * D_MODEL,
)
D_IN = int(sum(SPLIT_SIZES))
SPLIT_POINTS = [int(s) for s in np.cumsum(SPLIT_SIZES)[:-1]]


def rms_norm(t, g):
    tf = t.astype(jnp.float32)
    tf = tf * lax.rsqrt(jnp.mean(tf * tf, axis=-1, keepdims=True) + EPS)
    return (tf * g.astype(jnp.float32)).astype(t.dtype)

def rope_tables(positions, rot_dim):
    half = rot_dim // 2
    inv_freq = ROPE_THETA ** (-jnp.arange(half, dtype=jnp.float32) / half)
    ang = positions.astype(jnp.float32)[..., None] * inv_freq
    return jnp.cos(ang), jnp.sin(ang)

def apply_partial_rope(t, cos, sin):
    half = cos.shape[-1]
    tf = t.astype(jnp.float32)
    c = cos[:, :, None, :]
    s = sin[:, :, None, :]
    t1 = tf[..., :half]
    t2 = tf[..., half:2 * half]
    out = jnp.concatenate([t1 * c - t2 * s, t1 * s + t2 * c, tf[..., 2 * half:]], axis=-1)
    return out.astype(t.dtype)

def dsa_attention(q, k, v, qi, ki, wi, k_sel):
    B, S = q.shape[0], q.shape[1]
    n_blocks = S // Q_BLOCK
    rep = N_HEADS_A // N_KV_A
    key_chunk = jnp.arange(S) // CHUNK
    scale = HEAD_DIM ** -0.5

    def block(i):
        start = i * Q_BLOCK
        qb = lax.dynamic_slice_in_dim(q, start, Q_BLOCK, axis=1)
        qib = lax.dynamic_slice_in_dim(qi, start, Q_BLOCK, axis=1)
        wib = lax.dynamic_slice_in_dim(wi, start, Q_BLOCK, axis=1)
        q_chunk = (start + jnp.arange(Q_BLOCK)) // CHUNK
        allowed = key_chunk[None, :] <= q_chunk[:, None]
        logits = jnp.einsum('bqhd,bsd->bqhs', qib, ki)
        iscore = jnp.einsum('bqhs,bqh->bqs', jax.nn.relu(logits), wib).astype(jnp.float32)
        iscore = jnp.where(allowed[None], iscore, -jnp.inf)
        _, idx = lax.top_k(iscore, k_sel)
        valid = key_chunk[idx] <= q_chunk[None, :, None]
        kg = jax.vmap(lambda kb, ib: kb[ib])(k, idx)
        vg = jax.vmap(lambda vb, ib: vb[ib])(v, idx)
        qg = qb.reshape(B, Q_BLOCK, N_KV_A, rep, HEAD_DIM)
        s = jnp.einsum('bqgrd,bqkgd->bqgrk', qg, kg).astype(jnp.float32) * scale
        s = jnp.where(valid[:, :, None, None, :], s, -jnp.inf)
        p = jax.nn.softmax(s, axis=-1).astype(v.dtype)
        o = jnp.einsum('bqgrk,bqkgd->bqgrd', p, vg)
        return o.reshape(B, Q_BLOCK, N_HEADS_A * HEAD_DIM)

    out = lax.map(block, jnp.arange(n_blocks))
    return out.transpose(1, 0, 2, 3).reshape(B, S, N_HEADS_A * HEAD_DIM)

def multiscale_pool(u, pool_w, pool_scale):
    B, S = u.shape[0], u.shape[1]
    ug = u.astype(jnp.float32).reshape(B, S, N_POOL_GROUPS, POOL_GROUP_DIM)
    cs = jnp.cumsum(ug, axis=1)
    t = jnp.arange(S)
    outs = []
    for g, w in enumerate(POOL_WINDOWS):
        c = cs[:, :, g]
        lagged = jnp.pad(c, ((0, 0), (w, 0), (0, 0)))[:, :S]
        count = jnp.minimum(t + 1, w).astype(jnp.float32)[None, :, None]
        outs.append((c - lagged) / count - ug[:, :, g])
    pooled = jnp.stack(outs, axis=2).astype(u.dtype)
    mixed = jnp.einsum('bsgc,gcd->bsgd', pooled, pool_w)
    return mixed.reshape(B, S, WIDTH_B) * pool_scale

def second_inputs(seed: int = 0) -> dict:
    key = jax.random.key(seed)
    ks = jax.random.split(key, 13)
    f32 = jnp.float32
    x = jax.random.normal(ks[0], (BATCH, SEQ, D_MODEL), f32)
    offsets = jax.random.randint(ks[1], (BATCH, 1), 0, 100000, dtype=jnp.int32)
    positions = (jnp.arange(SEQ, dtype=jnp.int32)[None, :] + offsets).astype(jnp.int32)
    norm_g = 1.0 + 0.02 * jax.random.normal(ks[2], (DEPTH, D_MODEL), f32)
    w_in = jax.random.normal(ks[3], (DEPTH, D_MODEL, D_IN), f32) * D_MODEL ** -0.5
    merge_bias = 0.02 * jax.random.normal(ks[4], (DEPTH, N_BRANCHES, D_MODEL), f32)
    q_norm_g = 1.0 + 0.02 * jax.random.normal(ks[5], (DEPTH, HEAD_DIM), f32)
    k_norm_g = 1.0 + 0.02 * jax.random.normal(ks[6], (DEPTH, HEAD_DIM), f32)
    pool_w = jax.random.normal(ks[7], (DEPTH, N_POOL_GROUPS, POOL_GROUP_DIM, POOL_GROUP_DIM), f32) * POOL_GROUP_DIM ** -0.5
    pool_scale = 1.0 + 0.1 * jax.random.normal(ks[8], (DEPTH, WIDTH_B), f32)
    w_branch_a = jax.random.normal(ks[9], (DEPTH, WIDTH_A, D_MODEL), f32) * WIDTH_A ** -0.5
    w_branch_b = jax.random.normal(ks[10], (DEPTH, WIDTH_B, D_MODEL), f32) * WIDTH_B ** -0.5
    w_out = jax.random.normal(ks[11], (DEPTH, D_MODEL, D_MODEL), f32) * D_MODEL ** -0.5
    return {"x": x, "positions": positions, "norm_g": norm_g, "w_in": w_in,
            "merge_bias": merge_bias, "q_norm_g": q_norm_g, "k_norm_g": k_norm_g,
            "pool_w": pool_w, "pool_scale": pool_scale, "w_branch_a": w_branch_a,
            "w_branch_b": w_branch_b, "w_out": w_out}

def second_block(x, positions, norm_g, w_in, merge_bias, q_norm_g, k_norm_g, pool_w, pool_scale,
              w_branch_a, w_branch_b, w_out):
    B, S = x.shape[0], x.shape[1]
    k_sel = min(TOPK_MAX, S // 4)
    cos_a, sin_a = rope_tables(positions, ROT_DIM)
    cos_i, sin_i = rope_tables(positions, IDX_ROT_DIM)
    for layer in range(DEPTH):
        h = rms_norm(x, norm_g[layer])
        proj = h @ w_in[layer]
        q, k, v, qi, ki, wi, z_a, u_b, z_b, gates = jnp.split(proj, SPLIT_POINTS, axis=-1)

        q = q.reshape(B, S, N_HEADS_A, HEAD_DIM)
        k = k.reshape(B, S, N_KV_A, HEAD_DIM)
        v = v.reshape(B, S, N_KV_A, HEAD_DIM)
        q = apply_partial_rope(rms_norm(q, q_norm_g[layer]), cos_a, sin_a)
        k = apply_partial_rope(rms_norm(k, k_norm_g[layer]), cos_a, sin_a)
        qi = apply_partial_rope(qi.reshape(B, S, N_IDX_HEADS, IDX_DIM), cos_i, sin_i) * (IDX_DIM ** -0.5)
        ki = apply_partial_rope(ki[:, :, None, :], cos_i, sin_i)[:, :, 0, :]
        wi = wi * (N_IDX_HEADS ** -0.5)
        a = dsa_attention(q, k, v, qi, ki, wi, k_sel) * jax.nn.silu(z_a)

        b = multiscale_pool(u_b, pool_w[layer], pool_scale[layer]) * jax.nn.silu(z_b)

        g = jax.nn.sigmoid(gates.reshape(B, S, N_BRANCHES, D_MODEL) + merge_bias[layer])
        y = g[:, :, 0] * (a @ w_branch_a[layer]) + g[:, :, 1] * (b @ w_branch_b[layer])
        x = x + y @ w_out[layer]
    return x


def setup_inputs(seed=0):
    out = dict(first_inputs(seed))
    for name, value in second_inputs(seed + 1).items():
        if name != "x":
            out[name + "_2"] = value
    return out


def reference(
    x, c, ada_w, ada_b, norm_pre, norm_post, w_in, w_out, attn_sinks, rwkv_mu_rkv, rwkv_mu_w,
    rwkv_mu_a, rwkv_w0, rwkv_w1, rwkv_w2, rwkv_a0, rwkv_a1, rwkv_a2, rwkv_k_k, rwkv_k_a,
    rwkv_r_k, rwkv_ln_w, rwkv_ln_b, gla_gk1, gla_gk2, gla_gk_b, gla_norm_w, positions_2,
    norm_g_2, w_in_2, merge_bias_2, q_norm_g_2, k_norm_g_2, pool_w_2, pool_scale_2,
    w_branch_a_2, w_branch_b_2, w_out_2,
):
    x = first_block(
        x, c, ada_w, ada_b, norm_pre, norm_post, w_in, w_out, attn_sinks, rwkv_mu_rkv,
        rwkv_mu_w, rwkv_mu_a, rwkv_w0, rwkv_w1, rwkv_w2, rwkv_a0, rwkv_a1, rwkv_a2, rwkv_k_k,
        rwkv_k_a, rwkv_r_k, rwkv_ln_w, rwkv_ln_b, gla_gk1, gla_gk2, gla_gk_b, gla_norm_w,
    )
    return second_block(
        x, positions_2, norm_g_2, w_in_2, merge_bias_2, q_norm_g_2, k_norm_g_2, pool_w_2,
        pool_scale_2, w_branch_a_2, w_branch_b_2, w_out_2,
    )


_drawn_inputs = setup_inputs


def setup_inputs(seed=0):
    import zlib

    import numpy as np

    out = dict(_drawn_inputs(seed))
    spreads = {}
    factors = {'norm_post': 3.296,
     'attn_sinks': 8.0,
     'rwkv_mu_w': 8.0,
     'rwkv_mu_a': 2.94,
     'rwkv_w1': 3.865,
     'rwkv_w2': 3.975,
     'rwkv_a0': 6.757,
     'rwkv_k_k': 8.0,
     'rwkv_k_a': 4.717,
     'rwkv_ln_w': 5.855,
     'rwkv_ln_b': 8.0,
     'gla_gk_b': 5.833,
     'gla_norm_w': 5.874,
     'norm_g_2': 6.221,
     'merge_bias_2': 8.0,
     'q_norm_g_2': 8.0,
     'k_norm_g_2': 8.0}
    for name, (base, spread) in spreads.items():
        noise = np.random.default_rng([zlib.crc32(name.encode()), seed]).standard_normal(out[name].shape)
        drawn = base * np.exp(spread * noise) if base else spread * noise
        out[name] = __import__('jax').numpy.asarray(drawn.astype(out[name].dtype))
    for name, factor in factors.items():
        out[name] = (out[name] * factor).astype(out[name].dtype)
    return out
```

```python
import concourse.bass as bass
from concourse import mybir
from contextlib import ExitStack
import numpy as np

F32 = mybir.dt.float32
I32 = mybir.dt.int32
U32 = mybir.dt.uint32
ALU = mybir.AluOpType
ACT = mybir.ActivationFunctionType
AX = mybir.AxisListType

P = 128
D = 1024
KD = D // P
SEQ = 2048
TILES = SEQ // P
HEAD = 64
EPS = 1e-6
NEG = -1.0e30

A_HEADS, A_KV = 8, 2
C_AQ, C_AK, C_AV, C_AG = 0, 512, 640, 768
C_RKV, C_RG = 1280, 2048
C_GQ, C_GK, C_GV, C_GG = 2304, 2432, 2560, 2816
IN1 = 3072
R_HEADS, R_W, R_CHUNK = 4, 256, 64
RWKV_LN_EPS = 64e-5
G_HEADS, G_KEY, G_VAL = 4, 32, 64
LEVELS = 7
INV_LEVELS = 6


class Signals(dict):

    def __init__(self, nc, phase):
        super().__init__()
        self.nc, self.phase = nc, phase

    def __missing__(self, name):
        self[name] = self.nc.alloc_semaphore(f"{self.phase}_{name}")
        return self[name]

    def close(self):
        self.nc.clear_and_free_semaphores(list(self.values()))
        self.nc.all_engine_barrier()


class Chain:

    def __init__(self, eng, sem):
        self.eng, self.sem, self.count = eng, sem, 0

    def link(self, ins):
        self.count += 1
        ins.then_inc(self.sem, 1)
        self.eng.wait_ge(self.sem, self.count)

    def start_over(self):
        self.eng.sem_clear(self.sem)
        self.count = 0


def row(ap_row, n=P):
    return ap_row.broadcast_to([n, ap_row.shape[1]])


def spread(ap, shape):
    return ap.broadcast_to(shape)


def adaptive_norm(nc, A, keep, const):
    g1, sh = keep["scale_ch"], keep["shift_ch"]
    with ExitStack() as ctx:
        sb = lambda n, s: ctx.enter_context(nc.sbuf_tensor("ad_" + n, s, F32))
        S = Signals(nc, "ad")
        ada = sb("w", [P, KD, 3 * D])
        cc, ce, ca = sb("c", [P, KD]), sb("ce", [P, KD]), sb("ca", [P, KD])
        cb = sb("cb", [P, KD, P])
        b_ch, npre = sb("b_ch", [P, 2 * KD]), sb("npre", [P, KD])
        b_row, np_row, gp = sb("b_row", [P, D]), sb("np_row", [P, D]), sb("gp", [P, D])
        ps = ctx.enter_context(nc.psum_tensor("ad_ps", [P, 512], F32))
        pg = ctx.enter_context(nc.psum_tensor("ad_pg", [P, 1024], F32))
        with nc.Block() as block:
            @block.sync
            def _(sp):
                sp.dma_start(cc[:, :], A["c_ch"]).then_inc(S["c_loaded"], 16)
                src = A["ada_w"][0].rearrange("(k p) n -> p k n", p=P)
                for k in range(KD):
                    sp.dma_start(ada[:, k, :], src[:, k, :]).then_inc(S["w_loaded"], 16)
                sp.dma_start(b_ch[:, :], A["ada_b_ch"][:, 0:2 * KD]).then_inc(S["small_loaded"], 16)
                sp.dma_start(npre[:, :], A["norm_pre_ch"]).then_inc(S["small_loaded"], 16)
                sp.dma_start(b_row[:, :], row(A["ada_b"][0:1, 2 * D:3 * D])).then_inc(S["small_loaded"], 16)
                sp.dma_start(np_row[:, :], row(A["norm_post"][0:1, :])).then_inc(S["small_loaded"], 16)
                sp.wait_ge(S["gate_ready"], 1)
                sp.dma_start(keep["gate_row"], gp[:, :]).then_inc(S["gate_stored"], 16)
                sp.wait_ge(S["gate_stored"], 16)

            @block.scalar
            def _(act):
                act.wait_ge(S["c_loaded"], 16)
                nc.scalar.activation(ce[:, :], cc[:, :], ACT.Exp, scale=-1.0).then_inc(S["exp_done"], 1)

            @block.vector
            def _(dve):
                ch = Chain(dve, S["dve_step"])
                dve.wait_ge(S["exp_done"], 1)
                ch.link(nc.vector.tensor_scalar(ce[:, :], ce[:, :], 1.0, None, ALU.add))
                ch.link(nc.vector.reciprocal(ce[:, :], ce[:, :]))
                ch.link(nc.vector.tensor_tensor(ca[:, :], cc[:, :], ce[:, :], ALU.mult))
                nc.vector.tensor_copy(cb[:, :, :], spread(ca[:, :].unsqueeze(2), [P, KD, P])).then_inc(S["c_act_ready"], 1)
                dve.wait_ge(S["products_done"], 1)
                dve.wait_ge(S["small_loaded"], 64)
                nc.vector.tensor_tensor(sh[:, :], ps[:, 0:KD], b_ch[:, 0:KD], ALU.add)
                ch.link(nc.vector.tensor_tensor(ce[:, :], ps[:, KD:2 * KD], b_ch[:, KD:2 * KD], ALU.add))
                nc.vector.scalar_tensor_tensor(g1[:, :], ce[:, :], 1.0, npre[:, :], ALU.add, ALU.mult)
                ch.link(nc.vector.tensor_tensor(b_row[:, :], pg[:, :], b_row[:, :], ALU.add))
                nc.vector.tensor_tensor(gp[:, :], b_row[:, :], np_row[:, :], ALU.mult).then_inc(S["gate_ready"], 1)

            @block.tensor
            def _(pe):
                pe.wait_ge(S["c_act_ready"], 1)
                pe.wait_ge(S["w_loaded"], 16 * KD)
                for m in range(2 * KD):
                    for k in range(KD):
                        nc.tensor.matmul(ps[:, m:m + 1], ada[:, k, m * P:(m + 1) * P], ca[:, k:k + 1],
                                         start=(k == 0), stop=(k == KD - 1))
                for half in range(2):
                    for k in range(KD):
                        last = nc.tensor.matmul(pg[:, half * 512:(half + 1) * 512], cb[:, k, :],
                                                ada[:, k, 2 * D + half * 512:2 * D + (half + 1) * 512],
                                                start=(k == 0), stop=(k == KD - 1))
                last.then_inc(S["products_done"], 1)
        S.close()


def mixers(nc, A, mixed, keep, const):
    scale_ch, shift_ch = keep["scale_ch"], keep["shift_ch"]
    ident = const["ident"]
    with ExitStack() as ctx:
        sb = lambda n, s: ctx.enter_context(nc.sbuf_tensor("b1_" + n, s, F32))
        S = Signals(nc, "b1")
        banks8 = ctx.enter_context(nc.psum_tensor("b1_banks", [P, 8, 512], F32))
        B = [banks8[:, i, :] for i in range(8)]
        w_in = sb("w_in", [P, KD, IN1])
        lora_cur, lora_prev = sb("lora_cur", [P, KD, P]), sb("lora_prev", [P, KD, P])
        gk1, gkb = sb("gk1", [P, KD, 16]), sb("gkb", [P, 1])
        mu_w, mu_a = sb("mu_w", [P, KD]), sb("mu_a", [P, KD])
        mu_rkv = sb("mu_rkv", [P, 6])
        wa2 = sb("wa2", [P, 2, R_W])
        lows = sb("lows", [P, 2 * R_W])
        gk2, wa0 = lows[0:16, 0:P], lows[32:33, :]
        ones = sb("ones", [P, P])
        rows = sb("rows", [P, 6, R_W])
        KK_, KA_, OMKA, RK_, LNW, LNB = range(6)
        gnorm, sinks = sb("gnorm", [P, G_VAL]), sb("sinks", [P, A_HEADS])
        masks = sb("masks", [P, LEVELS, P])
        tri = sb("tri", [P, 2, P])
        pair = sb("pair", [P, P])
        quad = sb("quad", [P, R_W])
        chunk_of = sb("chunk_of", [P, 2])
        alibi = sb("alibi", [P, A_HEADS, 2 * P])
        numbers = sb("numbers", [P, 6, 4])
        NEG_HALF, PER_D, PER_HEAD, EPS_X, EPS_GLA, EPS_RWKV = range(6)
        xt = sb("xt", [P, D])
        xn = sb("xn", [P, D])
        y = xn
        stat = sb("stat", [P, 8])
        hT = sb("hT", [P, KD, P + 1])
        h_last, raw_last = sb("h_last", [P, KD]), sb("raw_last", [P, 6])
        XY = hT[:, :, :].rearrange("p a b -> p (a b)")
        loraT, gk1T = sb("loraT", [P, P]), sb("gk1T", [16, P])
        sg = sb("sg", [P, D])
        SAG, SRG, SGG = 0, 512, 768
        qT = sb("qT", [P, 4, P])
        kT = sb("kT", [P, 2, P])
        vt = sb("vt", [P, 2, P])
        s = sb("s", [P, A_HEADS, 2 * P])
        G8 = sb("G8", [P, 16, P])
        pT = G8[:, :, :].rearrange("p (j e) t -> p j e t", e=4)
        am, nm, den = sb("am", [P, A_HEADS]), sb("nm", [P, A_HEADS]), sb("den", [P, A_HEADS])
        rkvT = sb("rkvT", [P, 6, P + 1])
        mixT = sb("mixT", [P, 6, P])
        tok = sb("tok", [P, 3, R_W])
        wa = sb("wa", [P, 2, R_W])
        lw = sb("lw", [P, R_W])
        ex = mixT[:, :, :].rearrange("p (e a) b -> p e (a b)", e=3)
        pend = sb("pend", [P, 4])
        t1, t2, t3 = sb("t1", [P, R_W]), sb("t2", [P, R_W]), sb("t3", [P, R_W])
        h4 = sb("h4", [P, 4, 4])
        bonus = sb("bonus", [P, 4])
        X4 = sb("X4", [P, 4, R_W])
        X4T = sb("X4T", [P, 4, 2, P])
        GB = G8[:, 0:8, :].rearrange("p (h a) t -> p h a t", a=2)
        GK = G8[:, 8:16, :].rearrange("p (h a) t -> p h a t", a=2)
        cT = rkvT[:, :, :].rearrange("p a b -> p (a b)")[:, 0:512].rearrange("p (h t) -> p h t", t=P)
        Zs = sb("Zs", [P, 4, P])
        X = XY[:, 0:512].rearrange("p (h t) -> p h t", t=P)
        Y = XY[:, 512:1024].rearrange("p (h t) -> p h t", t=P)
        akv, U = qT[:, 0:2, :].rearrange("p a b -> p (a b)"), qT[:, 2:4, :].rearrange("p a b -> p (a b)")
        WT = sb("WT", [P, 2, P])
        SA, M = sb("SA", [P, R_W]), sb("M", [P, 2, P])
        yR = t2
        gqT, gkT, gv = sb("gqT", [P, P]), sb("gkT", [P, P]), sb("gv", [P, R_W])
        gz, gb = sb("gz", [P, 2, P]), sb("gb", [P, P])
        ge = sb("ge", [P, LEVELS, P])
        gql, gkl = s[:, 0:4, :].rearrange("p a b -> p (a b)"), s[:, 4:8, :].rearrange("p a b -> p (a b)")
        geb = sb("geb", [P, 3, P])
        gA, gS = sb("gA", [P, 4, P]), sb("gS", [P, R_W])
        ke_tok = gz[:, 1, :]
        g1, g4 = t3, sb("g4", [P, 4, 4])

        def s3(ap):
            return ap.rearrange("p (l t) -> p l t", t=P)

        chunk_cols = ([P * c for c in range(4)]
                      + [C_AK, C_GQ, C_GK]
                      + [C_RKV + P * c for c in range(6)])

        with nc.Block() as block:
            @block.sync
            def _(sp):
                load = lambda dst, src: sp.dma_start(dst, src).then_inc(S["weights_loaded"], 16)
                wsrc = A["w_in"][0].rearrange("(k p) n -> p k n", p=P)
                for k in range(KD):
                    load(w_in[:, k, 512:], wsrc[:, k, 512:])
                    for g in range(A_KV):
                        load(w_in[:, k, 0:512].rearrange("p (c g d) -> p g c d", g=2, d=HEAD)[:, g],
                             wsrc[:, k, 256 * g:256 * g + 256].rearrange("p (c d) -> p c d", d=HEAD))
                load(lora_cur[:, :, 0:64], A["rwkv_w1"][0].rearrange("(k p) n -> p k n", p=P))
                load(lora_cur[:, :, 64:128], A["rwkv_a1"][0].rearrange("(k p) n -> p k n", p=P))
                load(gk1[:, :, :], A["gla_gk1"][0].rearrange("(k p) n -> p k n", p=P))
                load(gk2[:, :], A["gla_gk2"][0])
                load(gkb[:, :], A["gla_gk_b_ch"])
                load(mu_w[:, :], A["rwkv_mu_w_ch"])
                load(mu_a[:, :], A["rwkv_mu_a_ch"])
                load(mu_rkv[:, :], A["rwkv_mu_rkv_ch"])
                load(wa2[0:64, 0, :], A["rwkv_w2"][0])
                load(wa2[64:128, 1, :], A["rwkv_a2"][0])
                load(wa0[:, 0:R_W], A["rwkv_w0"][0:1, :])
                load(wa0[:, R_W:], A["rwkv_a0"][0:1, :])
                for n, name in ((KK_, "rwkv_k_k"), (KA_, "rwkv_k_a"), (LNW, "rwkv_ln_w"), (LNB, "rwkv_ln_b")):
                    load(rows[:, n, :], row(A[name][0:1, :]))
                load(rows[:, RK_, :], row(A["rwkv_r_k"].rearrange("a h d -> a (h d)")))
                load(gnorm[:, :], row(A["gla_norm_w"][0:1, :]))
                load(sinks[:, :], row(A["attn_sinks"][0:1, :]))
                load(masks[:, :, :], A["k_masks"])
                load(tri[:, :, :], A["k_tri"])
                load(pair[:, :], A["k_pair"])
                load(quad[:, :], A["k_quad"])
                load(chunk_of[:, :], A["k_chunk_of"])
                load(alibi[:, :, P:], A["k_alibi"][:, :, P:])
                with sp.Fori(0, TILES) as i:
                    n = sp.snap(i + 1)
                    sp.wait_ge(S["x_used"], i)
                    sp.dma_start(xt[:, :], A["x"][0][bass.ds(i * P, P), :]).then_inc(S["x_loaded"], 16)
                    sp.wait_ge(S["scores_done"], n)
                    sp.dma_start(alibi[:, :, 0:P], A["k_alibi"][:, :, 0:P]).then_inc(S["alibi_ready"], 16)
                    sp.wait_ge(S["y_ready"], n)
                    sp.dma_start(mixed[bass.ds(i * P, P), :], y[:, :]).then_inc(S["y_stored"], 16)
                sp.wait_ge(S["y_stored"], 16 * TILES)

            N_WEIGHTS = 16 * (3 * KD + 12 + 4 + 3 + 6)

            @block.gpsimd
            def _(pool):
                ch = Chain(pool, S["pool_step"])
                nc.gpsimd.memset(ones[:, :], 1.0)
                for at, value in enumerate((-0.5, 1.0 / D, 1.0 / HEAD, EPS, 1e-5, RWKV_LN_EPS)):
                    nc.gpsimd.memset(numbers[:, at, :], value)
                nc.gpsimd.memset(alibi[:, :, 0:P], NEG)
                nc.gpsimd.memset(kT[:, :, :], 0.0)
                nc.gpsimd.memset(vt[:, :, :], 0.0)
                nc.gpsimd.memset(h_last[:, :], 0.0)
                nc.gpsimd.memset(raw_last[:, :], 0.0)
                ch.link(nc.gpsimd.memset(M[:, :, :], 0.0))
                ch.link(nc.gpsimd.memset(wa2[0:64, 1, :], 0.0))
                ch.link(nc.gpsimd.memset(wa2[64:128, 0, :], 0.0))
                nc.gpsimd.memset(gS[:, :], 0.0)
                ch.link(nc.gpsimd.memset(pend[:, :], 0.0))
                pool.wait_ge(S["weights_loaded"], N_WEIGHTS)
                ch.link(nc.gpsimd.tensor_scalar(rows[:, OMKA, :], rows[:, KA_, :], -1.0, 1.0, ALU.mult, ALU.add))
                for mu_ch, hs in ((mu_w, slice(0, 64)), (mu_a, slice(64, 128))):
                    mu = spread(mu_ch[:, :].unsqueeze(2), [P, KD, 64])
                    ch.link(nc.gpsimd.tensor_tensor(lora_prev[:, :, hs], lora_cur[:, :, hs], mu, ALU.mult))
                    ch.link(nc.gpsimd.tensor_tensor(lora_cur[:, :, hs], lora_cur[:, :, hs], lora_prev[:, :, hs], ALU.subtract))
                nc.gpsimd.memset(stat[:, :], 1.0).then_inc(S["setup_done"], 1)
                ch.start_over()

                def inv_sqrt(out, sums, n, per, eps):
                    ch.link(nc.gpsimd.tensor_tensor(sums, sums, numbers[:, per, 0:n], ALU.mult))
                    ch.link(nc.gpsimd.tensor_tensor(sums, sums, numbers[:, eps, 0:n], ALU.add))
                    return nc.gpsimd.tensor_tensor(out, sums, numbers[:, NEG_HALF, 0:n], ALU.pow)

                with pool.Fori(0, TILES) as i:
                    n = pool.snap(i + 1)
                    pool.wait_ge(S["x_squares"], n)
                    inv_sqrt(stat[:, 1:2], stat[:, 0:1], 1, PER_D, EPS_X).then_inc(S["x_rstd"], 1)
                    pool.wait_ge(S["kk_squares"], n)
                    nc.gpsimd.tensor_tensor(h4[:, 1, :], h4[:, 0, :], numbers[:, NEG_HALF, :], ALU.pow).then_inc(S["kk_rnorm"], 1)
                    pool.wait_ge(S["gla_squares"], n)
                    inv_sqrt(g4[:, 1, :], g4[:, 0, :], 4, PER_HEAD, EPS_GLA).then_inc(S["gla_rstd"], 1)
                    pool.wait_ge(S["rwkv_squares"], n)
                    inv_sqrt(h4[:, 3, :], h4[:, 2, :], 4, PER_HEAD, EPS_RWKV).then_inc(S["rwkv_rstd"], 1)
                    ch.start_over()

            @block.tensor
            def _(pe):
                pe.wait_ge(S["weights_loaded"], N_WEIGHTS)
                pe.wait_ge(S["setup_done"], 1)
                mm, tr = nc.tensor.matmul, nc.tensor.transpose
                with pe.Fori(0, TILES) as i:
                    n = pe.snap(i + 1)
                    pe.wait_ge(S["x_used"], n)
                    for k in range(KD):
                        last = tr(B[k // 4][:, (k % 4) * P:(k % 4 + 1) * P], xn[:, k * P:(k + 1) * P], ident[:, :])
                        if k % 4 == 3:
                            last.then_inc(S["x_turned"], 1)
                    pe.wait_ge(S["hT_dve"], n)
                    pe.wait_ge(S["hT_act"], n)
                    spots = [(2, c) for c in range(4)] + [(3, c) for c in range(3)] + [(4, c) for c in range(4)] + [(5, c) for c in range(2)]
                    for c, (bank, spot) in zip(chunk_cols, spots):
                        out = B[bank][:, spot * P:(spot + 1) * P]
                        for k in range(KD):
                            last = mm(out, w_in[:, k, c:c + P], hT[:, k, 1:P + 1], start=(k == 0), stop=(k == KD - 1))
                        if (bank, spot) == (2, 3):
                            last.then_inc(S["q_proj"], 1)
                        if (bank, spot) == (4, 3):
                            last.then_inc(S["rk_proj"], 1)
                    for k in range(KD):
                        mm(B[3][:, 3 * P:4 * P], lora_cur[:, k, :], hT[:, k, 1:P + 1], start=(k == 0), stop=False)
                    for k in range(KD):
                        last = mm(B[3][:, 3 * P:4 * P], lora_prev[:, k, :], hT[:, k, 0:P], start=False, stop=(k == KD - 1))
                    last.then_inc(S["k_lora_proj"], 1)
                    for k in range(KD):
                        last = mm(B[5][0:16, 2 * P:3 * P], gk1[:, k, :], hT[:, k, 1:P + 1], start=(k == 0), stop=(k == KD - 1))
                    last.then_inc(S["v_gk1_proj"], 1)
                    for out, c, w, name in ((B[6][:, 0:P], C_AV, P, None), (B[6][:, P:P + 256], C_RG, 256, "av_rg_proj"),
                                            (B[7][:, :], C_AG, 512, "ag_proj"), (B[0][:, :], C_GV, 512, "gv_gg_proj")):
                        for k in range(KD):
                            last = mm(out, hT[:, k, 1:P + 1], w_in[:, k, c:c + w], start=(k == 0), stop=(k == KD - 1))
                        if name:
                            last.then_inc(S[name], 1)
                    pe.wait_ge(S["lora_ready"], n)
                    mm(B[1][:, :], loraT[:, :], wa2[:, :, :].rearrange("p a b -> p (a b)"), start=True, stop=False)
                    last = mm(B[1][:, :], ones[32:33, :], wa0[:, :], start=False, stop=True)
                    last.then_inc(S["wa_proj"], 1)
                    pe.wait_ge(S["q_taken"], n)
                    pe.wait_ge(S["mix_ready"], n)
                    pe.wait_ge(S["bank3_taken"], n)
                    for c in range(6):
                        bank, spot = (2, c) if c < 4 else (3, c - 4)
                        last = tr(B[bank][:, spot * P:(spot + 1) * P], mixT[:, c, :], ident[:, :])
                    last.then_inc(S["rkv_turned"], 1)
                    pe.wait_ge(S["raw_taken"], n)
                    pe.wait_ge(S["bank3_taken"], n)
                    pe.wait_ge(S["gates_taken"], n)
                    for h in range(A_HEADS):
                        g = h // 4
                        last = mm(B[4 + h // 2][:, (h % 2) * 256:(h % 2) * 256 + 256], qT[64 * g:64 * g + 64, h % 4, :],
                                  kT[64 * g:64 * g + 64, :, :].rearrange("p a b -> p (a b)"), start=True, stop=True)
                        if h % 2:
                            last.then_inc(S[f"scores{h // 2}"], 1)
                    pe.wait_ge(S["lw_ready"], n)
                    pe.wait_ge(S["wa_exp"], n)
                    mm(B[1][:, 0:R_W], tri[:, 1, :], lw[:, :], start=True, stop=True)
                    for p in range(2):
                        last = mm(B[1][:, R_W + 2 * p:R_W + 2 * p + 2], lw[:, p * P:(p + 1) * P], chunk_of[:, :], start=True, stop=True)
                    last.then_inc(S["cum_done"], 1)
                    for j in range(4):
                        pe.wait_ge(S[f"probs{j}"], n)
                        for e in range(4):
                            last = tr(B[4 + j][:, e * P:(e + 1) * P], s[:, 2 * j + e // 2, (e % 2) * P:(e % 2 + 1) * P], ident[:, :])
                        last.then_inc(S[f"probs_turned{j}"], 1)
                    pe.wait_ge(S["gates_exp"], n)
                    pe.wait_ge(S["pT_dve"], n)
                    pe.wait_ge(S["pT_act"], n)
                    for h in range(A_HEADS):
                        for half in range(2):
                            last = mm(B[4][:, h * 64:(h + 1) * 64], pT[:, h // 2, (h % 2) * 2 + half, :],
                                      vt[:, half, 64 * (h // 4):64 * (h // 4) + 64], start=(half == 0), stop=(half == 1))
                    last.then_inc(S["attended"], 1)
                    mm(B[5][:, 0:P], gk2[:, :], gk1T[:, :], start=True, stop=True).then_inc(S["gate_proj"], 1)
                    pe.wait_ge(S["X4_ready"], n)
                    for c in range(8):
                        last = tr(B[2 + c // 4][:, (c % 4) * P:(c % 4 + 1) * P], X4[:, c // 2, (c % 2) * P:(c % 2 + 1) * P], ident[:, :])
                    last.then_inc(S["X4_turned"], 1)
                    pe.wait_ge(S["X4T_ready"], n)
                    for what, banks, name in ((2, (0, 1), "gram_b"), (3, (2, 3), "gram_k")):
                        for h in range(4):
                            r, p = slice(64 * (h % 2), 64 * (h % 2) + 64), h // 2
                            last = mm(B[banks[h % 2]][:, p * 256:p * 256 + 256], X4T[r, what, p, :],
                                      X4T[r, 0:2, p, :], start=True, stop=True)
                        last.then_inc(S[name], 1)
                    pe.wait_ge(S["gla_scaled"], n)
                    tr(B[5][:, P:2 * P], geb[:, 2, :], ident[:, :]).then_inc(S["ke_turned"], 1)
                    pe.wait_ge(S["attn_out"], n)
                    pe.wait_ge(S["ke_ready"], n)

                    def gla_round(half):
                        for l in range(4 * half, 4 * half + 4):
                            for h in range(4):
                                r = slice(32 * h, 32 * h + 32)
                                a, b = (gkT[r, :], gqT[r, :]) if l == 0 else (s3(gkl[r, 0:LEVELS * P])[:, l - 1, :], s3(gql[r, 0:LEVELS * P])[:, l - 1, :])
                                last = mm(B[4 + h][:, (l % 4) * P:(l % 4 + 1) * P], a, b, start=True, stop=True)
                        last.then_inc(S[f"gla_round{half}"], 1)

                    gla_round(0)
                    for l in range(INV_LEVELS):
                        if l == 4:
                            pe.wait_ge(S["gla_levels_used"], n)
                            gla_round(1)
                        pe.wait_ge(S[f"cT_ready{l}"], n)
                        for h in range(4):
                            last = mm(B[0][:, h * P:(h + 1) * P], cT[:, h, :], ident[:, :] if l == 0 else X[:, h, :], start=True, stop=True)
                        last.then_inc(S[f"Z_done{l}"], 1)
                        if l > 0:
                            pe.wait_ge(S[f"Z_taken{l}"], n)
                            for h in range(4):
                                last = mm(B[2][:, h * P:(h + 1) * P], Zs[:, h, :], Y[:, h, :], start=True, stop=True)
                            last.then_inc(S[f"YZ_done{l}"], 1)
                            if l < INV_LEVELS - 1:
                                for h in range(4):
                                    last = mm(B[1][:, h * P:(h + 1) * P], Y[:, h, :], Zs[:, h, :], start=True, stop=True)
                                last.then_inc(S[f"XZ_done{l}"], 1)
                    for h in range(4):
                        last = mm(B[3][:, h * 64:(h + 1) * 64], GK[:, h, 0, :], tok[:, 2, h * 64:(h + 1) * 64], start=True, stop=True)
                    last.then_inc(S["akv_done"], 1)
                    pe.wait_ge(S["Y_ready"], n)
                    for h in range(4):
                        last = mm(B[1][64 * (h % 2):64 * (h % 2) + 64, (h // 2) * P:(h // 2 + 1) * P], X4[:, 0, h * 64:(h + 1) * 64], Y[:, h, :], start=True, stop=True)
                    last.then_inc(S["WT_done"], 1)
                    pe.wait_ge(S["akv_ready"], n)
                    for h in range(4):
                        last = mm(B[0][:, h * 64:(h + 1) * 64], Y[:, h, :], akv[:, h * 64:(h + 1) * 64], start=True, stop=True)
                    last.then_inc(S["U_done"], 1)
                    pe.wait_ge(S["gA_ready"], n)
                    for h in range(4):
                        c = slice(h * 64, (h + 1) * 64)
                        mm(B[4][:, c], geb[:, 1, :], gS[:, c], start=True, stop=False)
                        mm(B[4][:, c], gA[:, h, :], gv[:, c], start=False, stop=True)
                    last = mm(B[5][:, 256:512], ke_tok, gv[:, :], start=True, stop=True)
                    last.then_inc(S["gla_out"], 1)
                    pe.wait_ge(S["WT_ready"], n)
                    for c in range(2):
                        r = slice(64 * c, 64 * c + 64)
                        if c == 1:
                            pe.wait_ge(S["M_ready0"], n)
                        for p in range(2):
                            mm(B[2][r, p * P:(p + 1) * P], WT[:, p, r], M[:, p, :], start=True, stop=True)
                        for p in range(2):
                            last = mm(B[1][r, 256 + p * P:256 + (p + 1) * P], X4T[:, 1, p, r], M[:, p, :], start=True, stop=True)
                        last.then_inc(S[f"sa_done{c}"], 1)
                        pe.wait_ge(S[f"sa_ready{c}"], n)
                        for p in range(2):
                            mm(B[3][:, 256 + p * P:256 + (p + 1) * P], X4[r, 2, p * P:(p + 1) * P], SA[r, p * P:(p + 1) * P], start=True, stop=False)
                            last = mm(B[3][:, 256 + p * P:256 + (p + 1) * P], X4[r, 3, p * P:(p + 1) * P], tok[r, 2, p * P:(p + 1) * P], start=False, stop=True)
                        last.then_inc(S[f"dM_done{c}"], 1)
                    for h in range(4):
                        c = slice(h * 64, (h + 1) * 64)
                        mm(B[0][:, 256 + h * 64:256 + (h + 1) * 64], GB[:, h, 1, :], SA[:, c], start=True, stop=False)
                        last = mm(B[0][:, 256 + h * 64:256 + (h + 1) * 64], GK[:, h, 1, :], tok[:, 2, c], start=False, stop=True)
                    last.then_inc(S["rwkv_out"], 1)

            @block.scalar
            def _(act):
                ch = Chain(act, S["act_step"])
                f = nc.scalar.activation
                act.wait_ge(S["setup_done"], 1)
                with act.Fori(0, TILES) as i:
                    n = act.snap(i + 1)
                    act.wait_ge(S["x_loaded"], n * 16)
                    act.wait_ge(S["y_stored"], i * 16)
                    f(xn[:, :], xt[:, :], ACT.Square, accum_out=stat[:, 0:1]).then_inc(S["x_squares"], 1)
                    act.wait_ge(S["x_rstd"], n)
                    f(xn[:, :], xt[:, :], ACT.Copy, scale=stat[:, 1:2]).then_inc(S["x_used"], 1)
                    act.wait_ge(S["prev_kept"], n)
                    act.wait_ge(S["x_turned"], 2 * i + 1)
                    for k in range(4):
                        last = f(hT[:, k, 1:P + 1], B[0][:, k * P:(k + 1) * P], ACT.Identity, bias=shift_ch[:, k:k + 1], scale=scale_ch[:, k:k + 1])
                    last.then_inc(S["hT_act"], 1)
                    act.wait_ge(S["q_proj"], n)
                    f(qT[:, :, :].rearrange("p a b -> p (a b)"), B[2][:, :], ACT.Copy).then_inc(S["q_taken"], 1)
                    act.wait_ge(S["k_lora_proj"], n)
                    f(loraT[0:64, :], B[3][0:64, 3 * P:4 * P], ACT.Tanh)
                    f(loraT[64:128, :], B[3][64:128, 3 * P:4 * P], ACT.Copy).then_inc(S["lora_ready"], 1)
                    f(gqT[:, :], B[3][:, P:2 * P], ACT.Copy, scale=G_KEY ** -0.5)
                    f(gkT[:, :], B[3][:, 2 * P:3 * P], ACT.Copy)
                    f(kT[:, 1, :], B[3][:, 0:P], ACT.Copy).then_inc(S["bank3_taken"], 1)
                    act.wait_ge(S["av_rg_proj"], n)
                    f(vt[:, 1, :], B[6][:, 0:P], ACT.Copy)
                    f(sg[:, SRG:SRG + 256], B[6][:, P:P + 256], ACT.Exp, scale=-1.0)
                    act.wait_ge(S["ag_proj"], n)
                    f(sg[:, SAG:SAG + 512], B[7][:, :], ACT.Exp, scale=-1.0)
                    act.wait_ge(S["gv_gg_proj"], n)
                    f(gv[:, :], B[0][:, 0:256], ACT.Copy)
                    f(sg[:, SGG:SGG + 256], B[0][:, 256:512], ACT.Exp, scale=-1.0).then_inc(S["gates_exp"], 1)
                    act.wait_ge(S["wa_proj"], n)
                    f(wa[:, :, :].rearrange("p a b -> p (a b)"), B[1][:, :], ACT.Exp, scale=-1.0).then_inc(S["wa_exp"], 1)
                    act.wait_ge(S["rkv_turned"], n)
                    f(tok[:, 0:2, :].rearrange("p a b -> p (a b)"), B[2][:, :], ACT.Copy)
                    f(tok[:, 2, :], B[3][:, 0:256], ACT.Copy).then_inc(S["tok_ready"], 1)
                    act.wait_ge(S["cum_less"], n)
                    f(ex[:, 1, :], B[1][:, 0:R_W], ACT.Exp)
                    f(ex[:, 2, :], B[1][:, 0:R_W], ACT.Exp, scale=-1.0)
                    f(pend[:, :], B[1][:, R_W:R_W + 4], ACT.Exp)
                    f(ex[:, 0, :], ex[:, 0, :], ACT.Exp).then_inc(S["ex_ready"], 1)
                    act.wait_ge(S["max_ready"], n)
                    for h in range(A_HEADS):
                        last = f(s[:, h, :], s[:, h, :], ACT.Exp, bias=nm[:, h:h + 1], accum_out=den[:, h:h + 1])
                        if h % 2:
                            last.then_inc(S[f"probs{h // 2}"], 1)
                    f(am[:, :], am[:, :], ACT.Exp).then_inc(S["sink_exp"], 1)
                    for j in (0, 2):
                        act.wait_ge(S[f"probs_turned{j}"], n)
                        last = f(pT[:, j, :, :].rearrange("p a b -> p (a b)"), B[4 + j][:, :], ACT.Copy)
                    last.then_inc(S["pT_act"], 1)
                    act.wait_ge(S["gate_abs"], n)
                    ch.link(f(gz[:, 1, :], gz[:, 1, :], ACT.Exp, scale=-1.0))
                    f(gz[:, 1, :], gz[:, 1, :], ACT.Ln, bias=1.0).then_inc(S["gate_ln"], 1)
                    act.wait_ge(S["levels_ready"], n)
                    f(ge[:, :, :], ge[:, :, :], ACT.Exp)
                    f(geb[:, 1, :], gb[:, :], ACT.Exp)
                    f(geb[:, 2, :], gb[:, :], ACT.Exp, scale=-1.0, bias=gb[:, P - 1:P]).then_inc(S["levels_exp"], 1)
                    act.wait_ge(S["X4_turned"], n)
                    f(X4T[:, 0:2, :, :].rearrange("p a b c -> p (a b c)"), B[2][:, :], ACT.Copy)
                    f(X4T[:, 2:4, :, :].rearrange("p a b c -> p (a b c)"), B[3][:, :], ACT.Copy).then_inc(S["X4T_ready"], 1)
                    act.wait_ge(S["ke_turned"], n)
                    f(ke_tok, B[5][:, P:2 * P], ACT.Copy).then_inc(S["ke_ready"], 1)
                    for l in range(1, INV_LEVELS):
                        act.wait_ge(S[f"Z_done{l}"], n)
                        f(Zs[:, :, :].rearrange("p a b -> p (a b)"), B[0][:, :], ACT.Copy).then_inc(S[f"Z_taken{l}"], 1)
                    act.wait_ge(S["akv_done"], n)
                    f(akv[:, :], B[3][:, 0:R_W], ACT.Copy).then_inc(S["akv_ready"], 1)
                    act.wait_ge(S["WT_done"], n)
                    f(WT[:, :, :].rearrange("p a b -> p (a b)"), B[1][:, 0:R_W], ACT.Copy)
                    act.wait_ge(S["U_done"], n)
                    f(U[:, :], B[0][:, 0:R_W], ACT.Copy).then_inc(S["WT_ready"], 1)
                    for c in range(2):
                        act.wait_ge(S[f"sa_done{c}"], n)
                        last = f(yR[64 * c:64 * c + 64, :], B[1][64 * c:64 * c + 64, 256:512], ACT.Copy)
                    last.then_inc(S["yR_ready"], 1)
                    ch.start_over()

            @block.vector
            def _(dve):
                ch = Chain(dve, S["dve_step"])
                v = nc.vector
                tt, ts, stt = v.tensor_tensor, v.tensor_scalar, v.scalar_tensor_tensor
                dve.wait_ge(S["setup_done"], 1)
                ch.link(v.memset(am[:, :], 0.0))
                dve.sem_clear(S["dve_step"])
                ch.count = 0

                def heads(ap, d=HEAD):
                    return ap.rearrange("p (h d) -> p h d", d=d)

                with dve.Fori(0, TILES) as i:
                    n = dve.snap(i + 1)
                    dve.wait_ge(S["y_ready"], i)
                    v.tensor_copy(hT[:, :, 0:1], h_last[:, :].unsqueeze(2))
                    v.tensor_copy(rkvT[:, :, 0:1], raw_last[:, :].unsqueeze(2))
                    v.tensor_copy(kT[:, 0, :], kT[:, 1, :])
                    v.tensor_copy(vt[:, 0, :], vt[:, 1, :]).then_inc(S["prev_kept"], 1)
                    dve.wait_ge(S["x_turned"], 2 * n)
                    for k in range(4, 8):
                        last = ts(hT[:, k, 1:P + 1], B[1][:, (k - 4) * P:(k - 3) * P], scale_ch[:, k:k + 1], shift_ch[:, k:k + 1], ALU.mult, ALU.add)
                    last.then_inc(S["hT_dve"], 1)
                    dve.wait_ge(S["rk_proj"], n)
                    v.tensor_copy(rkvT[:, 0:4, 1:P + 1], B[4][:, :].rearrange("p (a b) -> p a b", b=P))
                    dve.wait_ge(S["v_gk1_proj"], n)
                    v.tensor_copy(gk1T[:, :], B[5][0:16, 2 * P:3 * P])
                    v.tensor_copy(rkvT[:, 4:6, 1:P + 1], B[5][:, 0:2 * P].rearrange("p (a b) -> p a b", b=P)).then_inc(S["raw_taken"], 1)
                    dve.wait_ge(S["raw_taken"], n)
                    ch.link(tt(mixT[:, :, :], rkvT[:, :, 0:P], rkvT[:, :, 1:P + 1], ALU.subtract))
                    for c in range(6):
                        last = stt(mixT[:, c, :], mixT[:, c, :], mu_rkv[:, c:c + 1], rkvT[:, c, 1:P + 1], ALU.mult, ALU.add)
                    last.then_inc(S["mix_ready"], 1)
                    ch.link(v.tensor_copy(raw_last[:, :].unsqueeze(2), rkvT[:, :, P:P + 1]))
                    dve.wait_ge(S["hT_act"], n)
                    ch.link(v.tensor_copy(h_last[:, :].unsqueeze(2), hT[:, :, P:P + 1]))
                    dve.wait_ge(S["gates_exp"], n)
                    ch.link(ts(sg[:, :], sg[:, :], 1.0, None, ALU.add))
                    ch.link(v.reciprocal(sg[:, :], sg[:, :]))
                    tt(sg[:, SAG:SAG + 512], B[7][:, :], sg[:, SAG:SAG + 512], ALU.mult)
                    tt(sg[:, SRG:SRG + 256], B[6][:, P:P + 256], sg[:, SRG:SRG + 256], ALU.mult)
                    tt(sg[:, SGG:SGG + 256], B[0][:, 256:512], sg[:, SGG:SGG + 256], ALU.mult).then_inc(S["gates_taken"], 1)
                    dve.wait_ge(S["wa_exp"], n)
                    ch.link(ts(wa[:, :, :], wa[:, :, :], 1.0, None, ALU.add))
                    ch.link(v.reciprocal(wa[:, :, :], wa[:, :, :]))
                    ts(lw[:, :], wa[:, 0, :], -float(np.exp(-0.5)), None, ALU.mult).then_inc(S["lw_ready"], 1)
                    dve.wait_ge(S["lw_ready"], n)
                    dve.wait_ge(S["alibi_ready"], i * 16)
                    for j in range(4):
                        dve.wait_ge(S[f"scores{j}"], n)
                        last = stt(s[:, 2 * j:2 * j + 2, :].rearrange("p a b -> p (a b)"), B[4 + j][:, :], HEAD ** -0.5,
                                   alibi[:, 2 * j:2 * j + 2, :].rearrange("p a b -> p (a b)"), ALU.mult, ALU.add)
                    last.then_inc(S["scores_done"], 1)
                    dve.wait_ge(S["scores_done"], n)
                    ch.link(v.tensor_reduce(am[:, :], s[:, :, :], AX.X, ALU.max))
                    ch.link(tt(am[:, :], am[:, :], sinks[:, :], ALU.max))
                    ch.link(ts(nm[:, :], am[:, :], -1.0, None, ALU.mult))
                    tt(am[:, :], sinks[:, :], nm[:, :], ALU.add).then_inc(S["max_ready"], 1)
                    dve.wait_ge(S["cum_done"], n)
                    tt(ex[:, 0, :], B[1][:, 0:R_W], lw[:, :], ALU.subtract).then_inc(S["cum_less"], 1)
                    dve.wait_ge(S["tok_ready"], n)
                    ch.link(tt(t1[:, :], tok[:, 1, :], rows[:, KK_, :], ALU.mult))
                    ch.link(tt(t2[:, :], t1[:, :], t1[:, :], ALU.mult))
                    ch.link(v.tensor_reduce(h4[:, 0, :], heads(t2[:, :]), AX.X, ALU.add))
                    ts(h4[:, 0, :], h4[:, 0, :], 1e-24, None, ALU.max).then_inc(S["kk_squares"], 1)
                    ch.link(tt(t3[:, :], wa[:, 1, :], rows[:, KA_, :], ALU.mult))
                    ch.link(tt(t3[:, :], t3[:, :], rows[:, OMKA, :], ALU.add))
                    ch.link(tt(t3[:, :], t3[:, :], tok[:, 1, :], ALU.mult))
                    ch.link(tt(t2[:, :], tok[:, 0, :], t3[:, :], ALU.mult))
                    ch.link(tt(t2[:, :], t2[:, :], rows[:, RK_, :], ALU.mult))
                    ch.link(v.tensor_reduce(bonus[:, :], heads(t2[:, :]), AX.X, ALU.add))
                    dve.wait_ge(S["kk_rnorm"], n)
                    ch.link(tt(heads(t1[:, :]), heads(t1[:, :]), spread(h4[:, 1, :].unsqueeze(2), [P, 4, HEAD]), ALU.mult))
                    ch.link(tt(t2[:, :], t1[:, :], wa[:, 1, :], ALU.mult))
                    dve.wait_ge(S["ex_ready"], n)
                    tt(X4[:, 0, :], t1[:, :], ex[:, 0, :], ALU.mult)
                    tt(X4[:, 1, :], tok[:, 0, :], ex[:, 1, :], ALU.mult)
                    tt(X4[:, 2, :], t2[:, :], ex[:, 2, :], ALU.mult)
                    tt(X4[:, 3, :], t3[:, :], ex[:, 2, :], ALU.mult).then_inc(S["X4_ready"], 1)
                    for j in (1, 3):
                        dve.wait_ge(S[f"probs_turned{j}"], n)
                        last = v.tensor_copy(pT[:, j, :, :].rearrange("p a b -> p (a b)"), B[4 + j][:, :])
                    last.then_inc(S["pT_dve"], 1)
                    dve.wait_ge(S["sink_exp"], n)
                    ch.link(tt(den[:, :], den[:, :], am[:, :], ALU.add))
                    ch.link(v.reciprocal(den[:, :], den[:, :]))
                    dve.wait_ge(S["attended"], n)
                    tt(heads(y[:, 0:512]), heads(B[4][:, :]), spread(den[:, :].unsqueeze(2), [P, A_HEADS, HEAD]), ALU.mult).then_inc(S["attn_out"], 1)
                    dve.wait_ge(S["attn_out"], n)
                    ch.link(tt(y[:, 0:512], y[:, 0:512], sg[:, 0:512], ALU.mult))
                    dve.wait_ge(S["gate_proj"], n)
                    ch.link(ts(gz[:, 0, :], B[5][:, 0:P], gkb[:, 0:1], None, ALU.add))
                    stt(gz[:, 1, :], gz[:, 0, :], -1.0, gz[:, 0, :], ALU.mult, ALU.max).then_inc(S["gate_abs"], 1)
                    ch.link(ts(gz[:, 0, :], gz[:, 0, :], 0.0, None, ALU.min))
                    dve.wait_ge(S["gate_ln"], n)
                    ch.link(tt(gz[:, 0, :], gz[:, 0, :], gz[:, 1, :], ALU.subtract))
                    ch.link(ts(gz[:, 0, :], gz[:, 0, :], 1.0 / 16.0, None, ALU.mult))
                    ch.link(v.tensor_tensor_scan(gb[:, :], ones[:, :], gz[:, 0, :], 0.0, ALU.mult, ALU.add))
                    for l in range(LEVELS):
                        half = 1 << l
                        blocks = lambda ap: ap.rearrange("p (m w) -> p m w", w=2 * half)
                        mid = spread(blocks(gb[:, :])[:, :, half - 1:half], [P, P // (2 * half), 2 * half])
                        last = tt(blocks(ge[:, l, :]), blocks(gb[:, :]), mid, ALU.subtract)
                    ch.link(last)
                    stt(ge[:, :, :], ge[:, :, :], -1.0, ge[:, :, :], ALU.mult, ALU.min).then_inc(S["levels_ready"], 1)
                    dve.wait_ge(S["levels_exp"], n)
                    tt(s3(gql[:, 0:LEVELS * P]), ge[:, :, :], spread(gqT[:, :].unsqueeze(1), [P, LEVELS, P]), ALU.mult)
                    tt(s3(gkl[:, 0:LEVELS * P]), ge[:, :, :], spread(gkT[:, :].unsqueeze(1), [P, LEVELS, P]), ALU.mult)
                    v.tensor_copy(g4[:, 3, 0:1], geb[:, 1, P - 1:P])
                    ch.link(tt(geb[:, 2, :], geb[:, 2, :], gkT[:, :], ALU.mult))
                    tt(geb[:, 1, :], geb[:, 1, :], gqT[:, :], ALU.mult).then_inc(S["gla_scaled"], 1)
                    for name, banks, dst in (("gram_b", (0, 1), GB), ("gram_k", (2, 3), GK)):
                        dve.wait_ge(S[name], n)
                        for j in range(2):
                            last = tt(dst.rearrange("p (q j) a b -> p j q (a b)", j=2)[:, j],
                                      B[banks[j]][:, :].rearrange("p (h a) -> p h a", h=2),
                                      spread(tri[:, :, :].rearrange("p a b -> p (a b)").unsqueeze(1), [P, 2, 2 * P]), ALU.mult)
                        ch.link(last)

                    def level(l):
                        src = banks8[:, 4:8, (l % 4) * P:(l % 4 + 1) * P]
                        if l == 0:
                            last = tt(gA[:, :, :], src, spread(ident[:, :].unsqueeze(1), [P, 4, P]), ALU.mult)
                        else:
                            last = v.copy_predicated(gA[:, :, :], spread(masks[:, l - 1, :].bitcast(U32).unsqueeze(1), [P, 4, P]), src)
                        if l == 3:
                            last.then_inc(S["gla_levels_used"], 1)
                            dve.wait_ge(S["gla_levels_used"], n)
                        else:
                            ch.link(last)

                    for l in range(INV_LEVELS):
                        if l > 0:
                            dve.wait_ge(S[f"Z_done{l - 1}"], n)
                        if l % 4 == 0:
                            dve.wait_ge(S[f"gla_round{l // 4}"], n)
                        tt(cT[:, :, :], GB[:, :, 0, :], spread(masks[:, l, :].unsqueeze(1), [P, 4, P]), ALU.mult).then_inc(S[f"cT_ready{l}"], 1)
                        level(l)
                        if l == 0:
                            dve.wait_ge(S["cT_ready0"], n)
                            idn = spread(ident[:, :].unsqueeze(1), [P, 4, P])
                            ch.link(tt(Y[:, :, :], idn, cT[:, :, :], ALU.subtract))
                            dve.wait_ge(S["Z_done0"], n)
                            ch.link(tt(X[:, :, :], idn, B[0][:, :].rearrange("p (h t) -> p h t", t=P), ALU.subtract))
                        elif l < INV_LEVELS - 1:
                            dve.wait_ge(S[f"XZ_done{l}"], n)
                            flat = lambda a: a[:, :, :].rearrange("p a b -> p (a b)")
                            tt(flat(Y), flat(Y), B[2][:, :], ALU.subtract)
                            ch.link(tt(flat(X), flat(X), B[1][:, :], ALU.subtract))
                        else:
                            dve.wait_ge(S[f"YZ_done{l}"], n)
                            tt(flat(Y), flat(Y), B[2][:, :], ALU.subtract).then_inc(S["Y_ready"], 1)
                    level(6)
                    level(7)
                    v.tensor_copy(g1[:, 1:2], g4[:, 3, 0:1]).then_inc(S["gA_ready"], 1)
                    dve.wait_ge(S["gla_out"], n)
                    ch.link(tt(g1[:, :], B[5][:, 256:512], quad[:, :], ALU.mult))
                    ch.link(stt(gS[:, :], gS[:, :], g4[:, 3, 0:1], g1[:, :], ALU.mult, ALU.add))
                    ch.link(v.tensor_copy(y[:, 768:1024], B[4][:, 0:R_W]))
                    ch.link(tt(g1[:, :], y[:, 768:1024], y[:, 768:1024], ALU.mult))
                    v.tensor_reduce(g4[:, 0, :], heads(g1[:, :]), AX.X, ALU.add).then_inc(S["gla_squares"], 1)
                    dve.wait_ge(S["gla_rstd"], n)
                    yg = heads(y[:, 768:1024])
                    ch.link(tt(yg, yg, spread(g4[:, 1, :].unsqueeze(2), [P, 4, HEAD]), ALU.mult))
                    ch.link(tt(yg, yg, spread(gnorm[:, :].unsqueeze(1), [P, 4, HEAD]), ALU.mult))
                    ch.link(tt(y[:, 768:1024], y[:, 768:1024], sg[:, SGG:SGG + 256], ALU.mult))
                    dve.wait_ge(S["WT_ready"], n)
                    for c in range(2):
                        r = slice(64 * c, 64 * c + 64)
                        dve.wait_ge(S[f"sa_done{c}"], n)
                        stt(SA[r, :], B[2][r, 0:R_W], -1.0, U[r, :], ALU.mult, ALU.subtract).then_inc(S[f"sa_ready{c}"], 1)
                        dve.wait_ge(S[f"dM_done{c}"], n)
                        dM = t1[:, :].rearrange("p (a b) -> p a b", b=P)
                        ch.link(tt(dM, B[3][:, 256:512].rearrange("p (a b) -> p a b", b=P), spread(pair[:, :].unsqueeze(1), [P, 2, P]), ALU.mult))
                        ch.link(tt(M[:, :, :], M[:, :, :], dM, ALU.add))
                        ts(M[:, 0, :], M[:, 0, :], pend[:, c:c + 1], None, ALU.mult)
                        ts(M[:, 1, :], M[:, 1, :], pend[:, 2 + c:3 + c], None, ALU.mult).then_inc(S[f"M_ready{c}"], 1)
                    dve.wait_ge(S["yR_ready"], n)
                    dve.wait_ge(S["rwkv_out"], n)
                    yr = heads(t1[:, :])
                    dve.wait_ge(S["M_ready1"], n)
                    ch.link(tt(t1[:, :], B[0][:, 256:512], yR[:, :], ALU.add))
                    ch.link(v.tensor_reduce(h4[:, 0, :], yr, AX.X, ALU.add))
                    ch.link(ts(h4[:, 0, :], h4[:, 0, :], 1.0 / HEAD, None, ALU.mult))
                    ch.link(tt(yr, yr, spread(h4[:, 0, :].unsqueeze(2), [P, 4, HEAD]), ALU.subtract))
                    ch.link(tt(t2[:, :], t1[:, :], t1[:, :], ALU.mult))
                    v.tensor_reduce(h4[:, 2, :], heads(t2[:, :]), AX.X, ALU.add).then_inc(S["rwkv_squares"], 1)
                    ch.link(tt(heads(t3[:, :]), heads(tok[:, 2, :]), spread(bonus[:, :].unsqueeze(2), [P, 4, HEAD]), ALU.mult))
                    dve.wait_ge(S["rwkv_rstd"], n)
                    ch.link(tt(yr, yr, spread(h4[:, 3, :].unsqueeze(2), [P, 4, HEAD]), ALU.mult))
                    ch.link(tt(t1[:, :], t1[:, :], rows[:, LNW, :], ALU.mult))
                    ch.link(tt(t1[:, :], t1[:, :], rows[:, LNB, :], ALU.add))
                    ch.link(tt(t1[:, :], t1[:, :], t3[:, :], ALU.add))
                    tt(y[:, 512:768], t1[:, :], sg[:, SRG:SRG + 256], ALU.mult).then_inc(S["y_ready"], 1)
                    ch.start_over()
        S.close()


def output_and_residual(nc, A, mixed, x1, keep, const):
    ident = const["ident"]
    with ExitStack() as ctx:
        sb = lambda n, s: ctx.enter_context(nc.sbuf_tensor("o1_" + n, s, F32))
        S = Signals(nc, "o1")
        B = [ctx.enter_context(nc.psum_tensor(f"o1_bank{i}", [P, 512], F32)) for i in range(8)]
        w, gate_row = sb("w", [P, KD, D]), sb("gate_row", [P, D])
        y, x, r = sb("y", [P, 2, D]), sb("x", [P, 2, D]), sb("r", [P, 2, D])
        yT, sq = sb("yT", [P, 2, KD, P]), sb("sq", [P, 512])
        st, neg_half = sb("st", [P, 2, 4]), sb("neg_half", [P, 1])
        PAIRS = TILES // 2

        with nc.Block() as block:
            @block.sync
            def _(sp):
                src = A["w_out"][0].rearrange("(k p) n -> p k n", p=P)
                for k in range(KD):
                    sp.dma_start(w[:, k, :], src[:, k, :]).then_inc(S["w_loaded"], 16)
                sp.dma_start(gate_row[:, :], keep["gate_row"]).then_inc(S["gate_loaded"], 16)
                with sp.Fori(0, PAIRS) as i:
                    for b in range(2):
                        sp.wait_ge(S[f"y_turned{b}"], i)
                        sp.dma_start(y[:, b, :], mixed[bass.ds((2 * i + b) * P, P), :]).then_inc(S[f"y_loaded{b}"], 16)
                        sp.wait_ge(S[f"x_used{b}"], i)
                        sp.dma_start(x[:, b, :], A["x"][0][bass.ds((2 * i + b) * P, P), :]).then_inc(S[f"x_loaded{b}"], 16)

            @block.gpsimd
            def _(pool):
                ch = Chain(pool, S["pool_step"])
                ch.link(nc.gpsimd.memset(neg_half[:, :], -0.5))
                ch.start_over()
                with pool.Fori(0, PAIRS) as i:
                    n = pool.snap(i + 1)
                    for b in range(2):
                        pool.wait_ge(S[f"squares{b}"], n)
                        ch.link(nc.gpsimd.tensor_tensor(st[:, b, 0:1], st[:, b, 0:1], st[:, b, 1:2], ALU.add))
                        ch.link(nc.gpsimd.tensor_scalar(st[:, b, 0:1], st[:, b, 0:1], 1.0 / D, EPS, ALU.mult, ALU.add))
                        nc.gpsimd.tensor_tensor(st[:, b, 2:3], st[:, b, 0:1], neg_half[:, :], ALU.pow).then_inc(S[f"rstd{b}"], 1)
                    ch.start_over()

            @block.tensor
            def _(pe):
                pe.wait_ge(S["w_loaded"], 16 * KD)
                with pe.Fori(0, PAIRS) as i:
                    n = pe.snap(i + 1)
                    for b in range(2):
                        pe.wait_ge(S[f"y_loaded{b}"], n * 16)
                        pe.wait_ge(S[f"yT_act{b}"], i)
                        pe.wait_ge(S[f"yT_dve{b}"], i)
                        for k in range(KD):
                            last = nc.tensor.transpose(B[2 * b + k // 4][:, (k % 4) * P:(k % 4 + 1) * P], y[:, b, k * P:(k + 1) * P], ident[:, :])
                        last.then_inc(S[f"y_turned{b}"], 1)
                    for b in range(2):
                        pe.wait_ge(S[f"yT_act{b}"], n)
                        pe.wait_ge(S[f"yT_dve{b}"], n)
                        pe.wait_ge(S[f"scaled{b}"], i)
                        for half in range(2):
                            for k in range(KD):
                                last = nc.tensor.matmul(B[4 + 2 * b + half][:, :], yT[:, b, k, :], w[:, k, half * 512:(half + 1) * 512], start=(k == 0), stop=(k == KD - 1))
                        last.then_inc(S[f"projected{b}"], 1)

            @block.scalar
            def _(act):
                flat = lambda b, a: yT[:, b, a:a + 4, :].rearrange("p a b -> p (a b)")
                with act.Fori(0, PAIRS) as i:
                    n = act.snap(i + 1)
                    for b in range(2):
                        act.wait_ge(S[f"y_turned{b}"], n)
                        act.wait_ge(S[f"projected{b}"], i)
                        nc.scalar.activation(flat(b, 0), B[2 * b][:, :], ACT.Copy).then_inc(S[f"yT_act{b}"], 1)
                    for b in range(2):
                        act.wait_ge(S[f"projected{b}"], n)
                        act.wait_ge(S[f"rstd{b}"], i)
                        nc.scalar.activation(sq[:, :], B[4 + 2 * b][:, :], ACT.Square, accum_out=st[:, b, 0:1]).then_inc(S["act_step"], 1)
                        act.wait_ge(S["act_step"], 1)
                        act.sem_clear(S["act_step"])
                        nc.scalar.activation(sq[:, :], B[5 + 2 * b][:, :], ACT.Square, accum_out=st[:, b, 1:2]).then_inc(S[f"squares{b}"], 1)
                        act.wait_ge(S[f"squares{b}"], n)
                        act.wait_ge(S[f"x_used{b}"], n)
                        act.dma_start(x1[bass.ds((2 * i + b) * P, P), :], r[:, b, :]).then_inc(S[f"x1_stored{b}"], 16)
                for b in range(2):
                    act.wait_ge(S[f"x1_stored{b}"], 16 * PAIRS)

            @block.vector
            def _(dve):
                flat = lambda b, a: yT[:, b, a:a + 4, :].rearrange("p a b -> p (a b)")
                dve.wait_ge(S["gate_loaded"], 16)
                with dve.Fori(0, PAIRS) as i:
                    n = dve.snap(i + 1)
                    for b in range(2):
                        dve.wait_ge(S[f"y_turned{b}"], n)
                        dve.wait_ge(S[f"projected{b}"], i)
                        nc.vector.tensor_copy(flat(b, 4), B[2 * b + 1][:, :]).then_inc(S[f"yT_dve{b}"], 1)
                    for b in range(2):
                        dve.wait_ge(S[f"rstd{b}"], n)
                        dve.wait_ge(S[f"x1_stored{b}"], i * 16)
                        for half in range(2):
                            c = slice(half * 512, (half + 1) * 512)
                            last = nc.vector.scalar_tensor_tensor(r[:, b, c], B[4 + 2 * b + half][:, :], st[:, b, 2:3], gate_row[:, c], ALU.mult, ALU.mult)
                        last.then_inc(S[f"scaled{b}"], 1)
                        dve.wait_ge(S[f"scaled{b}"], n)
                        dve.wait_ge(S[f"x_loaded{b}"], n * 16)
                        nc.vector.tensor_tensor(r[:, b, :], r[:, b, :], x[:, b, :], ALU.add).then_inc(S[f"x_used{b}"], 1)
        S.close()
A2_HEADS, A2_KV = 8, 2
IDX_HEADS, IDX_DIM = 8, 32
ROT, IDX_ROT = 8, 4
TOPK = 256
POOL_GROUPS = 4
HIST = 16
C2_Q, C2_K, C2_V, C2_QI, C2_KI, C2_ZA, C2_U, C2_ZB, C2_GATES = 0, 512, 640, 768, 1024, 1064, 1576, 2088, 2600
IN2 = 4648
T_QT, T_QI, T_W, T_ZA, T_BT, T_G, T_KT, T_KI, T_V, T_END = 0, 512, 768, 784, 1296, 1808, 3856, 3984, 4112, 4240


def rotary_tables(nc, A, tables):
    NF = ROT + IDX_ROT
    N = TILES * NF
    TWO_PI = 2 * np.pi
    part1 = float(np.float32(6.28125))
    part2 = float(np.float32(int((TWO_PI - part1) * 2 ** 21) / 2 ** 21))
    part3 = float(np.float32(TWO_PI - part1 - part2))
    MAGIC = float(1.5 * 2 ** 23)
    with ExitStack() as ctx:
        sb = lambda n, s, d=F32: ctx.enter_context(nc.sbuf_tensor("ro_" + n, s, d))
        S = Signals(nc, "ro")
        pos_i, pos, freq = sb("pos_i", [P, TILES], I32), sb("pos", [P, TILES]), sb("freq", [P, NF])
        ang, turns, red = sb("ang", [P, TILES, NF]), sb("turns", [P, TILES, NF]), sb("red", [P, 2, TILES, NF])
        with nc.Block() as block:
            @block.sync
            def _(sp):
                sp.dma_start(pos_i[:, :], A["positions_2_ch"]).then_inc(S["loaded"], 16)
                sp.dma_start(freq[:, :], row(A["k_freq"])).then_inc(S["loaded"], 16)

            @block.vector
            def _(dve):
                ch = Chain(dve, S["dve_step"])
                v = nc.vector
                dve.wait_ge(S["loaded"], 32)
                ch.link(v.tensor_copy(pos[:, :], pos_i[:, :]))
                ch.link(v.tensor_tensor(ang[:, :, :], spread(pos[:, :].unsqueeze(2), [P, TILES, NF]),
                                        spread(freq[:, :].unsqueeze(1), [P, TILES, NF]), ALU.mult))
                for which, quarter in ((0, 0.25), (1, 0.0)):
                    r = red[:, which, :, :]
                    ch.link(v.tensor_scalar(turns[:, :, :], ang[:, :, :], 1.0 / TWO_PI, quarter, ALU.mult, ALU.add))
                    ch.link(v.tensor_scalar(turns[:, :, :], turns[:, :, :], MAGIC, None, ALU.add))
                    ch.link(v.tensor_scalar(turns[:, :, :], turns[:, :, :], MAGIC, None, ALU.subtract))
                    ch.link(v.scalar_tensor_tensor(r, turns[:, :, :], -part1, ang[:, :, :], ALU.mult, ALU.add))
                    ch.link(v.scalar_tensor_tensor(r, turns[:, :, :], -part2, r, ALU.mult, ALU.add))
                    ch.link(v.scalar_tensor_tensor(r, turns[:, :, :], -part3, r, ALU.mult, ALU.add))
                    ch.link(v.tensor_scalar(r, r, quarter * TWO_PI, None, ALU.add))
                    for beyond, bound in ((ALU.is_gt, np.pi), (ALU.is_lt, -np.pi)):
                        ch.link(v.tensor_scalar(turns[:, :, :], r, float(bound), -2.0 * float(bound), beyond, ALU.mult))
                        ch.link(v.tensor_tensor(r, r, turns[:, :, :], ALU.add))
                    ch.link(v.tensor_scalar(r, r, 3.1415925, -3.1415925, ALU.min, ALU.max))
                v.memset(pos[:, :], 0.0).then_inc(S["reduced"], 1)

            @block.scalar
            def _(act):
                act.wait_ge(S["reduced"], 1)
                for which in range(2):
                    nc.scalar.activation(tables[:, :, which, :], red[:, which, :, :], ACT.Sin)
        S.close()


def projections(nc, A, x1, stage, tables, const):
    ident = const["ident"]
    with ExitStack() as ctx:
        sb = lambda n, s: ctx.enter_context(nc.sbuf_tensor("p2_" + n, s, F32))
        S = Signals(nc, "p2")
        B = [ctx.enter_context(nc.psum_tensor(f"p2_bank{i}", [P, 512], F32)) for i in range(8)]
        w = sb("w", [P, KD, IN2])
        g_ch, pscale = sb("g_ch", [P, KD]), sb("pscale", [P, POOL_GROUPS])
        pw = sb("pw", [P, POOL_GROUPS, P])
        mb = sb("mb", [P, 512])
        ones = sb("ones", [P, P])
        qk_g = sb("qk_g", [P, 10, HEAD])
        xt, xn, hT = sb("xt", [P, D]), sb("xn", [P, D]), sb("hT", [P, KD, P])
        stat, numbers = sb("stat", [P, 2]), sb("numbers", [P, 4, 10])
        NEG_HALF, PER_D, PER_HEAD, EPS_ = range(4)
        pr = sb("pr", [P, C2_ZA])
        qk = sb("qk", [P, 10, HEAD])
        ssq, rsq = sb("ssq", [P, 10]), sb("rsq", [P, 10])
        cs = sb("cs", [P, 2, ROT + IDX_ROT])
        r4 = sb("r4", [P, 4, 10, ROT])
        ki4 = sb("ki4", [P, 4, IDX_DIM])
        u = sb("u", [P, POOL_GROUPS, HIST + P])
        w1, w2 = sb("w1", [P, POOL_GROUPS, HIST + P]), sb("w2", [P, POOL_GROUPS, HIST + P])
        inv = sb("inv", [P, POOL_GROUPS, P])
        zb = sb("zb", [P, POOL_GROUPS, P])
        st = sb("st", [P, T_END])
        flat = lambda ap: ap.rearrange("p a b -> p (a b)")
        with nc.Block() as block:
            @block.sync
            def _(sp):
                load = lambda dst, src: sp.dma_start(dst, src).then_inc(S["weights_loaded"], 16)
                src = A["w_in_2"][0].rearrange("(k p) n -> p k n", p=P)
                for k in range(KD):
                    load(w[:, k, :], src[:, k, :])
                load(g_ch[:, :], A["norm_g_2_ch"])
                load(pscale[:, :], A["pool_scale_2_ch"])
                load(pw[:, :, :], A["pool_w_2"][0].rearrange("g c d -> c g d"))
                for r in range(4):
                    load(mb[32 * r:32 * r + 1, :], A["merge_bias_2"][0, r // 2:r // 2 + 1, (r % 2) * 512:(r % 2) * 512 + 512])
                load(qk_g[:, 0:8, :], A["q_norm_g_2"].unsqueeze(1).broadcast_to([P, 8, HEAD]))
                load(qk_g[:, 8:10, :], A["k_norm_g_2"].unsqueeze(1).broadcast_to([P, 2, HEAD]))
                load(inv[:, :, :], A["k_inv"][0])
                with sp.Fori(0, TILES) as i:
                    n = sp.snap(i + 1)
                    sp.wait_ge(S["xn_ready"], i)
                    sp.dma_start(xt[:, :], x1[bass.ds(i * P, P), :]).then_inc(S["x_loaded"], 16)
                    sp.wait_ge(S["pooled_ready"], n)
                    sp.dma_start(inv[:, :, :], A["k_inv"][1]).then_inc(S["inv_ready"], 16)
                    sp.wait_ge(S["bT_ready"], n)
                    sp.wait_ge(S["gates23_taken"], n)
                    sp.dma_start(stage[bass.ds(i * P, P), :], st[:, :]).then_inc(S["stage_stored"], 16)
                sp.wait_ge(S["stage_stored"], 16 * TILES)

            N_WEIGHTS = 16 * (KD + 3 + 4 + 3)

            @block.gpsimd
            def _(pool):
                ch = Chain(pool, S["pool_step"])
                for at, value in enumerate((-0.5, 1.0 / D, 1.0 / HEAD, EPS)):
                    nc.gpsimd.memset(numbers[:, at, :], value)
                nc.gpsimd.memset(u[:, :, :], 0.0)
                nc.gpsimd.memset(w1[:, :, :], 0.0)
                nc.gpsimd.memset(w2[:, :, :], 0.0)
                ch.link(nc.gpsimd.memset(stat[:, :], 0.0))
                nc.gpsimd.memset(ones[:, :], 1.0).then_inc(S["setup_done"], 1)
                ch.start_over()

                def inv_sqrt(out, sums, n, per):
                    ch.link(nc.gpsimd.tensor_tensor(sums, sums, numbers[:, per, 0:n], ALU.mult))
                    ch.link(nc.gpsimd.tensor_tensor(sums, sums, numbers[:, EPS_, 0:n], ALU.add))
                    return nc.gpsimd.tensor_tensor(out, sums, numbers[:, NEG_HALF, 0:n], ALU.pow)

                with pool.Fori(0, TILES) as i:
                    n = pool.snap(i + 1)
                    pool.wait_ge(S["x_squares"], n)
                    inv_sqrt(stat[:, 1:2], stat[:, 0:1], 1, PER_D).then_inc(S["x_rstd"], 1)
                    pool.wait_ge(S["qk_squares"], n)
                    inv_sqrt(rsq[:, :], ssq[:, :], 10, PER_HEAD).then_inc(S["qk_rstd"], 1)
                    ch.start_over()

            @block.tensor
            def _(pe):
                mm, tr = nc.tensor.matmul, nc.tensor.transpose
                pe.wait_ge(S["weights_loaded"], N_WEIGHTS)
                pe.wait_ge(S["setup_done"], 1)
                with pe.Fori(0, TILES) as i:
                    n = pe.snap(i + 1)

                    def tokens(out, c, width, name):
                        for k in range(KD):
                            last = mm(out, hT[:, k, :], w[:, k, c:c + width], start=(k == 0), stop=(k == KD - 1))
                        last.then_inc(S[name], 1)

                    def channels(bank, c, name):
                        for m in range(4):
                            for k in range(KD):
                                last = mm(bank[:, m * P:(m + 1) * P], w[:, k, c + m * P:c + (m + 1) * P], hT[:, k, :], start=(k == 0), stop=(k == KD - 1))
                        last.then_inc(S[name], 1)

                    def gate(bank, r, name):
                        for k in range(KD):
                            mm(bank[:, :], hT[:, k, :], w[:, k, C2_GATES + r * 512:C2_GATES + (r + 1) * 512], start=(k == 0), stop=False)
                        mm(bank[:, :], ones[32 * r:32 * r + 1, :], mb[32 * r:32 * r + 1, :], start=False, stop=True).then_inc(S[name], 1)

                    pe.wait_ge(S["xn_ready"], n)
                    pe.wait_ge(S["gates01_taken"], i)
                    for k in range(KD):
                        last = tr(B[k // 4][:, (k % 4) * P:(k % 4 + 1) * P], xn[:, k * P:(k + 1) * P], ident[:, :])
                        if k % 4 == 3:
                            last.then_inc(S["x_turned"], 1)
                    pe.wait_ge(S["hT_act"], n)
                    pe.wait_ge(S["hT_dve"], n)
                    pe.wait_ge(S["gates23_taken"], i)
                    tokens(B[2][:, :], C2_Q, 512, "q_proj")
                    tokens(B[3][:, :], C2_K, 512, "kv_proj")
                    pe.wait_ge(S["qT_taken"], i)
                    tokens(B[4][:, 0:40], C2_KI, 40, "ki_proj")
                    pe.wait_ge(S["bT_ready"], i)
                    channels(B[6], C2_U, "u_proj")
                    channels(B[7], C2_ZB, "zb_proj")
                    pe.wait_ge(S["kT_taken"], i)
                    tokens(B[5][:, :], C2_ZA, 512, "za_proj")
                    gate(B[0], 0, "gate0")
                    gate(B[1], 1, "gate1")
                    pe.wait_ge(S["qk_ready"], n)
                    pe.wait_ge(S["pr_taken"], n)
                    pr_qk = flat(qk[:, :, :])
                    for c in range(4):
                        last = tr(B[4][:, c * P:(c + 1) * P], pr_qk[:, c * P:(c + 1) * P], ident[:, :])
                    last.then_inc(S["q_turned"], 1)
                    pe.wait_ge(S["za_ready"], n)
                    tr(B[5][:, 0:P], pr_qk[:, 512:640], ident[:, :])
                    tr(B[5][:, P:2 * P], flat(ki4[:, :, :]), ident[:, :])
                    for c in range(2):
                        last = tr(B[5][:, (2 + c) * P:(3 + c) * P], pr[:, C2_QI + c * P:C2_QI + (c + 1) * P], ident[:, :])
                    last.then_inc(S["k_turned"], 1)
                    pe.wait_ge(S["pooled_ready"], n)
                    for g in range(POOL_GROUPS):
                        last = mm(B[6][:, g * P:(g + 1) * P], pw[:, g, :], w1[:, g, 0:P], start=True, stop=True)
                    last.then_inc(S["pool_mixed"], 1)
                    gate(B[2], 2, "gate2")
                    gate(B[3], 3, "gate3")

            @block.scalar
            def _(act):
                f = nc.scalar.activation
                act.wait_ge(S["weights_loaded"], N_WEIGHTS)
                act.wait_ge(S["setup_done"], 1)
                with act.Fori(0, TILES) as i:
                    n = act.snap(i + 1)
                    act.wait_ge(S["x_loaded"], n * 16)
                    act.wait_ge(S["x_turned"], 2 * i)
                    f(xn[:, :], xt[:, :], ACT.Square, accum_out=stat[:, 0:1]).then_inc(S["x_squares"], 1)
                    act.wait_ge(S["x_rstd"], n)
                    f(xn[:, :], xt[:, :], ACT.Copy, scale=stat[:, 1:2]).then_inc(S["xn_ready"], 1)
                    act.wait_ge(S["gate3"], i)
                    act.wait_ge(S["x_turned"], 2 * i + 1)
                    for k in range(4):
                        last = f(hT[:, k, :], B[0][:, k * P:(k + 1) * P], ACT.Copy, scale=g_ch[:, k:k + 1])
                    last.then_inc(S["hT_act"], 1)
                    act.wait_ge(S["q_proj"], n)
                    act.wait_ge(S["k_turned"], i)
                    f(pr[:, 0:512], B[2][:, :], ACT.Copy).then_inc(S["q_taken"], 1)
                    act.wait_ge(S["stage_stored"], i * 16)
                    act.wait_ge(S["zb_proj"], n)
                    f(flat(zb[:, :, :]), B[7][:, :], ACT.Sigmoid).then_inc(S["zb_sigmoid"], 1)
                    act.wait_ge(S["za_proj"], n)
                    f(st[:, T_ZA:T_ZA + 512], B[5][:, :], ACT.Sigmoid).then_inc(S["za_sigmoid"], 1)
                    for r in range(2):
                        act.wait_ge(S[f"gate{r}"], n)
                        last = f(st[:, T_G + 512 * r:T_G + 512 * (r + 1)], B[r][:, :], ACT.Sigmoid)
                    last.then_inc(S["gates01_taken"], 1)
                    act.wait_ge(S["q_turned"], n)
                    f(st[:, T_QT:T_QT + 512], B[4][:, :], ACT.Copy).then_inc(S["qT_taken"], 1)
                    for r in range(2, 4):
                        act.wait_ge(S[f"gate{r}"], n)
                        last = f(st[:, T_G + 512 * r:T_G + 512 * (r + 1)], B[r][:, :], ACT.Sigmoid)
                    last.then_inc(S["gates23_taken"], 1)

            @block.vector
            def _(dve):
                ch = Chain(dve, S["dve_step"])
                v = nc.vector
                tt, ts, stt = v.tensor_tensor, v.tensor_scalar, v.scalar_tensor_tensor
                dve.wait_ge(S["weights_loaded"], N_WEIGHTS)
                dve.wait_ge(S["setup_done"], 1)

                def rotate(vectors, cos, sin, half):
                    heads = vectors.shape[1]
                    a, b = vectors[:, :, 0:half], vectors[:, :, half:2 * half]
                    c, s_ = spread(cos.unsqueeze(1), [P, heads, half]), spread(sin.unsqueeze(1), [P, heads, half])
                    t = [r4[:, e, 0:heads, 0:half] for e in range(4)]
                    tt(t[0], a, c, ALU.mult)
                    tt(t[1], b, s_, ALU.mult)
                    tt(t[2], a, s_, ALU.mult)
                    ch.link(tt(t[3], b, c, ALU.mult))
                    tt(a, t[0], t[1], ALU.subtract)
                    return tt(b, t[2], t[3], ALU.add)

                with dve.Fori(0, TILES) as i:
                    n = dve.snap(i + 1)
                    v.tensor_copy(cs[:, :, :], tables[:, bass.ds(i, 1), :, :].rearrange("p a b c -> p (a b) c"))
                    dve.wait_ge(S["gate3"], i)
                    dve.wait_ge(S["x_turned"], 2 * n)
                    for k in range(4, 8):
                        last = ts(hT[:, k, :], B[1][:, (k - 4) * P:(k - 3) * P], g_ch[:, k:k + 1], None, ALU.mult)
                    last.then_inc(S["hT_dve"], 1)
                    dve.wait_ge(S["kv_proj"], n)
                    dve.wait_ge(S["k_turned"], i)
                    v.tensor_copy(pr[:, 512:1024], B[3][:, :])
                    dve.wait_ge(S["ki_proj"], n)
                    v.tensor_copy(pr[:, 1024:1064], B[4][:, 0:40]).then_inc(S["pr_taken"], 1)
                    dve.wait_ge(S["q_taken"], n)
                    dve.wait_ge(S["pr_taken"], n)
                    ch.link(tt(flat(qk[:, :, :]), pr[:, 0:640], pr[:, 0:640], ALU.mult))
                    v.tensor_reduce(ssq[:, :], qk[:, :, :], AX.X, ALU.add).then_inc(S["qk_squares"], 1)
                    ch.link(rotate(pr[:, C2_QI:C2_QI + 9 * IDX_DIM].rearrange("p (h d) -> p h d", d=IDX_DIM), cs[:, 0, ROT:], cs[:, 1, ROT:], IDX_ROT))
                    v.tensor_copy(ki4[:, :, :], spread(pr[:, C2_KI:C2_KI + IDX_DIM].unsqueeze(1), [P, 4, IDX_DIM]))
                    dve.wait_ge(S["stage_stored"], i * 16)
                    v.tensor_copy(st[:, T_V:T_V + P], pr[:, C2_V:C2_V + P])
                    wi, mag, sgn = pr[:, 1056:1064], st[:, T_W:T_W + 8], st[:, T_W + 8:T_W + 16]
                    ch.link(stt(mag, wi, -1.0, wi, ALU.mult, ALU.max))
                    ch.link(ts(mag, mag, 1.0 / 16.0, None, ALU.mult))
                    ch.link(ts(sgn, wi, 0.0, 2.0, ALU.is_ge, ALU.mult))
                    ch.link(ts(sgn, sgn, -1.0, None, ALU.add))
                    dve.wait_ge(S["qk_rstd"], n)
                    q_in = pr[:, 0:512].rearrange("p (g c d) -> p g c d", g=2, c=4)
                    q_out = flat(qk[:, 0:8, :]).rearrange("p (c g d) -> p g c d", g=2, c=4)
                    for g in range(2):
                        tt(q_out[:, g], q_in[:, g], spread(rsq[:, 4 * g:4 * g + 4].unsqueeze(2), [P, 4, HEAD]), ALU.mult)
                    ch.link(tt(qk[:, 8:10, :], pr[:, 512:640].rearrange("p (h d) -> p h d", d=HEAD), spread(rsq[:, 8:10].unsqueeze(2), [P, 2, HEAD]), ALU.mult))
                    ch.link(tt(flat(qk[:, :, :]), flat(qk[:, :, :]), flat(qk_g[:, :, :]), ALU.mult))
                    rotate(qk[:, :, :], cs[:, 0, 0:ROT], cs[:, 1, 0:ROT], ROT).then_inc(S["qk_ready"], 1)
                    dve.wait_ge(S["u_proj"], n)
                    dve.wait_ge(S["pool_mixed"], i)
                    ch.link(v.tensor_copy(u[:, :, HIST:], B[6][:, :].rearrange("p (g t) -> p g t", t=P)))
                    E = HIST + P
                    ch.link(tt(w1[:, :, 1:E], u[:, :, 1:E], u[:, :, 0:E - 1], ALU.add))
                    ch.link(tt(w2[:, 1:4, 3:E], w1[:, 1:4, 3:E], w1[:, 1:4, 1:E - 2], ALU.add))
                    ch.link(tt(w1[:, 2:4, 7:E], w2[:, 2:4, 7:E], w2[:, 2:4, 3:E - 4], ALU.add))
                    ch.link(tt(w2[:, 3:4, 15:E], w1[:, 3:4, 15:E], w1[:, 3:4, 7:E - 8], ALU.add))
                    dve.wait_ge(S["inv_ready"], i * 16)
                    for g, full in enumerate((w1, w2, w1, w2)):
                        last = tt(w2[:, g, HIST:], full[:, g, HIST:], inv[:, g, :], ALU.mult)
                    ch.link(last)
                    tt(w1[:, :, 0:P], w2[:, :, HIST:], u[:, :, HIST:], ALU.subtract).then_inc(S["pooled_ready"], 1)
                    dve.wait_ge(S["pooled_ready"], n)
                    ch.link(v.tensor_copy(u[:, :, 0:HIST], u[:, :, P:P + HIST]))
                    dve.wait_ge(S["zb_sigmoid"], n)
                    ch.link(tt(flat(zb[:, :, :]), B[7][:, :], flat(zb[:, :, :]), ALU.mult))
                    dve.wait_ge(S["za_sigmoid"], n)
                    tt(st[:, T_ZA:T_ZA + 512], B[5][:, :], st[:, T_ZA:T_ZA + 512], ALU.mult).then_inc(S["za_ready"], 1)
                    dve.wait_ge(S["k_turned"], n)
                    v.tensor_copy(st[:, T_KT:T_KT + 2 * P], B[5][:, 0:2 * P])
                    v.tensor_copy(st[:, T_QI:T_QI + 256], B[5][:, 256:512]).then_inc(S["kT_taken"], 1)
                    dve.wait_ge(S["pool_mixed"], n)
                    for g in range(POOL_GROUPS):
                        last = stt(st[:, T_BT + g * P:T_BT + (g + 1) * P], B[6][:, g * P:(g + 1) * P], pscale[:, g:g + 1], zb[:, g, :], ALU.mult, ALU.mult)
                    last.then_inc(S["bT_ready"], 1)
                    ch.start_over()
        S.close()
BLK = 512
GROUP = BLK // P
HALVINGS = 25
BIG = 8.0e30
LEAST = 1.0e-30


class Turn:

    def __init__(self, blocks, a, b, in_group, units_a, units_b):
        self.blocks, self.a, self.b, self.in_group = blocks, a, b, in_group
        self.units_a, self.units_b = units_a, units_b
        self.width = blocks * BLK


def turns(eng):
    yield Turn(1, 0, None, 0, 0, 0)
    units_a, units_b = 8, 0
    for g in range(TILES // GROUP):
        first = max(g * GROUP, 1)
        count, per = (g + 1) * GROUP - first, 8 * (g + 1)
        with eng.Fori(0, count) as i:
            yield Turn(g + 1, eng.snap(i + first), eng.snap(i + (first - 1)), i + (first - g * GROUP),
                       i * per + units_a, i * per + units_b)
        units_a, units_b = units_a + count * per, units_b + count * per
    yield Turn(TILES // GROUP, None, TILES - 1, 0, 0, units_b)


def attention(nc, A, x1, stage, out, const):
    ident = const["ident"]
    with ExitStack() as ctx:
        sb = lambda n, s: ctx.enter_context(nc.sbuf_tensor("at_" + n, s, F32))
        S = Signals(nc, "at")
        B = [ctx.enter_context(nc.psum_tensor(f"at_bank{i}", [P, 512], F32)) for i in range(8)]
        LOGIT, SCORE, TURNED, OUT = B[0:2], B[2:4], B[4:6], B[6]
        KT, KI, VC = sb("KT", [P, SEQ]), sb("KI", [P, SEQ]), sb("VC", [P, TILES, P])
        wa, wb, wo = sb("wa", [P, 4, D]), sb("wb", [P, 4, D]), sb("wo", [P, KD, D])
        halves, allowed = sb("halves", [P, HALVINGS]), sb("allowed", [P, BLK + 3 * P])
        ones = sb("ones", [P, 1])
        qi = sb("qi", [P, 272])
        qT, rest = sb("qT", [P, 4, P]), sb("rest", [P, T_KT - T_ZA])
        x = sb("x", [P, D])
        r = sb("r", [P, 4, BLK])
        acc, bias = sb("acc", [P, SEQ]), sb("bias", [P, SEQ])
        tie, over, run = sb("tie", [P, SEQ]), sb("over", [P, SEQ]), sb("run", [P, SEQ])
        mid, cnt, width = sb("mid", [P, 4]), sb("cnt", [P, 4]), sb("width", [P, HALVINGS])
        s = sb("s", [P, 2, SEQ])
        pT = sb("pT", [P, 2, TILES, P])
        mx, nm, den = sb("mx", [P, 2, 4]), sb("nm", [P, 8]), sb("den", [P, 8])
        at, aT = sb("a", [P, 512]), sb("aT", [P, 4, P])
        y, yT, o = sb("y", [P, D]), sb("yT", [P, KD, P]), sb("o", [P, D])
        za, bT = rest[:, 0:512], rest[:, T_BT - T_ZA:T_G - T_ZA]
        gates = rest[:, T_G - T_ZA:T_KT - T_ZA]
        flat = lambda ap: ap.rearrange("p a b -> p (a b)")
        rows_of = lambda t: bass.ds(t * P, P)
        FIRST_STEPS = 2
        tests = [0, 0] + [HALVINGS // 6 + (1 if e < HALVINGS % 6 else 0) for e in range(6)]

        with nc.Block() as block:
            @block.sync
            def _(sp):
                load = lambda dst, src: sp.dma_start(dst, src).then_inc(S["constants_loaded"], 16)
                by_tile = stage.rearrange("(t p) c -> p t c", p=P)
                load(KI[:, :].rearrange("p (t c) -> p t c", c=P), by_tile[:, :, T_KI:T_KI + P])
                load(halves[:, :], row(A["k_halves"]))
                load(allowed[:, :], A["k_allowed"])
                load(KT[:, :].rearrange("p (t c) -> p t c", c=P), by_tile[:, :, T_KT:T_KT + P])
                load(VC[:, :, :], by_tile[:, :, T_V:T_V + P])
                load(wa[:, :, :], A["w_branch_a_2"][0].rearrange("(k p) n -> p k n", p=P))
                load(wb[:, :, :], A["w_branch_b_2"][0].rearrange("(k p) n -> p k n", p=P))
                load(wo[:, :, :], A["w_out_2"][0].rearrange("(k p) n -> p k n", p=P))
                for t in turns(sp):
                    if t.a is not None:
                        sp.wait_ge(S["index_done"], t.a)
                        sp.dma_start(qi[:, :], stage[rows_of(t.a), T_QI:T_ZA]).then_inc(S["qi_loaded"], 16)
                    if t.b is not None:
                        sp.wait_ge(S["pv_done"], t.b * 8)
                        sp.dma_start(flat(qT[:, :, :]), stage[rows_of(t.b), T_QT:T_QT + 512]).then_inc(S["qT_loaded"], 16)
                        sp.wait_ge(S["out_ready"], t.b)
                        sp.dma_start(rest[:, :], stage[rows_of(t.b), T_ZA:T_KT]).then_inc(S["rest_loaded"], 16)
                        sp.dma_start(x[:, :], x1[rows_of(t.b), :]).then_inc(S["rest_loaded"], 16)

            N_CONST = 16 * 8

            @block.gpsimd
            def _(pool):
                ch = Chain(pool, S["pool_step"])
                nc.gpsimd.memset(bias[:, :], -BIG)
                ch.link(nc.gpsimd.memset(mid[:, :], 0.0))
                nc.gpsimd.memset(ones[:, :], 1.0).then_inc(S["setup_done"], 1)
                for t in turns(pool):
                    if t.b is not None:
                        pool.wait_ge(S["out_ready"], t.b + 1)
                        pool.dma_start(out[rows_of(t.b), :], o[:, :]).then_inc(S["out_stored"], 16)
                pool.wait_ge(S["out_stored"], 16 * TILES)

            @block.tensor
            def _(pe):
                mm, tr = nc.tensor.matmul, nc.tensor.transpose
                pe.wait_ge(S["constants_loaded"], N_CONST)
                for t in turns(pe):
                    n = t.blocks

                    def index_products(h):
                        rows_h = slice(32 * (h % 4), 32 * (h % 4) + 32)
                        for kb in range(n):
                            j = h * n + kb
                            if not (isinstance(t.units_a, int) and t.units_a + j < 2):
                                pe.wait_ge(S["relu_done"], t.units_a + (j - 1))
                            mm(LOGIT[j % 2][:, :], qi[rows_h, (h // 4) * P:(h // 4 + 1) * P], KI[rows_h, kb * BLK:(kb + 1) * BLK],
                               start=True, stop=True).then_inc(S["logits"], 1)

                    def score_products(h):
                        g = slice(64 * (h // 4), 64 * (h // 4) + 64)
                        for kb in range(n):
                            j = h * n + kb
                            pe.wait_ge(S["masked"], t.units_b + (j + 1))
                            mm(SCORE[j % 2][:, :], qT[g, h % 4, :], KT[g, kb * BLK:(kb + 1) * BLK], start=True, stop=True).then_inc(S["scores"], 1)

                    def turn_probabilities(h):
                        pe.wait_ge(S["probs"], t.b * 8 + (h + 1))
                        for kb in range(n):
                            j = h * n + kb
                            pe.wait_ge(S["pT_taken"], t.units_b + (j + 1))
                            for e in range(GROUP):
                                last = tr(TURNED[j % 2][:, e * P:(e + 1) * P], s[:, h % 2, kb * BLK + e * P:kb * BLK + (e + 1) * P], ident[:, :])
                            last.then_inc(S["probs_turned"], 1)

                    def values(h):
                        pe.wait_ge(S["pT_taken"], t.units_b + ((h + 1) * n + 2))
                        for kt in range(GROUP * n):
                            last = mm(OUT[:, h * 64:(h + 1) * 64], pT[:, h % 2, kt, :], VC[:, kt, 64 * (h // 4):64 * (h // 4) + 64],
                                      start=(kt == 0), stop=(kt == GROUP * n - 1))
                        last.then_inc(S["pv_done"], 1)

                    if t.a is not None:
                        pe.wait_ge(S["qi_loaded"], t.a * 16 + 16)
                    if t.b is not None:
                        pe.wait_ge(S["qT_loaded"], t.b * 16 + 16)
                        pe.wait_ge(S["out_ready"], t.b)
                        score_products(0)
                    for h in range(8):
                        if t.a is not None and h < FIRST_STEPS:
                            for e in range(4 * h, 4 * h + 4):
                                index_products(e)
                        if t.b is None:
                            continue
                        if h < 7:
                            score_products(h + 1)
                        turn_probabilities(h)
                        if h > 0:
                            values(h - 1)
                    if t.b is None:
                        continue
                    values(7)
                    pe.wait_ge(S["a_ready"], t.b + 1)
                    for c in range(4):
                        last = tr(TURNED[0][:, c * P:(c + 1) * P], at[:, c * P:(c + 1) * P], ident[:, :])
                    last.then_inc(S["a_turned"], 1)
                    pe.wait_ge(S["rest_loaded"], t.b * 32 + 32)
                    for half in range(2):
                        for k in range(4):
                            last = mm((B[7], TURNED[1])[half][:, :], bT[:, k * P:(k + 1) * P], wb[:, k, half * 512:(half + 1) * 512], start=(k == 0), stop=(k == 3))
                    pe.wait_ge(S["aT_ready"], t.b + 1)
                    for half in range(2):
                        for k in range(4):
                            last = mm(SCORE[half][:, :], aT[:, k, :], wa[:, k, half * 512:(half + 1) * 512], start=(k == 0), stop=(k == 3))
                    last.then_inc(S["branches_done"], 1)
                    pe.wait_ge(S["y_ready"], t.b + 1)
                    for k in range(KD):
                        last = tr(SCORE[k // 4][:, (k % 4) * P:(k % 4 + 1) * P], y[:, k * P:(k + 1) * P], ident[:, :])
                    last.then_inc(S["y_turned"], 1)
                    pe.wait_ge(S["yT_ready"], t.b + 1)
                    for half in range(2):
                        for k in range(KD):
                            last = mm(TURNED[half][:, :], yT[:, k, :], wo[:, k, half * 512:(half + 1) * 512], start=(k == 0), stop=(k == KD - 1))
                    last.then_inc(S["projected"], 1)

            @block.scalar
            def _(act):
                f = nc.scalar.activation
                act.sem_inc(S["pT_taken"], 2)
                for t in turns(act):
                    n = t.blocks
                    if t.a is not None:
                        act.wait_ge(S["qi_loaded"], t.a * 16 + 16)

                    def index_relu(h):
                        for kb in range(n):
                            j = h * n + kb
                            act.wait_ge(S["logits"], t.units_a + (j + 1))
                            if not (isinstance(t.units_a, int) and t.units_a + j < 4):
                                act.wait_ge(S["summed"], t.units_a + (j - 3))
                            f(r[:, j % 4, :], LOGIT[j % 2][:, :], ACT.Relu, scale=qi[:, 256 + h:257 + h]).then_inc(S["relu_done"], 1)

                    for h in range(8):
                        if t.b is not None:
                            act.wait_ge(S["row_max"], t.b * 8 + (h + 1))
                            f(s[:, h % 2, 0:t.width], s[:, h % 2, 0:t.width], ACT.Exp, bias=nm[:, h:h + 1], accum_out=den[:, h:h + 1]).then_inc(S["probs"], 1)
                        if t.a is not None and h < FIRST_STEPS:
                            for e in range(4 * h, 4 * h + 4):
                                index_relu(e)
                        if t.b is not None:
                            if h >= 2:
                                act.wait_ge(S["pv_done"], t.b * 8 + (h - 1))
                            for kb in range(n):
                                j = h * n + kb
                                act.wait_ge(S["probs_turned"], t.units_b + (j + 1))
                                f(flat(pT[:, h % 2, kb * GROUP:(kb + 1) * GROUP, :]), TURNED[j % 2][:, :], ACT.Copy).then_inc(S["pT_taken"], 1)
                    if t.b is not None:
                        act.wait_ge(S["a_turned"], t.b + 1)
                        f(flat(aT[:, :, :]), TURNED[0][:, :], ACT.Copy).then_inc(S["aT_ready"], 1)
                        act.wait_ge(S["y_turned"], t.b + 1)
                        f(flat(yT[:, 0:4, :]), SCORE[0][:, :], ACT.Copy)
                        f(flat(yT[:, 4:8, :]), SCORE[1][:, :], ACT.Copy).then_inc(S["yT_ready"], 1)

            @block.vector
            def _(dve):
                ch = Chain(dve, S["dve_step"])
                v = nc.vector
                tt, ts, stt = v.tensor_tensor, v.tensor_scalar, v.scalar_tensor_tensor
                dve.sem_inc(S["masked"], 2)
                dve.wait_ge(S["constants_loaded"], N_CONST)
                dve.wait_ge(S["setup_done"], 1)
                for t in turns(dve):
                    n, L = t.blocks, t.width

                    def index_sum(h):
                        sgn = qi[:, 264 + h:265 + h]
                        for kb in range(n):
                            j = h * n + kb
                            dve.wait_ge(S["relu_done"], t.units_a + (j + 1))
                            part = acc[:, kb * BLK:(kb + 1) * BLK]
                            if h == 0:
                                last = ts(part, r[:, j % 4, :], sgn, None, ALU.mult)
                            else:
                                dve.wait_ge(S["summed"], t.units_a + (j - n + 1))
                                last = stt(part, r[:, j % 4, :], sgn, part, ALU.mult, ALU.add)
                            last.then_inc(S["summed"], 1)

                    def search_range():
                        dve.wait_ge(S["summed"], t.units_a + 8 * n)
                        ch.link(v.tensor_reduce(cnt[:, 1:2], acc[:, 0:L], AX.X, ALU.max, apply_absolute_value=True))
                        ch.link(ts(cnt[:, 1:2].bitcast(I32), cnt[:, 1:2].bitcast(I32), 0x7f800000, None, ALU.bitwise_and))
                        ch.link(ts(cnt[:, 1:2], cnt[:, 1:2], 2.0, LEAST, ALU.mult, ALU.max))
                        ts(width[:, :], halves[:, :], cnt[:, 1:2], None, ALU.mult)
                        v.memset(mid[:, 0:1], 0.0)
                        start = t.in_group * (-P) + 3 * P
                        last_block = acc[:, L - BLK:L]
                        tt(last_block, last_block, allowed[:, bass.ds(start, BLK)], ALU.add).then_inc(S["index_done"], 1)
                        dve.wait_ge(S["index_done"], t.a + 1)

                    def halve(k):
                        ch.link(ts(run[:, 0:L], acc[:, 0:L], mid[:, 0:1], 0.0, ALU.is_ge, ALU.add, accum_out=cnt[:, 0:1]))
                        if k < HALVINGS - 1:
                            ch.link(ts(cnt[:, 2:3], cnt[:, 0:1], TOPK - 0.5, -0.5, ALU.is_ge, ALU.add))
                            ch.link(stt(mid[:, 0:1], cnt[:, 2:3], width[:, k:k + 1], mid[:, 0:1], ALU.mult, ALU.add))
                        else:
                            ch.link(ts(cnt[:, 2:3], cnt[:, 0:1], TOPK - 0.5, -1.0, ALU.is_ge, ALU.add))
                            ch.link(stt(mid[:, 1:2], cnt[:, 2:3], width[:, k:k + 1], mid[:, 0:1], ALU.mult, ALU.add))
                            ch.link(tt(mid[:, 2:3], mid[:, 1:2], width[:, k:k + 1], ALU.add))

                    def select():
                        lo, hi = mid[:, 1:2], mid[:, 2:3]
                        ts(tie[:, 0:L], acc[:, 0:L], lo, None, ALU.is_ge)
                        ch.link(ts(over[:, 0:L], acc[:, 0:L], hi, 0.0, ALU.is_ge, ALU.add, accum_out=cnt[:, 0:1]))
                        ch.link(tt(tie[:, 0:L], tie[:, 0:L], over[:, 0:L], ALU.subtract))
                        ts(cnt[:, 3:4], cnt[:, 0:1], -1.0, float(TOPK), ALU.mult, ALU.add)
                        ch.link(v.tensor_tensor_scan(run[:, 0:L], spread(ones[:, :], [P, L]), tie[:, 0:L], 0.0, ALU.mult, ALU.add))
                        ch.link(stt(tie[:, 0:L], run[:, 0:L], cnt[:, 3:4], tie[:, 0:L], ALU.is_le, ALU.mult))
                        ch.link(tt(tie[:, 0:L], tie[:, 0:L], over[:, 0:L], ALU.add))
                        ch.link(ts(bias[:, 0:L], tie[:, 0:L], BIG, -BIG, ALU.mult, ALU.add))

                    def mask(h):
                        if h >= 2:
                            dve.wait_ge(S["probs_turned"], t.units_b + (h - 1) * n)
                        for kb in range(n):
                            j = h * n + kb
                            c = slice(kb * BLK, (kb + 1) * BLK)
                            dve.wait_ge(S["scores"], t.units_b + (j + 1))
                            dve.sem_inc(S["score_seen"], 1)
                            v.tensor_tensor_reduce(out=s[:, h % 2, c], in0=SCORE[j % 2][:, :], in1=bias[:, c], scale=HEAD ** -0.5, scalar=-3.0e38,
                                                   op0=ALU.add, op1=ALU.max, accum_out=mx[:, h % 2, kb:kb + 1]).then_inc(S["masked"], 1)
                        dve.wait_ge(S["masked"], t.units_b + ((h + 1) * n + 2))
                        ch.link(v.tensor_reduce(nm[:, h:h + 1], mx[:, h % 2, 0:n], AX.X, ALU.max))
                        ts(nm[:, h:h + 1], nm[:, h:h + 1], -1.0, None, ALU.mult).then_inc(S["row_max"], 1)

                    if t.a is not None:
                        dve.wait_ge(S["qi_loaded"], t.a * 16 + 16)
                    done = 0
                    for h in range(8):
                        if t.b is not None:
                            mask(h)
                        if t.a is not None:
                            if h < FIRST_STEPS:
                                for e in range(4 * h, 4 * h + 4):
                                    index_sum(e)
                            if h == FIRST_STEPS:
                                search_range()
                            for _k in range(tests[h]):
                                halve(done)
                                done += 1
                    if t.b is not None:
                        dve.wait_ge(S["pv_done"], t.b * 8 + 8)
                        ch.link(v.reciprocal(den[:, :], den[:, :]))
                        hd = lambda ap: ap.rearrange("p (h d) -> p h d", d=HEAD)
                        ch.link(tt(hd(at[:, :]), hd(OUT[:, :]), spread(den[:, :].unsqueeze(2), [P, 8, HEAD]), ALU.mult))
                        dve.wait_ge(S["rest_loaded"], t.b * 32 + 32)
                        tt(at[:, :], at[:, :], za, ALU.mult).then_inc(S["a_ready"], 1)
                    if t.a is not None:
                        select()
                    if t.b is not None:
                        dve.wait_ge(S["branches_done"], t.b + 1)
                        dve.wait_ge(S["out_stored"], t.b * 16)
                        for half in range(2):
                            c = slice(half * 512, (half + 1) * 512)
                            tt(y[:, c], SCORE[half][:, :], gates[:, half * 512:(half + 1) * 512], ALU.mult)
                            last = tt(o[:, c], (B[7], TURNED[1])[half][:, :], gates[:, 1024 + half * 512:1024 + (half + 1) * 512], ALU.mult)
                        ch.link(last)
                        tt(y[:, :], y[:, :], o[:, :], ALU.add).then_inc(S["y_ready"], 1)
                        dve.wait_ge(S["y_ready"], t.b + 1)
                        dve.wait_ge(S["projected"], t.b + 1)
                        for half in range(2):
                            c = slice(half * 512, (half + 1) * 512)
                            last = tt(o[:, c], TURNED[half][:, :], x[:, c], ALU.add)
                        last.then_inc(S["out_ready"], 1)
                    ch.start_over()
        S.close()


def build(nc, A, out):
    with ExitStack() as ctx:
        sb = lambda n, s: ctx.enter_context(nc.sbuf_tensor(n, s, F32))
        dram = lambda n, s: nc.dram_tensor(n, s, F32, kind="Internal").ap()
        const = dict(ident=sb("ident", [P, P]))
        keep = dict(scale_ch=sb("scale_ch", [P, KD]), shift_ch=sb("shift_ch", [P, KD]), gate_row=dram("gate_row", (P, D)))
        mixed, x1, stage = dram("mixed", (SEQ, D)), dram("x1", (SEQ, D)), dram("stage", (SEQ, T_END))
        identity_loaded = nc.alloc_semaphore("identity_loaded")
        with nc.Block() as block:
            @block.sync
            def _(sp):
                sp.dma_start(const["ident"][:, :], A["k_ident"]).then_inc(identity_loaded, 16)
                sp.wait_ge(identity_loaded, 16)
        adaptive_norm(nc, A, keep, const)
        mixers(nc, A, mixed, keep, const)
        output_and_residual(nc, A, mixed, x1, keep, const)
        with nc.sbuf_tensor("tables", [P, TILES, 2, ROT + IDX_ROT], F32) as tables:
            rotary_tables(nc, A, tables)
            projections(nc, A, x1, stage, tables, const)
        attention(nc, A, x1, stage, out, const)


def shape_constants():
    s, t = np.arange(P)[:, None], np.arange(P)[None]
    masks = np.zeros((P, LEVELS, P), np.float32)
    for level in range(LEVELS):
        half = 1 << level
        masks[:, level] = (s // (2 * half) == t // (2 * half)) & (t // half % 2 == 1) & (s // half % 2 == 0)
    one_chunk = s // R_CHUNK == t // R_CHUNK
    tri = np.stack([(s < t) & one_chunk, (s <= t) & one_chunk], axis=1).astype(np.float32)
    quad = (s // G_KEY == np.arange(R_W)[None] // G_VAL).astype(np.float32)
    chunk_of = (s // R_CHUNK == np.arange(2)[None]).astype(np.float32)
    dist = np.arange(P)[:, None] - np.arange(2 * P)[None] + P
    slopes = (2.0 ** -np.arange(1, A_HEADS + 1)).astype(np.float32)
    alibi = np.where(((dist >= 0) & (dist < P))[:, None, :], -slopes[None, :, None] * dist[:, None, :].astype(np.float32), NEG)
    freq8 = ["0x1p+0", "0x1.8d275ep-3", "0x1.34119p-5", "0x1.ddee9cp-8", "0x1.72ba44p-10", "0x1.1f91fp-12", "0x1.be2188p-15", "0x1.5a0f4ep-17"]
    freq = np.array([[float.fromhex(f) for f in freq8 + freq8[::2]]], np.float32)
    inv = np.zeros((2, P, POOL_GROUPS, P), np.float32)
    for g, w in enumerate((2, 4, 8, 16)):
        inv[0, :, g], inv[1, :, g] = 1.0 / np.minimum(np.arange(P) + 1, w), 1.0 / w
    reach = np.arange(BLK + 3 * P)[None] - 3 * P
    allowed = np.where(reach < 64 * (np.arange(P)[:, None] >= 64) + 64, 0.0, NEG)
    return {
        "k_ident": np.eye(P, dtype=np.float32), "k_masks": masks, "k_tri": tri,
        "k_pair": (s // HEAD == t // HEAD).astype(np.float32), "k_quad": quad, "k_chunk_of": chunk_of,
        "k_alibi": alibi.astype(np.float32), "k_freq": freq, "k_inv": inv, "k_allowed": allowed.astype(np.float32),
        "k_halves": (2.0 ** -np.arange(HALVINGS))[None].astype(np.float32),
    }


def kernel(**inputs):
    import concourse.bacc as bacc
    from concourse.bass_utils import run_bass_kernel_spmd as run

    nc = bacc.Bacc("TRN2", target_bir_lowering=False, num_devices=1)
    arrays = {}
    by_column = ("c", "ada_b", "norm_pre", "gla_gk_b", "rwkv_mu_w", "rwkv_mu_a", "rwkv_mu_rkv", "norm_g_2", "pool_scale_2", "positions_2")
    only_so = ("c", "norm_pre", "gla_gk_b", "rwkv_mu_w", "rwkv_mu_a", "rwkv_mu_rkv", "norm_g_2", "pool_scale_2", "positions_2")
    for name, value in inputs.items():
        a = np.ascontiguousarray(value)
        if name in by_column:
            arrays[name + "_ch"] = np.ascontiguousarray(a.reshape(-1, P).T)
        if name not in only_so:
            arrays[name] = a
    arrays.update(shape_constants())
    A, fed = {}, {}
    for name, a in arrays.items():
        fed["in_" + name] = a
        A[name] = nc.dram_tensor("in_" + name, a.shape, mybir.dt.from_np(a.dtype), kind="ExternalInput").ap()
    out = nc.dram_tensor("out", (1, SEQ, D), F32, kind="ExternalOutput").ap()
    build(nc, A, out[0])
    return run(nc, [fed], core_ids=[0]).results[0]["out"]
```

```python
import concourse.bass as bass
from concourse import mybir
from contextlib import ExitStack
import numpy as np

F32 = mybir.dt.float32
I32 = mybir.dt.int32
U32 = mybir.dt.uint32
ALU = mybir.AluOpType
ACT = mybir.ActivationFunctionType
AX = mybir.AxisListType

P = 128
D = 1024
KD = D // P
SEQ = 2048
TILES = SEQ // P
HEAD = 64
EPS = 1e-6
NEG = -1.0e30

A_HEADS, A_KV = 8, 2
C_AQ, C_AK, C_AV, C_AG = 0, 512, 640, 768
C_RKV, C_RG = 1280, 2048
C_GQ, C_GK, C_GV, C_GG = 2304, 2432, 2560, 2816
IN1 = 3072
R_HEADS, R_W, R_CHUNK = 4, 256, 64
RWKV_LN_EPS = 64e-5
G_HEADS, G_KEY, G_VAL = 4, 32, 64
LEVELS = 7
INV_LEVELS = 6


class Signals(dict):

    def __init__(self, nc, phase):
        super().__init__()
        self.nc, self.phase = nc, phase

    def __missing__(self, name):
        self[name] = self.nc.alloc_semaphore(f"{self.phase}_{name}")
        return self[name]

    def close(self):
        self.nc.clear_and_free_semaphores(list(self.values()))
        self.nc.all_engine_barrier()


class Chain:

    def __init__(self, eng, sem):
        self.eng, self.sem, self.count = eng, sem, 0

    def link(self, ins):
        self.count += 1
        ins.then_inc(self.sem, 1)
        self.eng.wait_ge(self.sem, self.count)

    def start_over(self):
        self.eng.sem_clear(self.sem)
        self.count = 0


class Tile:

    def __init__(self, turn, t, n, b, more):
        self.turn, self.t, self.n, self.b, self.more = turn, t, n, b, more


def tile_pairs(eng):
    with eng.Fori(0, TILES // 2 - 1) as i:
        for b in range(2):
            yield Tile(i, eng.snap(2 * i + b), eng.snap(2 * i + (b + 1)), b, True)
    for b in range(2):
        yield Tile(TILES // 2 - 1, TILES - 2 + b, TILES - 1 + b, b, b == 0)


def row(ap_row, n=P):
    return ap_row.broadcast_to([n, ap_row.shape[1]])


def spread(ap, shape):
    return ap.broadcast_to(shape)


def adaptive_norm(nc, A, w_in, w_in_loaded, keep, const):
    g1, sh = keep["scale_ch"], keep["shift_ch"]
    with ExitStack() as ctx:
        sb = lambda n, s: ctx.enter_context(nc.sbuf_tensor("ad_" + n, s, F32))
        S = Signals(nc, "ad")
        ada = sb("w", [P, KD, 3 * D])
        cc, ce, ca = sb("c", [P, KD]), sb("ce", [P, KD]), sb("ca", [P, KD])
        cb = sb("cb", [P, KD, P])
        b_ch, npre = sb("b_ch", [P, 2 * KD]), sb("npre", [P, KD])
        gate_row, np_row = sb("gate_row", [P, D]), sb("np_row", [P, D])
        ps = ctx.enter_context(nc.psum_tensor("ad_ps", [P, 512], F32))
        pg = ctx.enter_context(nc.psum_tensor("ad_pg", [P, 1024], F32))
        with nc.Block() as block:
            @block.sync
            def _(sp):
                sp.dma_start(cc[:, :], A["c_ch"]).then_inc(S["c_loaded"], 16)
                src = A["ada_w"][0].rearrange("(k p) n -> p k n", p=P)
                for c in range(6):
                    cols = slice(c * 512, (c + 1) * 512)
                    sp.dma_start(ada[:, :, cols], src[:, :, cols]).then_inc(S[f"w_loaded{c}"], 16)
                sp.dma_start(b_ch[:, :], A["ada_b_ch"][:, 0:2 * KD]).then_inc(S["small_loaded"], 16)
                sp.dma_start(npre[:, :], A["norm_pre_ch"]).then_inc(S["small_loaded"], 16)
                sp.dma_start(gate_row[:, :], row(A["ada_b"][0:1, 2 * D:3 * D])).then_inc(S["small_loaded"], 16)
                sp.dma_start(np_row[:, :], row(A["norm_post"][0:1, :])).then_inc(S["small_loaded"], 16)
                wsrc = A["w_in"][0].rearrange("(k p) n -> p k n", p=P)
                for k in range(KD):
                    sp.dma_start(w_in[:, k, 512:], wsrc[:, k, 512:]).then_inc(w_in_loaded, 16)
                    for g in range(A_KV):
                        sp.dma_start(w_in[:, k, 0:512].rearrange("p (c g d) -> p g c d", g=2, d=HEAD)[:, g],
                                     wsrc[:, k, 256 * g:256 * g + 256].rearrange("p (c d) -> p c d", d=HEAD)).then_inc(w_in_loaded, 16)
                sp.wait_ge(S["gate_ready"], 1)
                sp.dma_start(keep["gate_row"], gate_row[:, :]).then_inc(S["gate_stored"], 16)
                sp.wait_ge(S["gate_stored"], 16)

            @block.scalar
            def _(act):
                act.wait_ge(S["c_loaded"], 16)
                nc.scalar.activation(ce[:, :], cc[:, :], ACT.Exp, scale=-1.0).then_inc(S["exp_done"], 1)

            @block.vector
            def _(dve):
                ch = Chain(dve, S["dve_step"])
                dve.wait_ge(S["exp_done"], 1)
                ch.link(nc.vector.tensor_scalar(ce[:, :], ce[:, :], 1.0, None, ALU.add))
                ch.link(nc.vector.reciprocal(ce[:, :], ce[:, :]))
                ch.link(nc.vector.tensor_tensor(ca[:, :], cc[:, :], ce[:, :], ALU.mult))
                nc.vector.tensor_copy(cb[:, :, :], spread(ca[:, :].unsqueeze(2), [P, KD, P])).then_inc(S["c_act_ready"], 1)
                dve.wait_ge(S["products_done"], 1)
                dve.wait_ge(S["small_loaded"], 64)
                nc.vector.tensor_tensor(sh[:, :], ps[:, 0:KD], b_ch[:, 0:KD], ALU.add)
                ch.link(nc.vector.tensor_tensor(ce[:, :], ps[:, KD:2 * KD], b_ch[:, KD:2 * KD], ALU.add))
                nc.vector.scalar_tensor_tensor(g1[:, :], ce[:, :], 1.0, npre[:, :], ALU.add, ALU.mult)
                ch.link(nc.vector.tensor_tensor(gate_row[:, :], pg[:, :], gate_row[:, :], ALU.add))
                nc.vector.tensor_tensor(gate_row[:, :], gate_row[:, :], np_row[:, :], ALU.mult).then_inc(S["gate_ready"], 1)

            @block.tensor
            def _(pe):
                pe.wait_ge(S["c_act_ready"], 1)
                for m in range(2 * KD):
                    if m % 4 == 0:
                        pe.wait_ge(S[f"w_loaded{m // 4}"], 16)
                    for k in range(KD):
                        nc.tensor.matmul(ps[:, m:m + 1], ada[:, k, m * P:(m + 1) * P], ca[:, k:k + 1],
                                         start=(k == 0), stop=(k == KD - 1))
                for half in range(2):
                    pe.wait_ge(S[f"w_loaded{4 + half}"], 16)
                    for k in range(KD):
                        last = nc.tensor.matmul(pg[:, half * 512:(half + 1) * 512], cb[:, k, :],
                                                ada[:, k, 2 * D + half * 512:2 * D + (half + 1) * 512],
                                                start=(k == 0), stop=(k == KD - 1))
                last.then_inc(S["products_done"], 1)
        S.close()


M_Q, M_K, M_V, M_SG, M_RKV, M_WA, M_GQ, M_GK, M_GB, M_GV, M_END = 0, 512, 640, 768, 1792, 2560, 3072, 3200, 3328, 3456, 3712


def mixer_projections(nc, A, w_in, w_in_loaded, stage1, keep, const):
    scale_ch, shift_ch = keep["scale_ch"], keep["shift_ch"]
    ident = const["ident"]
    with ExitStack() as ctx:
        sb = lambda n, s: ctx.enter_context(nc.sbuf_tensor("p1_" + n, s, F32))
        S = Signals(nc, "p1")
        B = [ctx.enter_context(nc.psum_tensor(f"p1_bank{i}", [P, 512], F32)) for i in range(8)]
        lora_cur, lora_prev = sb("lora_cur", [P, KD, P]), sb("lora_prev", [P, KD, P])
        gk1, gkb = sb("gk1", [P, KD, 16]), sb("gkb", [P, 1])
        mu_w, mu_a = sb("mu_w", [P, KD]), sb("mu_a", [P, KD])
        mu_rkv = sb("mu_rkv", [P, 6])
        wa2 = sb("wa2", [P, 2, R_W])
        lows = sb("lows", [P, 2 * R_W])
        gk2, wa0 = lows[0:16, 0:P], lows[32:33, :]
        ones, numbers = sb("ones", [P, P]), sb("numbers", [P, 3])
        xt, xn = sb("xt", [P, D]), sb("xn", [P, D])
        stat = sb("stat", [P, 2])
        hTs = sb("hT", [P, 2, KD, P + 1])
        loraT, gk1T = sb("loraT", [P, P]), sb("gk1T", [16, P])
        rkvT, mixT = sb("rkvT", [P, 6, P + 1]), sb("mixT", [P, 6, P])
        gz = sb("gz", [P, 2, P])
        st = sb("st", [P, 2, M_END])
        flat = lambda ap: ap.rearrange("p a b -> p (a b)")
        with nc.Block() as block:
            @block.sync
            def _(sp):
                load = lambda dst, src: sp.dma_start(dst, src).then_inc(S["weights_loaded"], 16)
                sp.dma_start(xt[:, :], A["x"][0][0:P, :]).then_inc(S["x_loaded"], 16)
                load(lora_cur[:, :, 0:64], A["rwkv_w1"][0].rearrange("(k p) n -> p k n", p=P))
                load(lora_cur[:, :, 64:128], A["rwkv_a1"][0].rearrange("(k p) n -> p k n", p=P))
                load(gk1[:, :, :], A["gla_gk1"][0].rearrange("(k p) n -> p k n", p=P))
                load(gk2[:, :], A["gla_gk2"][0])
                load(gkb[:, :], A["gla_gk_b_ch"])
                load(mu_w[:, :], A["rwkv_mu_w_ch"])
                load(mu_a[:, :], A["rwkv_mu_a_ch"])
                load(mu_rkv[:, :], A["rwkv_mu_rkv_ch"])
                load(wa2[0:64, 0, :], A["rwkv_w2"][0])
                load(wa2[64:128, 1, :], A["rwkv_a2"][0])
                load(wa0[:, 0:R_W], A["rwkv_w0"][0:1, :])
                load(wa0[:, R_W:], A["rwkv_a0"][0:1, :])
                for tile in tile_pairs(sp):
                    i, n = tile.t, tile.n
                    if tile.more:
                        sp.wait_ge(S["xn_ready"], n)
                        sp.dma_start(xt[:, :], A["x"][0][bass.ds(n * P, P), :]).then_inc(S["x_loaded"], 16)
                    sp.wait_ge(S["act_staged"], n)
                    sp.wait_ge(S["dve_staged"], n)
                    sp.dma_start(stage1[bass.ds(i * P, P), :], st[:, tile.b, :]).then_inc(S[f"stage_stored{tile.b}"], 16)
                for b in range(2):
                    sp.wait_ge(S[f"stage_stored{b}"], 16 * TILES // 2)

            N_WEIGHTS = 16 * 12

            @block.gpsimd
            def _(pool):
                ch = Chain(pool, S["pool_step"])
                for at, value in enumerate((-0.5, 1.0 / D, EPS)):
                    nc.gpsimd.memset(numbers[:, at:at + 1], value)
                nc.gpsimd.memset(ones[:, :], 1.0)
                nc.gpsimd.memset(hTs[:, 0, :, 0:1], 0.0)
                nc.gpsimd.memset(rkvT[:, :, P:P + 1], 0.0)
                ch.link(nc.gpsimd.memset(wa2[0:64, 1, :], 0.0))
                ch.link(nc.gpsimd.memset(wa2[64:128, 0, :], 0.0))
                pool.wait_ge(S["weights_loaded"], N_WEIGHTS)
                for mu_ch, hs in ((mu_w, slice(0, 64)), (mu_a, slice(64, 128))):
                    mu = spread(mu_ch[:, :].unsqueeze(2), [P, KD, 64])
                    ch.link(nc.gpsimd.tensor_tensor(lora_prev[:, :, hs], lora_cur[:, :, hs], mu, ALU.mult))
                    ch.link(nc.gpsimd.tensor_tensor(lora_cur[:, :, hs], lora_cur[:, :, hs], lora_prev[:, :, hs], ALU.subtract))
                nc.gpsimd.memset(stat[:, :], 1.0).then_inc(S["setup_done"], 1)
                ch.start_over()

                def x_norm(n):
                    pool.wait_ge(S["x_squares"], n)
                    ch.link(nc.gpsimd.tensor_tensor(stat[:, 0:1], stat[:, 0:1], numbers[:, 1:2], ALU.mult))
                    ch.link(nc.gpsimd.tensor_tensor(stat[:, 0:1], stat[:, 0:1], numbers[:, 2:3], ALU.add))
                    nc.gpsimd.tensor_tensor(stat[:, 1:2], stat[:, 0:1], numbers[:, 0:1], ALU.pow).then_inc(S["x_rstd"], 1)

                x_norm(1)
                ch.start_over()
                for tile in tile_pairs(pool):
                    if tile.more:
                        x_norm(tile.n + 1)
                    ch.start_over()

            @block.tensor
            def _(pe):
                mm, tr = nc.tensor.matmul, nc.tensor.transpose

                def turn_x(n):
                    pe.wait_ge(S["xn_ready"], n)
                    for k in range(KD):
                        last = tr(B[k // 4][:, (k % 4) * P:(k % 4 + 1) * P], xn[:, k * P:(k + 1) * P], ident[:, :])
                    last.then_inc(S["x_turned"], 1)

                pe.wait_ge(w_in_loaded, 16 * 3 * KD)
                pe.wait_ge(S["setup_done"], 1)
                turn_x(1)
                for tile in tile_pairs(pe):
                    i, n, hT = tile.t, tile.n, hTs[:, tile.b]

                    def channels(out, c):
                        for k in range(KD):
                            last = mm(out, w_in[:, k, c:c + P], hT[:, k, 1:P + 1], start=(k == 0), stop=(k == KD - 1))
                        return last

                    def tokens(out, c, width):
                        for k in range(KD):
                            last = mm(out, hT[:, k, 1:P + 1], w_in[:, k, c:c + width], start=(k == 0), stop=(k == KD - 1))
                        return last

                    pe.wait_ge(S["hT_act"], n)
                    pe.wait_ge(S["hT_dve"], n)
                    pe.wait_ge(S["gate_biased"], i)
                    for k in range(KD):
                        mm(B[3][:, 3 * P:4 * P], lora_cur[:, k, :], hT[:, k, 1:P + 1], start=(k == 0), stop=False)
                    for k in range(KD):
                        last = mm(B[3][:, 3 * P:4 * P], lora_prev[:, k, :], hT[:, k, 0:P], start=False, stop=(k == KD - 1))
                    for spot, c in enumerate((C_AK, C_GQ, C_GK)):
                        last = channels(B[3][:, spot * P:(spot + 1) * P], c)
                    last.then_inc(S["k_lora_proj"], 1)
                    pe.wait_ge(S["tok_taken"], i)
                    for c in range(4):
                        last = channels(B[4][:, c * P:(c + 1) * P], C_RKV + P * c)
                    last.then_inc(S["rk_proj"], 1)
                    for c in range(2):
                        channels(B[5][:, c * P:(c + 1) * P], C_RKV + P * (4 + c))
                    for k in range(KD):
                        last = mm(B[5][0:16, 2 * P:3 * P], gk1[:, k, :], hT[:, k, 1:P + 1], start=(k == 0), stop=(k == KD - 1))
                    last.then_inc(S["v_gk1_proj"], 1)
                    tokens(B[0][:, :], C_GV, 512).then_inc(S["gv_gg_proj"], 1)
                    pe.wait_ge(S["lora_ready"], n)
                    mm(B[1][:, :], loraT[:, :], flat(wa2[:, :, :]), start=True, stop=False)
                    mm(B[1][:, :], ones[32:33, :], wa0[:, :], start=False, stop=True).then_inc(S["wa_proj"], 1)
                    pe.wait_ge(S["q_taken"], i)
                    for c in range(4):
                        last = channels(B[2][:, c * P:(c + 1) * P], c * P)
                    last.then_inc(S["q_proj"], 1)
                    pe.wait_ge(S["raw_taken"], n)
                    pe.wait_ge(S["bank3_taken"], n)
                    mm(B[3][:, 0:P], gk2[:, :], gk1T[:, :], start=True, stop=True).then_inc(S["gate_proj"], 1)
                    pe.wait_ge(S["mix_ready"], n)
                    for c in range(6):
                        bank, spot = (4, c) if c < 4 else (5, c - 4)
                        last = tr(B[bank][:, spot * P:(spot + 1) * P], mixT[:, c, :], ident[:, :])
                    last.then_inc(S["rkv_turned"], 1)
                    if tile.more:
                        pe.wait_ge(S["gg_taken"], n)
                        pe.wait_ge(S["wa_taken"], n)
                        turn_x(n + 1)
                    pe.wait_ge(S["dve_staged"], i)
                    tokens(B[7][:, :], C_AG, 512).then_inc(S["ag_proj"], 1)
                    tokens(B[6][:, 0:P], C_AV, P)
                    tokens(B[6][:, P:P + 256], C_RG, 256).then_inc(S["av_rg_proj"], 1)

            @block.scalar
            def _(act):
                ch = Chain(act, S["act_step"])
                f = nc.scalar.activation

                def norm_x(n, t):
                    act.wait_ge(S["x_loaded"], n * 16)
                    act.wait_ge(S["x_turned"], t)
                    f(xn[:, :], xt[:, :], ACT.Square, accum_out=stat[:, 0:1]).then_inc(S["x_squares"], 1)
                    act.wait_ge(S["x_rstd"], n)
                    f(xn[:, :], xt[:, :], ACT.Copy, scale=stat[:, 1:2]).then_inc(S["xn_ready"], 1)

                def take_h(n, hT):
                    act.wait_ge(S["x_turned"], n)
                    for k in range(4):
                        last = f(hT[:, k, 1:P + 1], B[0][:, k * P:(k + 1) * P], ACT.Identity, bias=shift_ch[:, k:k + 1], scale=scale_ch[:, k:k + 1])
                    last.then_inc(S["hT_act"], 1)

                act.wait_ge(S["setup_done"], 1)
                norm_x(1, 0)
                take_h(1, hTs[:, 0])
                for tile in tile_pairs(act):
                    n = tile.n
                    out = lambda a, b: st[:, tile.b, a:b]
                    act.wait_ge(S[f"stage_stored{tile.b}"], tile.turn * 16)
                    act.wait_ge(S["k_lora_proj"], n)
                    f(loraT[0:64, :], B[3][0:64, 3 * P:4 * P], ACT.Tanh)
                    f(loraT[64:128, :], B[3][64:128, 3 * P:4 * P], ACT.Copy).then_inc(S["lora_ready"], 1)
                    f(out(M_GQ, M_GK), B[3][:, P:2 * P], ACT.Copy, scale=G_KEY ** -0.5)
                    f(out(M_GK, M_GB), B[3][:, 2 * P:3 * P], ACT.Copy)
                    f(out(M_K, M_V), B[3][:, 0:P], ACT.Copy).then_inc(S["bank3_taken"], 1)
                    act.wait_ge(S["gv_gg_proj"], n)
                    f(out(M_GV, M_END), B[0][:, 0:256], ACT.Copy)
                    f(out(M_SG + 768, M_SG + 1024), B[0][:, 256:512], ACT.Sigmoid).then_inc(S["gg_sigmoid"], 1)
                    act.wait_ge(S["wa_proj"], n)
                    f(out(M_WA, M_GQ), B[1][:, :], ACT.Sigmoid).then_inc(S["wa_taken"], 1)
                    if tile.more:
                        norm_x(n + 1, n)
                    act.wait_ge(S["q_proj"], n)
                    f(out(M_Q, M_K), B[2][:, :], ACT.Copy).then_inc(S["q_taken"], 1)
                    act.wait_ge(S["rkv_turned"], n)
                    f(out(M_RKV, M_RKV + 512), B[4][:, :], ACT.Copy)
                    f(out(M_RKV + 512, M_WA), B[5][:, 0:256], ACT.Copy).then_inc(S["tok_taken"], 1)
                    if tile.more:
                        take_h(n + 1, hTs[:, 1 - tile.b])
                    act.wait_ge(S["gate_abs"], n)
                    ch.link(f(gz[:, 1, :], gz[:, 1, :], ACT.Exp, scale=-1.0))
                    f(gz[:, 1, :], gz[:, 1, :], ACT.Ln, bias=1.0).then_inc(S["gate_ln"], 1)
                    act.wait_ge(S["ag_proj"], n)
                    f(out(M_SG, M_SG + 512), B[7][:, :], ACT.Sigmoid).then_inc(S["ag_sigmoid"], 1)
                    act.wait_ge(S["av_rg_proj"], n)
                    f(out(M_V, M_SG), B[6][:, 0:P], ACT.Copy)
                    f(out(M_SG + 512, M_SG + 768), B[6][:, P:P + 256], ACT.Sigmoid).then_inc(S["act_staged"], 1)
                    ch.start_over()

            @block.vector
            def _(dve):
                ch = Chain(dve, S["dve_step"])
                v = nc.vector
                tt, ts, stt = v.tensor_tensor, v.tensor_scalar, v.scalar_tensor_tensor

                def take_h(n, hT):
                    dve.wait_ge(S["x_turned"], n)
                    for k in range(4, 8):
                        last = ts(hT[:, k, 1:P + 1], B[1][:, (k - 4) * P:(k - 3) * P], scale_ch[:, k:k + 1], shift_ch[:, k:k + 1], ALU.mult, ALU.add)
                    return last

                dve.wait_ge(S["setup_done"], 1)
                take_h(1, hTs[:, 0]).then_inc(S["hT_dve"], 1)
                for tile in tile_pairs(dve):
                    n = tile.n
                    out = lambda a, b: st[:, tile.b, a:b]
                    ch.link(v.tensor_copy(rkvT[:, :, 0:1], rkvT[:, :, P:P + 1]))
                    dve.wait_ge(S["rk_proj"], n)
                    v.tensor_copy(rkvT[:, 0:4, 1:P + 1], B[4][:, :].rearrange("p (a b) -> p a b", b=P))
                    dve.wait_ge(S["v_gk1_proj"], n)
                    v.tensor_copy(gk1T[:, :], B[5][0:16, 2 * P:3 * P])
                    v.tensor_copy(rkvT[:, 4:6, 1:P + 1], B[5][:, 0:2 * P].rearrange("p (a b) -> p a b", b=P)).then_inc(S["raw_taken"], 1)
                    dve.wait_ge(S["raw_taken"], n)
                    ch.link(tt(mixT[:, :, :], rkvT[:, :, 0:P], rkvT[:, :, 1:P + 1], ALU.subtract))
                    for c in range(6):
                        last = stt(mixT[:, c, :], mixT[:, c, :], mu_rkv[:, c:c + 1], rkvT[:, c, 1:P + 1], ALU.mult, ALU.add)
                    last.then_inc(S["mix_ready"], 1)
                    dve.wait_ge(S["gg_sigmoid"], n)
                    tt(out(M_SG + 768, M_SG + 1024), B[0][:, 256:512], out(M_SG + 768, M_SG + 1024), ALU.mult).then_inc(S["gg_taken"], 1)
                    dve.wait_ge(S["gate_proj"], n)
                    ts(gz[:, 0, :], B[3][:, 0:P], gkb[:, 0:1], None, ALU.add).then_inc(S["gate_biased"], 1)
                    dve.wait_ge(S["gate_biased"], n)
                    stt(gz[:, 1, :], gz[:, 0, :], -1.0, gz[:, 0, :], ALU.mult, ALU.max).then_inc(S["gate_abs"], 1)
                    ch.link(ts(gz[:, 0, :], gz[:, 0, :], 0.0, None, ALU.min))
                    if tile.more:
                        take_h(n + 1, hTs[:, 1 - tile.b])
                        dve.wait_ge(S["hT_act"], n)
                        v.tensor_copy(hTs[:, 1 - tile.b, :, 0:1], hTs[:, tile.b, :, P:P + 1]).then_inc(S["hT_dve"], 1)
                    dve.wait_ge(S["gate_ln"], n)
                    ch.link(tt(gz[:, 0, :], gz[:, 0, :], gz[:, 1, :], ALU.subtract))
                    ch.link(ts(gz[:, 0, :], gz[:, 0, :], 1.0 / 16.0, None, ALU.mult))
                    v.tensor_tensor_scan(out(M_GB, M_GV), ones[:, :], gz[:, 0, :], 0.0, ALU.mult, ALU.add)
                    dve.wait_ge(S["ag_sigmoid"], n)
                    tt(out(M_SG, M_SG + 512), B[7][:, :], out(M_SG, M_SG + 512), ALU.mult)
                    dve.wait_ge(S["act_staged"], n)
                    tt(out(M_SG + 512, M_SG + 768), B[6][:, P:P + 256], out(M_SG + 512, M_SG + 768), ALU.mult).then_inc(S["dve_staged"], 1)
                    ch.start_over()
        S.close()


def mixers(nc, A, stage1, mixed, const):
    ident = const["ident"]
    with ExitStack() as ctx:
        sb = lambda n, s: ctx.enter_context(nc.sbuf_tensor("b1_" + n, s, F32))
        S = Signals(nc, "b1")
        banks8 = ctx.enter_context(nc.psum_tensor("b1_banks", [P, 8, 512], F32))
        B = [banks8[:, i, :] for i in range(8)]
        rows = sb("rows", [P, 6, R_W])
        KK_, KA_, OMKA, RK_, LNW, LNB = range(6)
        gnorm, sinks = sb("gnorm", [P, G_VAL]), sb("sinks", [P, A_HEADS])
        masks = sb("masks", [P, LEVELS, P])
        tri = sb("tri", [P, 2, P])
        pair = sb("pair", [P, P])
        quad = sb("quad", [P, R_W])
        chunk_of = sb("chunk_of", [P, 2])
        alibi = sb("alibi", [P, A_HEADS, 2 * P])
        numbers = sb("numbers", [P, 6, 4])
        NEG_HALF, PER_D, PER_HEAD, EPS_X, EPS_GLA, EPS_RWKV = range(6)
        tile_in = sb("tile_in", [P, 2, M_END])
        ys = sb("y", [P, 2, D])
        XY = sb("XY", [P, 2 * 4 * P])
        kT = sb("kT", [P, 2, P])
        vt = sb("vt", [P, 2, P])
        s = sb("s", [P, A_HEADS, 2 * P])
        G8 = sb("G8", [P, 16, P])
        pT = G8[:, :, :].rearrange("p (j e) t -> p j e t", e=4)
        am, nm, den = sb("am", [P, A_HEADS]), sb("nm", [P, A_HEADS]), sb("den", [P, A_HEADS])
        lw = sb("lw", [P, R_W])
        ex = sb("ex", [P, 3, R_W])
        pend = sb("pend", [P, 4])
        t1, t2, t3 = sb("t1", [P, R_W]), sb("t2", [P, R_W]), sb("t3", [P, R_W])
        h4 = sb("h4", [P, 4, 4])
        bonus = sb("bonus", [P, 4])
        X4 = sb("X4", [P, 4, R_W])
        X4T = sb("X4T", [P, 4, 2, P])
        GB = G8[:, 0:8, :].rearrange("p (h a) t -> p h a t", a=2)
        GK = G8[:, 8:16, :].rearrange("p (h a) t -> p h a t", a=2)
        cT = sb("cT", [P, 4, P])
        Zs = sb("Zs", [P, 4, P])
        X = XY[:, 0:512].rearrange("p (h t) -> p h t", t=P)
        Y = XY[:, 512:1024].rearrange("p (h t) -> p h t", t=P)
        akv, U = sb("akv", [P, R_W]), sb("U", [P, R_W])
        WT = sb("WT", [P, 2, P])
        SA, M = sb("SA", [P, R_W]), sb("M", [P, 2, P])
        yR = sb("yR", [P, R_W])
        ge = sb("ge", [P, LEVELS, P])
        gql, gkl = sb("gql", [P, LEVELS * P]), sb("gkl", [P, LEVELS * P])
        geb = sb("geb", [P, 3, P])
        gA, gS = sb("gA", [P, 4, P]), sb("gS", [P, R_W])
        ke_tok, g1, g4 = sb("ke_tok", [P, P]), sb("g1", [P, R_W]), sb("g4", [P, 4, 4])

        def s3(ap):
            return ap.rearrange("p (l t) -> p l t", t=P)

        class Staged:

            def __init__(self, b):
                part = lambda a, e: tile_in[:, b, a:e]
                self.qT = part(M_Q, M_K).rearrange("p (c t) -> p c t", t=P)
                self.k, self.v = part(M_K, M_V), part(M_V, M_SG)
                self.sg = part(M_SG, M_RKV)
                self.tok = part(M_RKV, M_WA).rearrange("p (e c) -> p e c", c=R_W)
                self.wa = part(M_WA, M_GQ).rearrange("p (e c) -> p e c", c=R_W)
                self.gqT, self.gkT, self.gb, self.gv = part(M_GQ, M_GK), part(M_GK, M_GB), part(M_GB, M_GV), part(M_GV, M_END)

        SAG, SRG, SGG = 0, 512, 768

        with nc.Block() as block:
            @block.sync
            def _(sp):
                load = lambda dst, src: sp.dma_start(dst, src).then_inc(S["weights_loaded"], 16)
                fetch = lambda t, b: sp.dma_start(tile_in[:, b, :], stage1[bass.ds(t * P, P), :]).then_inc(S[f"tile_loaded{b}"], 16)
                store = lambda t, b: sp.dma_start(mixed[bass.ds(t * P, P), :], ys[:, b, :]).then_inc(S[f"y_stored{b}"], 16)
                fetch(0, 0)
                for n, name in ((KK_, "rwkv_k_k"), (KA_, "rwkv_k_a"), (LNW, "rwkv_ln_w"), (LNB, "rwkv_ln_b")):
                    load(rows[:, n, :], row(A[name][0:1, :]))
                load(rows[:, RK_, :], row(A["rwkv_r_k"].rearrange("a h d -> a (h d)")))
                load(gnorm[:, :], row(A["gla_norm_w"][0:1, :]))
                load(sinks[:, :], row(A["attn_sinks"][0:1, :]))
                load(masks[:, :, :], A["k_masks"])
                load(tri[:, :, :], A["k_tri"])
                load(pair[:, :], A["k_pair"])
                load(quad[:, :], A["k_quad"])
                load(chunk_of[:, :], A["k_chunk_of"])
                load(alibi[:, :, P:], A["k_alibi"][:, :, P:])
                fetch(1, 1)
                sp.wait_ge(S["scores_done"], 1)
                sp.dma_start(alibi[:, :, 0:P], A["k_alibi"][:, :, 0:P]).then_inc(S["alibi_ready"], 16)
                with sp.Fori(0, TILES // 2 - 1) as i:
                    for b in range(2):
                        sp.wait_ge(S["y_ready"], 2 * i + (b + 1))
                        fetch(2 * i + (b + 2), b)
                        store(2 * i + b, b)
                for b in range(2):
                    sp.wait_ge(S["y_ready"], TILES - 1 + b)
                    store(TILES - 2 + b, b)
                for b in range(2):
                    sp.wait_ge(S[f"y_stored{b}"], 16 * TILES // 2)

            N_WEIGHTS = 16 * (4 + 3 + 6)

            @block.gpsimd
            def _(pool):
                ch = Chain(pool, S["pool_step"])
                for at, value in enumerate((-0.5, 1.0 / D, 1.0 / HEAD, EPS, 1e-5, RWKV_LN_EPS)):
                    nc.gpsimd.memset(numbers[:, at, :], value)
                nc.gpsimd.memset(alibi[:, :, 0:P], NEG)
                nc.gpsimd.memset(kT[:, :, :], 0.0)
                nc.gpsimd.memset(vt[:, :, :], 0.0)
                nc.gpsimd.memset(M[:, :, :], 0.0)
                nc.gpsimd.memset(gS[:, :], 0.0)
                ch.link(nc.gpsimd.memset(pend[:, :], 0.0))
                pool.wait_ge(S["weights_loaded"], N_WEIGHTS)
                nc.gpsimd.tensor_scalar(rows[:, OMKA, :], rows[:, KA_, :], -1.0, 1.0, ALU.mult, ALU.add).then_inc(S["setup_done"], 1)
                ch.start_over()

                def inv_sqrt(out, sums, n, per, eps):
                    ch.link(nc.gpsimd.tensor_tensor(sums, sums, numbers[:, per, 0:n], ALU.mult))
                    ch.link(nc.gpsimd.tensor_tensor(sums, sums, numbers[:, eps, 0:n], ALU.add))
                    return nc.gpsimd.tensor_tensor(out, sums, numbers[:, NEG_HALF, 0:n], ALU.pow)

                with pool.Fori(0, TILES) as i:
                    n = pool.snap(i + 1)
                    pool.wait_ge(S["kk_squares"], n)
                    nc.gpsimd.tensor_tensor(h4[:, 1, :], h4[:, 0, :], numbers[:, NEG_HALF, :], ALU.pow).then_inc(S["kk_rnorm"], 1)
                    pool.wait_ge(S["gla_squares"], n)
                    inv_sqrt(g4[:, 1, :], g4[:, 0, :], 4, PER_HEAD, EPS_GLA).then_inc(S["gla_rstd"], 1)
                    pool.wait_ge(S["rwkv_squares"], n)
                    inv_sqrt(h4[:, 3, :], h4[:, 2, :], 4, PER_HEAD, EPS_RWKV).then_inc(S["rwkv_rstd"], 1)
                    ch.start_over()

            @block.tensor
            def _(pe):
                pe.wait_ge(S["setup_done"], 1)
                mm, tr = nc.tensor.matmul, nc.tensor.transpose
                for tile in tile_pairs(pe):
                    i, n, y, T = tile.t, tile.n, ys[:, tile.b], Staged(tile.b)
                    pe.wait_ge(S["kept"], n)
                    pe.wait_ge(S["y_ready"], i)
                    for h in range(A_HEADS):
                        g = h // 4
                        last = mm(B[4 + h // 2][:, (h % 2) * 256:(h % 2) * 256 + 256], T.qT[64 * g:64 * g + 64, h % 4, :],
                                  kT[64 * g:64 * g + 64, :, :].rearrange("p a b -> p (a b)"), start=True, stop=True)
                        if h % 2:
                            last.then_inc(S[f"scores{h // 2}"], 1)
                    pe.wait_ge(S["lw_ready"], n)
                    mm(B[1][:, 0:R_W], tri[:, 1, :], lw[:, :], start=True, stop=True)
                    for p in range(2):
                        last = mm(B[1][:, R_W + 2 * p:R_W + 2 * p + 2], lw[:, p * P:(p + 1) * P], chunk_of[:, :], start=True, stop=True)
                    last.then_inc(S["cum_done"], 1)
                    for j in range(4):
                        pe.wait_ge(S[f"probs{j}"], n)
                        for e in range(4):
                            last = tr(B[4 + j][:, e * P:(e + 1) * P], s[:, 2 * j + e // 2, (e % 2) * P:(e % 2 + 1) * P], ident[:, :])
                        last.then_inc(S[f"probs_turned{j}"], 1)
                    pe.wait_ge(S["pT_dve"], n)
                    pe.wait_ge(S["pT_act"], n)
                    for h in range(A_HEADS):
                        for half in range(2):
                            last = mm(B[4][:, h * 64:(h + 1) * 64], pT[:, h // 2, (h % 2) * 2 + half, :],
                                      vt[:, half, 64 * (h // 4):64 * (h // 4) + 64], start=(half == 0), stop=(half == 1))
                    last.then_inc(S["attended"], 1)
                    pe.wait_ge(S["X4_ready"], n)
                    for c in range(8):
                        last = tr(B[2 + c // 4][:, (c % 4) * P:(c % 4 + 1) * P], X4[:, c // 2, (c % 2) * P:(c % 2 + 1) * P], ident[:, :])
                    last.then_inc(S["X4_turned"], 1)
                    pe.wait_ge(S["X4T_ready"], n)
                    for what, banks, name in ((2, (0, 1), "gram_b"), (3, (2, 3), "gram_k")):
                        for h in range(4):
                            r, p = slice(64 * (h % 2), 64 * (h % 2) + 64), h // 2
                            last = mm(B[banks[h % 2]][:, p * 256:p * 256 + 256], X4T[r, what, p, :],
                                      X4T[r, 0:2, p, :], start=True, stop=True)
                        last.then_inc(S[name], 1)
                    pe.wait_ge(S["gla_scaled"], n)
                    tr(B[5][:, P:2 * P], geb[:, 2, :], ident[:, :]).then_inc(S["ke_turned"], 1)
                    pe.wait_ge(S["attn_out"], n)
                    pe.wait_ge(S["ke_ready"], n)

                    def gla_round(half):
                        for l in range(4 * half, 4 * half + 4):
                            for h in range(4):
                                r = slice(32 * h, 32 * h + 32)
                                a, b = (T.gkT[r, :], T.gqT[r, :]) if l == 0 else (s3(gkl[r, 0:LEVELS * P])[:, l - 1, :], s3(gql[r, 0:LEVELS * P])[:, l - 1, :])
                                last = mm(B[4 + h][:, (l % 4) * P:(l % 4 + 1) * P], a, b, start=True, stop=True)
                        last.then_inc(S[f"gla_round{half}"], 1)

                    gla_round(0)
                    for l in range(INV_LEVELS):
                        if l == 4:
                            pe.wait_ge(S["gla_levels_used"], n)
                            gla_round(1)
                        pe.wait_ge(S[f"cT_ready{l}"], n)
                        for h in range(4):
                            last = mm(B[0][:, h * P:(h + 1) * P], cT[:, h, :], ident[:, :] if l == 0 else X[:, h, :], start=True, stop=True)
                        last.then_inc(S[f"Z_done{l}"], 1)
                        if l > 0:
                            pe.wait_ge(S[f"Z_taken{l}"], n)
                            for h in range(4):
                                last = mm(B[2][:, h * P:(h + 1) * P], Zs[:, h, :], Y[:, h, :], start=True, stop=True)
                            last.then_inc(S[f"YZ_done{l}"], 1)
                            if l < INV_LEVELS - 1:
                                for h in range(4):
                                    last = mm(B[1][:, h * P:(h + 1) * P], Y[:, h, :], Zs[:, h, :], start=True, stop=True)
                                last.then_inc(S[f"XZ_done{l}"], 1)
                    for h in range(4):
                        last = mm(B[3][:, h * 64:(h + 1) * 64], GK[:, h, 0, :], T.tok[:, 2, h * 64:(h + 1) * 64], start=True, stop=True)
                    last.then_inc(S["akv_done"], 1)
                    pe.wait_ge(S["Y_ready"], n)
                    for h in range(4):
                        last = mm(B[1][64 * (h % 2):64 * (h % 2) + 64, (h // 2) * P:(h // 2 + 1) * P], X4[:, 0, h * 64:(h + 1) * 64], Y[:, h, :], start=True, stop=True)
                    last.then_inc(S["WT_done"], 1)
                    pe.wait_ge(S["akv_ready"], n)
                    for h in range(4):
                        last = mm(B[0][:, h * 64:(h + 1) * 64], Y[:, h, :], akv[:, h * 64:(h + 1) * 64], start=True, stop=True)
                    last.then_inc(S["U_done"], 1)
                    pe.wait_ge(S["gA_ready"], n)
                    for h in range(4):
                        c = slice(h * 64, (h + 1) * 64)
                        mm(B[4][:, c], geb[:, 1, :], gS[:, c], start=True, stop=False)
                        mm(B[4][:, c], gA[:, h, :], T.gv[:, c], start=False, stop=True)
                    last = mm(B[5][:, 256:512], ke_tok[:, :], T.gv[:, :], start=True, stop=True)
                    last.then_inc(S["gla_out"], 1)
                    pe.wait_ge(S["WT_ready"], n)
                    for c in range(2):
                        r = slice(64 * c, 64 * c + 64)
                        if c == 1:
                            pe.wait_ge(S["M_ready0"], n)
                        for p in range(2):
                            mm(B[2][r, p * P:(p + 1) * P], WT[:, p, r], M[:, p, :], start=True, stop=True)
                        for p in range(2):
                            last = mm(B[1][r, 256 + p * P:256 + (p + 1) * P], X4T[:, 1, p, r], M[:, p, :], start=True, stop=True)
                        last.then_inc(S[f"sa_done{c}"], 1)
                        pe.wait_ge(S[f"sa_ready{c}"], n)
                        for p in range(2):
                            mm(B[3][:, 256 + p * P:256 + (p + 1) * P], X4[r, 2, p * P:(p + 1) * P], SA[r, p * P:(p + 1) * P], start=True, stop=False)
                            last = mm(B[3][:, 256 + p * P:256 + (p + 1) * P], X4[r, 3, p * P:(p + 1) * P], T.tok[r, 2, p * P:(p + 1) * P], start=False, stop=True)
                        last.then_inc(S[f"dM_done{c}"], 1)
                    for h in range(4):
                        c = slice(h * 64, (h + 1) * 64)
                        mm(B[0][:, 256 + h * 64:256 + (h + 1) * 64], GB[:, h, 1, :], SA[:, c], start=True, stop=False)
                        last = mm(B[0][:, 256 + h * 64:256 + (h + 1) * 64], GK[:, h, 1, :], T.tok[:, 2, c], start=False, stop=True)
                    last.then_inc(S["rwkv_out"], 1)

            @block.scalar
            def _(act):
                f = nc.scalar.activation
                for tile in tile_pairs(act):
                    i, n, y, T = tile.t, tile.n, ys[:, tile.b], Staged(tile.b)
                    act.wait_ge(S["cum_less"], n)
                    f(ex[:, 1, :], B[1][:, 0:R_W], ACT.Exp)
                    f(ex[:, 2, :], B[1][:, 0:R_W], ACT.Exp, scale=-1.0)
                    f(pend[:, :], B[1][:, R_W:R_W + 4], ACT.Exp)
                    f(ex[:, 0, :], ex[:, 0, :], ACT.Exp).then_inc(S["ex_ready"], 1)
                    act.wait_ge(S["max_ready"], n)
                    for h in range(A_HEADS):
                        last = f(s[:, h, :], s[:, h, :], ACT.Exp, bias=nm[:, h:h + 1], accum_out=den[:, h:h + 1])
                        if h % 2:
                            last.then_inc(S[f"probs{h // 2}"], 1)
                    f(am[:, :], am[:, :], ACT.Exp).then_inc(S["sink_exp"], 1)
                    for j in (0, 2):
                        act.wait_ge(S[f"probs_turned{j}"], n)
                        last = f(pT[:, j, :, :].rearrange("p a b -> p (a b)"), B[4 + j][:, :], ACT.Copy)
                    last.then_inc(S["pT_act"], 1)
                    act.wait_ge(S["levels_ready"], n)
                    f(ge[:, :, :], ge[:, :, :], ACT.Exp)
                    f(geb[:, 1, :], T.gb[:, :], ACT.Exp)
                    f(geb[:, 2, :], T.gb[:, :], ACT.Exp, scale=-1.0, bias=T.gb[:, P - 1:P]).then_inc(S["levels_exp"], 1)
                    act.wait_ge(S["X4_turned"], n)
                    f(X4T[:, 0:2, :, :].rearrange("p a b c -> p (a b c)"), B[2][:, :], ACT.Copy)
                    f(X4T[:, 2:4, :, :].rearrange("p a b c -> p (a b c)"), B[3][:, :], ACT.Copy).then_inc(S["X4T_ready"], 1)
                    act.wait_ge(S["ke_turned"], n)
                    f(ke_tok[:, :], B[5][:, P:2 * P], ACT.Copy).then_inc(S["ke_ready"], 1)
                    for l in range(1, INV_LEVELS):
                        act.wait_ge(S[f"Z_done{l}"], n)
                        f(Zs[:, :, :].rearrange("p a b -> p (a b)"), B[0][:, :], ACT.Copy).then_inc(S[f"Z_taken{l}"], 1)
                    act.wait_ge(S["akv_done"], n)
                    f(akv[:, :], B[3][:, 0:R_W], ACT.Copy).then_inc(S["akv_ready"], 1)
                    act.wait_ge(S["WT_done"], n)
                    f(WT[:, :, :].rearrange("p a b -> p (a b)"), B[1][:, 0:R_W], ACT.Copy)
                    act.wait_ge(S["U_done"], n)
                    f(U[:, :], B[0][:, 0:R_W], ACT.Copy).then_inc(S["WT_ready"], 1)
                    for c in range(2):
                        act.wait_ge(S[f"sa_done{c}"], n)
                        last = f(yR[64 * c:64 * c + 64, :], B[1][64 * c:64 * c + 64, 256:512], ACT.Copy)
                    last.then_inc(S["yR_ready"], 1)

            @block.vector
            def _(dve):
                ch = Chain(dve, S["dve_step"])
                v = nc.vector
                tt, ts, stt = v.tensor_tensor, v.tensor_scalar, v.scalar_tensor_tensor
                dve.wait_ge(S["setup_done"], 1)
                ch.link(v.memset(am[:, :], 0.0))
                dve.sem_clear(S["dve_step"])
                ch.count = 0

                def heads(ap, d=HEAD):
                    return ap.rearrange("p (h d) -> p h d", d=d)

                for tile in tile_pairs(dve):
                    i, n, y, T = tile.t, tile.n, ys[:, tile.b], Staged(tile.b)
                    dve.wait_ge(S[f"tile_loaded{tile.b}"], tile.turn * 16 + 16)
                    ts(lw[:, :], T.wa[:, 0, :], -float(np.exp(-0.5)), None, ALU.mult).then_inc(S["lw_ready"], 1)
                    ch.link(v.tensor_copy(kT[:, 0, :], kT[:, 1, :]))
                    ch.link(v.tensor_copy(vt[:, 0, :], vt[:, 1, :]))
                    v.tensor_copy(kT[:, 1, :], T.k)
                    v.tensor_copy(vt[:, 1, :], T.v).then_inc(S["kept"], 1)
                    for j in range(4):
                        dve.wait_ge(S[f"scores{j}"], n)
                        last = stt(s[:, 2 * j:2 * j + 2, :].rearrange("p a b -> p (a b)"), B[4 + j][:, :], HEAD ** -0.5,
                                   alibi[:, 2 * j:2 * j + 2, :].rearrange("p a b -> p (a b)"), ALU.mult, ALU.add)
                    last.then_inc(S["scores_done"], 1)
                    dve.wait_ge(S["scores_done"], n)
                    dve.wait_ge(S["alibi_ready"], 16)
                    ch.link(v.tensor_reduce(am[:, :], s[:, :, :], AX.X, ALU.max))
                    ch.link(tt(am[:, :], am[:, :], sinks[:, :], ALU.max))
                    ch.link(ts(nm[:, :], am[:, :], -1.0, None, ALU.mult))
                    tt(am[:, :], sinks[:, :], nm[:, :], ALU.add).then_inc(S["max_ready"], 1)
                    dve.wait_ge(S["cum_done"], n)
                    tt(ex[:, 0, :], B[1][:, 0:R_W], lw[:, :], ALU.subtract).then_inc(S["cum_less"], 1)
                    ch.link(tt(t1[:, :], T.tok[:, 1, :], rows[:, KK_, :], ALU.mult))
                    ch.link(tt(t2[:, :], t1[:, :], t1[:, :], ALU.mult))
                    ch.link(v.tensor_reduce(h4[:, 0, :], heads(t2[:, :]), AX.X, ALU.add))
                    ts(h4[:, 0, :], h4[:, 0, :], 1e-24, None, ALU.max).then_inc(S["kk_squares"], 1)
                    ch.link(tt(t3[:, :], T.wa[:, 1, :], rows[:, KA_, :], ALU.mult))
                    ch.link(tt(t3[:, :], t3[:, :], rows[:, OMKA, :], ALU.add))
                    ch.link(tt(t3[:, :], t3[:, :], T.tok[:, 1, :], ALU.mult))
                    ch.link(tt(t2[:, :], T.tok[:, 0, :], t3[:, :], ALU.mult))
                    ch.link(tt(t2[:, :], t2[:, :], rows[:, RK_, :], ALU.mult))
                    ch.link(v.tensor_reduce(bonus[:, :], heads(t2[:, :]), AX.X, ALU.add))
                    dve.wait_ge(S["kk_rnorm"], n)
                    ch.link(tt(heads(t1[:, :]), heads(t1[:, :]), spread(h4[:, 1, :].unsqueeze(2), [P, 4, HEAD]), ALU.mult))
                    ch.link(tt(t2[:, :], t1[:, :], T.wa[:, 1, :], ALU.mult))
                    dve.wait_ge(S["ex_ready"], n)
                    tt(X4[:, 0, :], t1[:, :], ex[:, 0, :], ALU.mult)
                    tt(X4[:, 1, :], T.tok[:, 0, :], ex[:, 1, :], ALU.mult)
                    tt(X4[:, 2, :], t2[:, :], ex[:, 2, :], ALU.mult)
                    tt(X4[:, 3, :], t3[:, :], ex[:, 2, :], ALU.mult).then_inc(S["X4_ready"], 1)
                    for j in (1, 3):
                        dve.wait_ge(S[f"probs_turned{j}"], n)
                        last = v.tensor_copy(pT[:, j, :, :].rearrange("p a b -> p (a b)"), B[4 + j][:, :])
                    last.then_inc(S["pT_dve"], 1)
                    dve.wait_ge(S["sink_exp"], n)
                    ch.link(tt(den[:, :], den[:, :], am[:, :], ALU.add))
                    ch.link(v.reciprocal(den[:, :], den[:, :]))
                    dve.wait_ge(S["attended"], n)
                    dve.wait_ge(S[f"y_stored{tile.b}"], tile.turn * 16)
                    tt(heads(y[:, 0:512]), heads(B[4][:, :]), spread(den[:, :].unsqueeze(2), [P, A_HEADS, HEAD]), ALU.mult).then_inc(S["attn_out"], 1)
                    dve.wait_ge(S["attn_out"], n)
                    ch.link(tt(y[:, 0:512], y[:, 0:512], T.sg[:, 0:512], ALU.mult))
                    for l in range(LEVELS):
                        half = 1 << l
                        blocks = lambda ap: ap.rearrange("p (m w) -> p m w", w=2 * half)
                        mid = spread(blocks(T.gb[:, :])[:, :, half - 1:half], [P, P // (2 * half), 2 * half])
                        last = tt(blocks(ge[:, l, :]), blocks(T.gb[:, :]), mid, ALU.subtract)
                    ch.link(last)
                    stt(ge[:, :, :], ge[:, :, :], -1.0, ge[:, :, :], ALU.mult, ALU.min).then_inc(S["levels_ready"], 1)
                    dve.wait_ge(S["levels_exp"], n)
                    tt(s3(gql[:, 0:LEVELS * P]), ge[:, :, :], spread(T.gqT[:, :].unsqueeze(1), [P, LEVELS, P]), ALU.mult)
                    tt(s3(gkl[:, 0:LEVELS * P]), ge[:, :, :], spread(T.gkT[:, :].unsqueeze(1), [P, LEVELS, P]), ALU.mult)
                    v.tensor_copy(g4[:, 3, 0:1], geb[:, 1, P - 1:P])
                    ch.link(tt(geb[:, 2, :], geb[:, 2, :], T.gkT[:, :], ALU.mult))
                    tt(geb[:, 1, :], geb[:, 1, :], T.gqT[:, :], ALU.mult).then_inc(S["gla_scaled"], 1)
                    for name, banks, dst in (("gram_b", (0, 1), GB), ("gram_k", (2, 3), GK)):
                        dve.wait_ge(S[name], n)
                        for j in range(2):
                            last = tt(dst.rearrange("p (q j) a b -> p j q (a b)", j=2)[:, j],
                                      B[banks[j]][:, :].rearrange("p (h a) -> p h a", h=2),
                                      spread(tri[:, :, :].rearrange("p a b -> p (a b)").unsqueeze(1), [P, 2, 2 * P]), ALU.mult)
                        ch.link(last)

                    def level(l):
                        src = banks8[:, 4:8, (l % 4) * P:(l % 4 + 1) * P]
                        if l == 0:
                            last = tt(gA[:, :, :], src, spread(ident[:, :].unsqueeze(1), [P, 4, P]), ALU.mult)
                        else:
                            last = v.copy_predicated(gA[:, :, :], spread(masks[:, l - 1, :].bitcast(U32).unsqueeze(1), [P, 4, P]), src)
                        if l == 3:
                            last.then_inc(S["gla_levels_used"], 1)
                            dve.wait_ge(S["gla_levels_used"], n)
                        else:
                            ch.link(last)

                    for l in range(INV_LEVELS):
                        if l > 0:
                            dve.wait_ge(S[f"Z_done{l - 1}"], n)
                        if l % 4 == 0:
                            dve.wait_ge(S[f"gla_round{l // 4}"], n)
                        tt(cT[:, :, :], GB[:, :, 0, :], spread(masks[:, l, :].unsqueeze(1), [P, 4, P]), ALU.mult).then_inc(S[f"cT_ready{l}"], 1)
                        level(l)
                        if l == 0:
                            dve.wait_ge(S["cT_ready0"], n)
                            idn = spread(ident[:, :].unsqueeze(1), [P, 4, P])
                            ch.link(tt(Y[:, :, :], idn, cT[:, :, :], ALU.subtract))
                            dve.wait_ge(S["Z_done0"], n)
                            ch.link(tt(X[:, :, :], idn, B[0][:, :].rearrange("p (h t) -> p h t", t=P), ALU.subtract))
                        elif l < INV_LEVELS - 1:
                            dve.wait_ge(S[f"XZ_done{l}"], n)
                            flat = lambda a: a[:, :, :].rearrange("p a b -> p (a b)")
                            tt(flat(Y), flat(Y), B[2][:, :], ALU.subtract)
                            ch.link(tt(flat(X), flat(X), B[1][:, :], ALU.subtract))
                        else:
                            dve.wait_ge(S[f"YZ_done{l}"], n)
                            tt(flat(Y), flat(Y), B[2][:, :], ALU.subtract).then_inc(S["Y_ready"], 1)
                    level(6)
                    level(7)
                    v.tensor_copy(g1[:, 1:2], g4[:, 3, 0:1]).then_inc(S["gA_ready"], 1)
                    dve.wait_ge(S["gla_out"], n)
                    ch.link(tt(g1[:, :], B[5][:, 256:512], quad[:, :], ALU.mult))
                    ch.link(stt(gS[:, :], gS[:, :], g4[:, 3, 0:1], g1[:, :], ALU.mult, ALU.add))
                    ch.link(v.tensor_copy(y[:, 768:1024], B[4][:, 0:R_W]))
                    ch.link(tt(g1[:, :], y[:, 768:1024], y[:, 768:1024], ALU.mult))
                    v.tensor_reduce(g4[:, 0, :], heads(g1[:, :]), AX.X, ALU.add).then_inc(S["gla_squares"], 1)
                    dve.wait_ge(S["gla_rstd"], n)
                    yg = heads(y[:, 768:1024])
                    ch.link(tt(yg, yg, spread(g4[:, 1, :].unsqueeze(2), [P, 4, HEAD]), ALU.mult))
                    ch.link(tt(yg, yg, spread(gnorm[:, :].unsqueeze(1), [P, 4, HEAD]), ALU.mult))
                    ch.link(tt(y[:, 768:1024], y[:, 768:1024], T.sg[:, SGG:SGG + 256], ALU.mult))
                    dve.wait_ge(S["WT_ready"], n)
                    for c in range(2):
                        r = slice(64 * c, 64 * c + 64)
                        dve.wait_ge(S[f"sa_done{c}"], n)
                        stt(SA[r, :], B[2][r, 0:R_W], -1.0, U[r, :], ALU.mult, ALU.subtract).then_inc(S[f"sa_ready{c}"], 1)
                        dve.wait_ge(S[f"dM_done{c}"], n)
                        dM = t1[:, :].rearrange("p (a b) -> p a b", b=P)
                        ch.link(tt(dM, B[3][:, 256:512].rearrange("p (a b) -> p a b", b=P), spread(pair[:, :].unsqueeze(1), [P, 2, P]), ALU.mult))
                        ch.link(tt(M[:, :, :], M[:, :, :], dM, ALU.add))
                        ts(M[:, 0, :], M[:, 0, :], pend[:, c:c + 1], None, ALU.mult)
                        ts(M[:, 1, :], M[:, 1, :], pend[:, 2 + c:3 + c], None, ALU.mult).then_inc(S[f"M_ready{c}"], 1)
                    dve.wait_ge(S["yR_ready"], n)
                    dve.wait_ge(S["rwkv_out"], n)
                    yr = heads(t1[:, :])
                    dve.wait_ge(S["M_ready1"], n)
                    ch.link(tt(t1[:, :], B[0][:, 256:512], yR[:, :], ALU.add))
                    ch.link(v.tensor_reduce(h4[:, 0, :], yr, AX.X, ALU.add))
                    ch.link(ts(h4[:, 0, :], h4[:, 0, :], 1.0 / HEAD, None, ALU.mult))
                    ch.link(tt(yr, yr, spread(h4[:, 0, :].unsqueeze(2), [P, 4, HEAD]), ALU.subtract))
                    ch.link(tt(t2[:, :], t1[:, :], t1[:, :], ALU.mult))
                    v.tensor_reduce(h4[:, 2, :], heads(t2[:, :]), AX.X, ALU.add).then_inc(S["rwkv_squares"], 1)
                    ch.link(tt(heads(t3[:, :]), heads(T.tok[:, 2, :]), spread(bonus[:, :].unsqueeze(2), [P, 4, HEAD]), ALU.mult))
                    dve.wait_ge(S["rwkv_rstd"], n)
                    ch.link(tt(yr, yr, spread(h4[:, 3, :].unsqueeze(2), [P, 4, HEAD]), ALU.mult))
                    ch.link(tt(t1[:, :], t1[:, :], rows[:, LNW, :], ALU.mult))
                    ch.link(tt(t1[:, :], t1[:, :], rows[:, LNB, :], ALU.add))
                    ch.link(tt(t1[:, :], t1[:, :], t3[:, :], ALU.add))
                    tt(y[:, 512:768], t1[:, :], T.sg[:, SRG:SRG + 256], ALU.mult).then_inc(S["y_ready"], 1)
                    ch.start_over()
        S.close()


def output_and_residual(nc, A, mixed, x1, w_in_2, w_in_2_loaded, keep, const):
    ident = const["ident"]
    with ExitStack() as ctx:
        sb = lambda n, s: ctx.enter_context(nc.sbuf_tensor("o1_" + n, s, F32))
        S = Signals(nc, "o1")
        B = [ctx.enter_context(nc.psum_tensor(f"o1_bank{i}", [P, 512], F32)) for i in range(8)]
        w, gate_row = sb("w", [P, KD, D]), sb("gate_row", [P, D])
        y, x, r = sb("y", [P, 2, D]), sb("x", [P, 2, D]), sb("r", [P, 2, D])
        yT = w_in_2[:, KD - 1, 0:2 * D].rearrange("p (b k t) -> p b k t", b=2, t=P)
        sq = w_in_2[:, KD - 1, 2 * D:2 * D + 512]
        st, neg_half = sb("st", [P, 2, 4]), sb("neg_half", [P, 1])
        PAIRS = TILES // 2
        assert PAIRS == KD

        with nc.Block() as block:
            @block.sync
            def _(sp):
                src = A["w_out"][0].rearrange("(k p) n -> p k n", p=P)
                for k in range(KD):
                    sp.dma_start(w[:, k, :], src[:, k, :]).then_inc(S["w_loaded"], 16)
                sp.dma_start(gate_row[:, :], keep["gate_row"]).then_inc(S["gate_loaded"], 16)
                src = A["w_in_2"][0].rearrange("(k p) n -> p k n", p=P)

                def fetch(i):
                    for b in range(2):
                        sp.wait_ge(S[f"y_turned{b}"], i)
                        sp.dma_start(y[:, b, :], mixed[bass.ds((2 * i + b) * P, P), :]).then_inc(S[f"y_loaded{b}"], 16)
                        sp.wait_ge(S[f"x_used{b}"], i)
                        sp.dma_start(x[:, b, :], A["x"][0][bass.ds((2 * i + b) * P, P), :]).then_inc(S[f"x_loaded{b}"], 16)

                with sp.Fori(0, PAIRS - 1) as i:
                    fetch(i)
                    sp.dma_start(w_in_2[:, bass.ds(i, 1), :], src[:, bass.ds(i, 1), :]).then_inc(w_in_2_loaded, 16)
                fetch(PAIRS - 1)

            @block.gpsimd
            def _(pool):
                ch = Chain(pool, S["pool_step"])
                ch.link(nc.gpsimd.memset(neg_half[:, :], -0.5))
                ch.start_over()
                with pool.Fori(0, PAIRS) as i:
                    n = pool.snap(i + 1)
                    for b in range(2):
                        pool.wait_ge(S[f"squares{b}"], n)
                        ch.link(nc.gpsimd.tensor_tensor(st[:, b, 0:1], st[:, b, 0:1], st[:, b, 1:2], ALU.add))
                        ch.link(nc.gpsimd.tensor_scalar(st[:, b, 0:1], st[:, b, 0:1], 1.0 / D, EPS, ALU.mult, ALU.add))
                        nc.gpsimd.tensor_tensor(st[:, b, 2:3], st[:, b, 0:1], neg_half[:, :], ALU.pow).then_inc(S[f"rstd{b}"], 1)
                    ch.start_over()

            @block.tensor
            def _(pe):
                pe.wait_ge(S["w_loaded"], 16 * KD)
                with pe.Fori(0, PAIRS) as i:
                    n = pe.snap(i + 1)
                    for b in range(2):
                        pe.wait_ge(S[f"y_loaded{b}"], n * 16)
                        pe.wait_ge(S[f"yT_act{b}"], i)
                        pe.wait_ge(S[f"yT_dve{b}"], i)
                        for k in range(KD):
                            last = nc.tensor.transpose(B[2 * b + k // 4][:, (k % 4) * P:(k % 4 + 1) * P], y[:, b, k * P:(k + 1) * P], ident[:, :])
                        last.then_inc(S[f"y_turned{b}"], 1)
                    for b in range(2):
                        pe.wait_ge(S[f"yT_act{b}"], n)
                        pe.wait_ge(S[f"yT_dve{b}"], n)
                        pe.wait_ge(S[f"scaled{b}"], i)
                        for half in range(2):
                            for k in range(KD):
                                last = nc.tensor.matmul(B[4 + 2 * b + half][:, :], yT[:, b, k, :], w[:, k, half * 512:(half + 1) * 512], start=(k == 0), stop=(k == KD - 1))
                        last.then_inc(S[f"projected{b}"], 1)

            @block.scalar
            def _(act):
                flat = lambda b, a: yT[:, b, a:a + 4, :].rearrange("p a b -> p (a b)")
                with act.Fori(0, PAIRS) as i:
                    n = act.snap(i + 1)
                    for b in range(2):
                        act.wait_ge(S[f"y_turned{b}"], n)
                        act.wait_ge(S[f"projected{b}"], i)
                        nc.scalar.activation(flat(b, 0), B[2 * b][:, :], ACT.Copy).then_inc(S[f"yT_act{b}"], 1)
                    for b in range(2):
                        act.wait_ge(S[f"projected{b}"], n)
                        act.wait_ge(S[f"rstd{b}"], i)
                        nc.scalar.activation(sq[:, :], B[4 + 2 * b][:, :], ACT.Square, accum_out=st[:, b, 0:1]).then_inc(S["act_step"], 1)
                        act.wait_ge(S["act_step"], 1)
                        act.sem_clear(S["act_step"])
                        nc.scalar.activation(sq[:, :], B[5 + 2 * b][:, :], ACT.Square, accum_out=st[:, b, 1:2]).then_inc(S[f"squares{b}"], 1)
                        act.wait_ge(S[f"squares{b}"], n)
                        act.wait_ge(S[f"x_used{b}"], n)
                        act.dma_start(x1[bass.ds((2 * i + b) * P, P), :], r[:, b, :]).then_inc(S[f"x1_stored{b}"], 16)
                for b in range(2):
                    act.wait_ge(S[f"x1_stored{b}"], 16 * PAIRS)

            @block.vector
            def _(dve):
                flat = lambda b, a: yT[:, b, a:a + 4, :].rearrange("p a b -> p (a b)")
                dve.wait_ge(S["gate_loaded"], 16)
                with dve.Fori(0, PAIRS) as i:
                    n = dve.snap(i + 1)
                    for b in range(2):
                        dve.wait_ge(S[f"y_turned{b}"], n)
                        dve.wait_ge(S[f"projected{b}"], i)
                        nc.vector.tensor_copy(flat(b, 4), B[2 * b + 1][:, :]).then_inc(S[f"yT_dve{b}"], 1)
                    for b in range(2):
                        dve.wait_ge(S[f"rstd{b}"], n)
                        dve.wait_ge(S[f"x1_stored{b}"], i * 16)
                        for half in range(2):
                            c = slice(half * 512, (half + 1) * 512)
                            last = nc.vector.scalar_tensor_tensor(r[:, b, c], B[4 + 2 * b + half][:, :], st[:, b, 2:3], gate_row[:, c], ALU.mult, ALU.mult)
                        last.then_inc(S[f"scaled{b}"], 1)
                        dve.wait_ge(S[f"scaled{b}"], n)
                        dve.wait_ge(S[f"x_loaded{b}"], n * 16)
                        nc.vector.tensor_tensor(r[:, b, :], r[:, b, :], x[:, b, :], ALU.add).then_inc(S[f"x_used{b}"], 1)
        S.close()
A2_HEADS, A2_KV = 8, 2
IDX_HEADS, IDX_DIM = 8, 32
ROT, IDX_ROT = 8, 4
TOPK = 256
POOL_GROUPS = 4
HIST = 16
C2_Q, C2_K, C2_V, C2_QI, C2_KI, C2_ZA, C2_U, C2_ZB, C2_GATES = 0, 512, 640, 768, 1024, 1064, 1576, 2088, 2600
IN2 = 4648
T_QT, T_QI, T_W, T_ZA, T_BT, T_G, T_KT, T_KI, T_V, T_END = 0, 512, 768, 784, 1296, 1808, 3856, 3984, 4112, 4240


def rotary_tables(nc, A, tables):
    NF = ROT + IDX_ROT
    N = TILES * NF
    TWO_PI = 2 * np.pi
    part1 = float(np.float32(6.28125))
    part2 = float(np.float32(int((TWO_PI - part1) * 2 ** 21) / 2 ** 21))
    part3 = float(np.float32(TWO_PI - part1 - part2))
    MAGIC = float(1.5 * 2 ** 23)
    with ExitStack() as ctx:
        sb = lambda n, s, d=F32: ctx.enter_context(nc.sbuf_tensor("ro_" + n, s, d))
        S = Signals(nc, "ro")
        pos_i, pos, freq = sb("pos_i", [P, TILES], I32), sb("pos", [P, TILES]), sb("freq", [P, NF])
        ang, turns, red = sb("ang", [P, TILES, NF]), sb("turns", [P, TILES, NF]), sb("red", [P, 2, TILES, NF])
        with nc.Block() as block:
            @block.sync
            def _(sp):
                sp.dma_start(pos_i[:, :], A["positions_2_ch"]).then_inc(S["loaded"], 16)
                sp.dma_start(freq[:, :], row(A["k_freq"])).then_inc(S["loaded"], 16)

            @block.vector
            def _(dve):
                ch = Chain(dve, S["dve_step"])
                v = nc.vector
                dve.wait_ge(S["loaded"], 32)
                ch.link(v.tensor_copy(pos[:, :], pos_i[:, :]))
                ch.link(v.tensor_tensor(ang[:, :, :], spread(pos[:, :].unsqueeze(2), [P, TILES, NF]),
                                        spread(freq[:, :].unsqueeze(1), [P, TILES, NF]), ALU.mult))
                for which, quarter in ((0, 0.25), (1, 0.0)):
                    r = red[:, which, :, :]
                    ch.link(v.tensor_scalar(turns[:, :, :], ang[:, :, :], 1.0 / TWO_PI, quarter, ALU.mult, ALU.add))
                    ch.link(v.tensor_scalar(turns[:, :, :], turns[:, :, :], MAGIC, None, ALU.add))
                    ch.link(v.tensor_scalar(turns[:, :, :], turns[:, :, :], MAGIC, None, ALU.subtract))
                    ch.link(v.scalar_tensor_tensor(r, turns[:, :, :], -part1, ang[:, :, :], ALU.mult, ALU.add))
                    ch.link(v.scalar_tensor_tensor(r, turns[:, :, :], -part2, r, ALU.mult, ALU.add))
                    ch.link(v.scalar_tensor_tensor(r, turns[:, :, :], -part3, r, ALU.mult, ALU.add))
                    ch.link(v.tensor_scalar(r, r, quarter * TWO_PI, None, ALU.add))
                    for beyond, bound in ((ALU.is_gt, np.pi), (ALU.is_lt, -np.pi)):
                        ch.link(v.tensor_scalar(turns[:, :, :], r, float(bound), -2.0 * float(bound), beyond, ALU.mult))
                        ch.link(v.tensor_tensor(r, r, turns[:, :, :], ALU.add))
                    ch.link(v.tensor_scalar(r, r, 3.1415925, -3.1415925, ALU.min, ALU.max))
                v.memset(pos[:, :], 0.0).then_inc(S["reduced"], 1)

            @block.scalar
            def _(act):
                act.wait_ge(S["reduced"], 1)
                for which in range(2):
                    nc.scalar.activation(tables[:, :, which, :], red[:, which, :, :], ACT.Sin)
        S.close()


def projections(nc, A, x1, w, w_loaded, stage, tables, const):
    ident = const["ident"]
    with ExitStack() as ctx:
        sb = lambda n, s: ctx.enter_context(nc.sbuf_tensor("p2_" + n, s, F32))
        S = Signals(nc, "p2")
        B = [ctx.enter_context(nc.psum_tensor(f"p2_bank{i}", [P, 512], F32)) for i in range(8)]
        g_ch, pscale = sb("g_ch", [P, KD]), sb("pscale", [P, POOL_GROUPS])
        pw = sb("pw", [P, POOL_GROUPS, P])
        mb = sb("mb", [P, 512])
        ones = sb("ones", [P, P])
        qk_g = sb("qk_g", [P, 10, HEAD])
        xt, xn, hTs = sb("xt", [P, D]), sb("xn", [P, D]), sb("hT", [P, 2, KD, P])
        stat, numbers = sb("stat", [P, 2]), sb("numbers", [P, 4, 10])
        NEG_HALF, PER_D, PER_HEAD, EPS_ = range(4)
        pr = sb("pr", [P, C2_ZA])
        qk = sb("qk", [P, 10, HEAD])
        ssq, rsq = sb("ssq", [P, 10]), sb("rsq", [P, 10])
        cs = sb("cs", [P, 2, ROT + IDX_ROT])
        r4 = sb("r4", [P, 4, 10, ROT])
        ki4 = sb("ki4", [P, 4, IDX_DIM])
        u = sb("u", [P, POOL_GROUPS, HIST + P])
        w1, w2 = sb("w1", [P, POOL_GROUPS, HIST + P]), sb("w2", [P, POOL_GROUPS, HIST + P])
        inv = sb("inv", [P, POOL_GROUPS, P])
        zb = sb("zb", [P, POOL_GROUPS, P])
        st = sb("st", [P, T_END])
        flat = lambda ap: ap.rearrange("p a b -> p (a b)")
        with nc.Block() as block:
            @block.sync
            def _(sp):
                load = lambda dst, src: sp.dma_start(dst, src).then_inc(S["weights_loaded"], 16)
                k = KD - 1
                sp.dma_start(w[:, k, :], A["w_in_2"][0].rearrange("(k p) n -> p k n", p=P)[:, k, :]).then_inc(w_loaded, 16)
                load(g_ch[:, :], A["norm_g_2_ch"])
                load(pscale[:, :], A["pool_scale_2_ch"])
                load(pw[:, :, :], A["pool_w_2"][0].rearrange("g c d -> c g d"))
                for r in range(4):
                    load(mb[32 * r:32 * r + 1, :], A["merge_bias_2"][0, r // 2:r // 2 + 1, (r % 2) * 512:(r % 2) * 512 + 512])
                load(qk_g[:, 0:8, :], A["q_norm_g_2"].unsqueeze(1).broadcast_to([P, 8, HEAD]))
                load(qk_g[:, 8:10, :], A["k_norm_g_2"].unsqueeze(1).broadcast_to([P, 2, HEAD]))
                load(inv[:, :, :], A["k_inv"][0])
                sp.dma_start(xt[:, :], x1[0:P, :]).then_inc(S["x_loaded"], 16)
                sp.wait_ge(S["xn_ready"], 1)
                sp.dma_start(xt[:, :], x1[P:2 * P, :]).then_inc(S["x_loaded"], 16)
                sp.wait_ge(S["inv_used"], 1)
                sp.dma_start(inv[:, :, :], A["k_inv"][1]).then_inc(S["inv_ready"], 16)

                def store(t):
                    sp.wait_ge(S["bT_ready"], t + 1)
                    sp.wait_ge(S["gates23_taken"], t + 1)
                    sp.dma_start(stage[bass.ds(t * P, P), :], st[:, :]).then_inc(S["stage_stored"], 16)

                with sp.Fori(0, TILES - 2) as i:
                    store(i)
                    sp.wait_ge(S["xn_ready"], i + 2)
                    sp.dma_start(xt[:, :], x1[bass.ds((i + 2) * P, P), :]).then_inc(S["x_loaded"], 16)
                for t in (TILES - 2, TILES - 1):
                    store(t)
                sp.wait_ge(S["stage_stored"], 16 * TILES)

            N_WEIGHTS = 16 * (3 + 4 + 3)

            @block.gpsimd
            def _(pool):
                ch = Chain(pool, S["pool_step"])
                for at, value in enumerate((-0.5, 1.0 / D, 1.0 / HEAD, EPS)):
                    nc.gpsimd.memset(numbers[:, at, :], value)
                nc.gpsimd.memset(u[:, :, :], 0.0)
                nc.gpsimd.memset(w1[:, :, :], 0.0)
                nc.gpsimd.memset(w2[:, :, :], 0.0)
                ch.link(nc.gpsimd.memset(stat[:, :], 0.0))
                nc.gpsimd.memset(ones[:, :], 1.0).then_inc(S["setup_done"], 1)
                ch.start_over()

                def inv_sqrt(out, sums, n, per):
                    ch.link(nc.gpsimd.tensor_tensor(sums, sums, numbers[:, per, 0:n], ALU.mult))
                    ch.link(nc.gpsimd.tensor_tensor(sums, sums, numbers[:, EPS_, 0:n], ALU.add))
                    return nc.gpsimd.tensor_tensor(out, sums, numbers[:, NEG_HALF, 0:n], ALU.pow)

                def x_norm(n):
                    pool.wait_ge(S["x_squares"], n)
                    inv_sqrt(stat[:, 1:2], stat[:, 0:1], 1, PER_D).then_inc(S["x_rstd"], 1)

                x_norm(1)
                ch.start_over()
                for tile in tile_pairs(pool):
                    n = tile.n
                    if tile.more:
                        x_norm(n + 1)
                    pool.wait_ge(S["qk_squares"], n)
                    inv_sqrt(rsq[:, :], ssq[:, :], 10, PER_HEAD).then_inc(S["qk_rstd"], 1)
                    ch.start_over()

            @block.tensor
            def _(pe):
                mm, tr = nc.tensor.matmul, nc.tensor.transpose
                pe.wait_ge(w_loaded, 16 * KD)
                pe.wait_ge(S["weights_loaded"], N_WEIGHTS)
                pe.wait_ge(S["setup_done"], 1)

                def turn_x(n):
                    pe.wait_ge(S["xn_ready"], n)
                    for k in range(KD):
                        last = tr(B[k // 4][:, (k % 4) * P:(k % 4 + 1) * P], xn[:, k * P:(k + 1) * P], ident[:, :])
                    last.then_inc(S["x_turned"], 1)

                turn_x(1)
                for tile in tile_pairs(pe):
                    i, n, hT = tile.t, tile.n, hTs[:, tile.b]

                    def tokens(out, c, width, name):
                        for k in range(KD):
                            last = mm(out, hT[:, k, :], w[:, k, c:c + width], start=(k == 0), stop=(k == KD - 1))
                        last.then_inc(S[name], 1)

                    def channels(bank, c, name):
                        for m in range(4):
                            for k in range(KD):
                                last = mm(bank[:, m * P:(m + 1) * P], w[:, k, c + m * P:c + (m + 1) * P], hT[:, k, :], start=(k == 0), stop=(k == KD - 1))
                        last.then_inc(S[name], 1)

                    def gate(bank, r, name):
                        for k in range(KD):
                            mm(bank[:, :], hT[:, k, :], w[:, k, C2_GATES + r * 512:C2_GATES + (r + 1) * 512], start=(k == 0), stop=False)
                        mm(bank[:, :], ones[32 * r:32 * r + 1, :], mb[32 * r:32 * r + 1, :], start=False, stop=True).then_inc(S[name], 1)

                    pe.wait_ge(S["hT_act"], n)
                    pe.wait_ge(S["hT_dve"], n)
                    pe.wait_ge(S["kT_taken"], i)
                    tokens(B[5][:, :], C2_ZA, 512, "za_proj")
                    pe.wait_ge(S["gates23_taken"], i)
                    tokens(B[2][:, :], C2_Q, 512, "q_proj")
                    tokens(B[3][:, :], C2_K, 512, "kv_proj")
                    pe.wait_ge(S["qT_taken"], i)
                    tokens(B[4][:, 0:40], C2_KI, 40, "ki_proj")
                    pe.wait_ge(S["bT_ready"], i)
                    channels(B[6], C2_U, "u_proj")
                    channels(B[7], C2_ZB, "zb_proj")
                    gate(B[0], 0, "gate0")
                    gate(B[1], 1, "gate1")
                    pe.wait_ge(S["qk_ready"], n)
                    pe.wait_ge(S["pr_taken"], n)
                    pr_qk = flat(qk[:, :, :])
                    for c in range(4):
                        last = tr(B[4][:, c * P:(c + 1) * P], pr_qk[:, c * P:(c + 1) * P], ident[:, :])
                    last.then_inc(S["q_turned"], 1)
                    pe.wait_ge(S["za_ready"], n)
                    tr(B[5][:, 0:P], pr_qk[:, 512:640], ident[:, :])
                    tr(B[5][:, P:2 * P], flat(ki4[:, :, :]), ident[:, :])
                    for c in range(2):
                        last = tr(B[5][:, (2 + c) * P:(3 + c) * P], pr[:, C2_QI + c * P:C2_QI + (c + 1) * P], ident[:, :])
                    last.then_inc(S["k_turned"], 1)
                    pe.wait_ge(S["pooled_ready"], n)
                    for g in range(POOL_GROUPS):
                        last = mm(B[6][:, g * P:(g + 1) * P], pw[:, g, :], w1[:, g, 0:P], start=True, stop=True)
                    last.then_inc(S["pool_mixed"], 1)
                    if tile.more:
                        pe.wait_ge(S["gates01_taken"], n)
                        turn_x(n + 1)
                    gate(B[2], 2, "gate2")
                    gate(B[3], 3, "gate3")

            @block.scalar
            def _(act):
                f = nc.scalar.activation
                act.wait_ge(S["weights_loaded"], N_WEIGHTS)
                act.wait_ge(S["setup_done"], 1)

                def norm_x(n, t):
                    act.wait_ge(S["x_loaded"], n * 16)
                    act.wait_ge(S["x_turned"], t)
                    f(xn[:, :], xt[:, :], ACT.Square, accum_out=stat[:, 0:1]).then_inc(S["x_squares"], 1)
                    act.wait_ge(S["x_rstd"], n)
                    f(xn[:, :], xt[:, :], ACT.Copy, scale=stat[:, 1:2]).then_inc(S["xn_ready"], 1)

                def take_h(n, hT):
                    act.wait_ge(S["x_turned"], n)
                    for k in range(4):
                        last = f(hT[:, k, :], B[0][:, k * P:(k + 1) * P], ACT.Copy, scale=g_ch[:, k:k + 1])
                    last.then_inc(S["hT_act"], 1)

                norm_x(1, 0)
                take_h(1, hTs[:, 0])
                for tile in tile_pairs(act):
                    i, n = tile.t, tile.n
                    if tile.more:
                        norm_x(n + 1, n)
                    act.wait_ge(S["stage_stored"], i * 16)
                    act.wait_ge(S["za_proj"], n)
                    f(st[:, T_ZA:T_ZA + 512], B[5][:, :], ACT.Sigmoid).then_inc(S["za_sigmoid"], 1)
                    act.wait_ge(S["q_proj"], n)
                    act.wait_ge(S["k_turned"], i)
                    f(pr[:, 0:512], B[2][:, :], ACT.Copy).then_inc(S["q_taken"], 1)
                    act.wait_ge(S["zb_proj"], n)
                    f(flat(zb[:, :, :]), B[7][:, :], ACT.Sigmoid).then_inc(S["zb_sigmoid"], 1)
                    for r in range(2):
                        act.wait_ge(S[f"gate{r}"], n)
                        last = f(st[:, T_G + 512 * r:T_G + 512 * (r + 1)], B[r][:, :], ACT.Sigmoid)
                    last.then_inc(S["gates01_taken"], 1)
                    act.wait_ge(S["q_turned"], n)
                    f(st[:, T_QT:T_QT + 512], B[4][:, :], ACT.Copy).then_inc(S["qT_taken"], 1)
                    if tile.more:
                        take_h(n + 1, hTs[:, 1 - tile.b])
                    for r in range(2, 4):
                        act.wait_ge(S[f"gate{r}"], n)
                        last = f(st[:, T_G + 512 * r:T_G + 512 * (r + 1)], B[r][:, :], ACT.Sigmoid)
                    last.then_inc(S["gates23_taken"], 1)

            @block.vector
            def _(dve):
                ch = Chain(dve, S["dve_step"])
                v = nc.vector
                tt, ts, stt = v.tensor_tensor, v.tensor_scalar, v.scalar_tensor_tensor
                dve.wait_ge(S["weights_loaded"], N_WEIGHTS)
                dve.wait_ge(S["setup_done"], 1)

                def rotate(vectors, cos, sin, half):
                    heads = vectors.shape[1]
                    a, b = vectors[:, :, 0:half], vectors[:, :, half:2 * half]
                    c, s_ = spread(cos.unsqueeze(1), [P, heads, half]), spread(sin.unsqueeze(1), [P, heads, half])
                    t = [r4[:, e, 0:heads, 0:half] for e in range(4)]
                    tt(t[0], a, c, ALU.mult)
                    tt(t[1], b, s_, ALU.mult)
                    tt(t[2], a, s_, ALU.mult)
                    ch.link(tt(t[3], b, c, ALU.mult))
                    tt(a, t[0], t[1], ALU.subtract)
                    return tt(b, t[2], t[3], ALU.add)

                def take_h(n, hT):
                    dve.wait_ge(S["x_turned"], n)
                    for k in range(4, 8):
                        last = ts(hT[:, k, :], B[1][:, (k - 4) * P:(k - 3) * P], g_ch[:, k:k + 1], None, ALU.mult)
                    last.then_inc(S["hT_dve"], 1)

                take_h(1, hTs[:, 0])
                for tile in tile_pairs(dve):
                    i, n = tile.t, tile.n
                    v.tensor_copy(cs[:, :, :], tables[:, bass.ds(i, 1), :, :].rearrange("p a b c -> p (a b) c"))
                    dve.wait_ge(S["kv_proj"], n)
                    dve.wait_ge(S["k_turned"], i)
                    v.tensor_copy(pr[:, 512:1024], B[3][:, :])
                    dve.wait_ge(S["ki_proj"], n)
                    v.tensor_copy(pr[:, 1024:1064], B[4][:, 0:40]).then_inc(S["pr_taken"], 1)
                    dve.wait_ge(S["q_taken"], n)
                    dve.wait_ge(S["pr_taken"], n)
                    ch.link(tt(flat(qk[:, :, :]), pr[:, 0:640], pr[:, 0:640], ALU.mult))
                    v.tensor_reduce(ssq[:, :], qk[:, :, :], AX.X, ALU.add).then_inc(S["qk_squares"], 1)
                    ch.link(rotate(pr[:, C2_QI:C2_QI + 9 * IDX_DIM].rearrange("p (h d) -> p h d", d=IDX_DIM), cs[:, 0, ROT:], cs[:, 1, ROT:], IDX_ROT))
                    v.tensor_copy(ki4[:, :, :], spread(pr[:, C2_KI:C2_KI + IDX_DIM].unsqueeze(1), [P, 4, IDX_DIM]))
                    dve.wait_ge(S["stage_stored"], i * 16)
                    v.tensor_copy(st[:, T_V:T_V + P], pr[:, C2_V:C2_V + P])
                    wi, mag, sgn = pr[:, 1056:1064], st[:, T_W:T_W + 8], st[:, T_W + 8:T_W + 16]
                    ch.link(stt(mag, wi, -1.0, wi, ALU.mult, ALU.max))
                    ch.link(ts(mag, mag, 1.0 / 16.0, None, ALU.mult))
                    ch.link(ts(sgn, wi, 0.0, 2.0, ALU.is_ge, ALU.mult))
                    ch.link(ts(sgn, sgn, -1.0, None, ALU.add))
                    dve.wait_ge(S["qk_rstd"], n)
                    q_in = pr[:, 0:512].rearrange("p (g c d) -> p g c d", g=2, c=4)
                    q_out = flat(qk[:, 0:8, :]).rearrange("p (c g d) -> p g c d", g=2, c=4)
                    for g in range(2):
                        tt(q_out[:, g], q_in[:, g], spread(rsq[:, 4 * g:4 * g + 4].unsqueeze(2), [P, 4, HEAD]), ALU.mult)
                    ch.link(tt(qk[:, 8:10, :], pr[:, 512:640].rearrange("p (h d) -> p h d", d=HEAD), spread(rsq[:, 8:10].unsqueeze(2), [P, 2, HEAD]), ALU.mult))
                    ch.link(tt(flat(qk[:, :, :]), flat(qk[:, :, :]), flat(qk_g[:, :, :]), ALU.mult))
                    rotate(qk[:, :, :], cs[:, 0, 0:ROT], cs[:, 1, 0:ROT], ROT).then_inc(S["qk_ready"], 1)
                    dve.wait_ge(S["u_proj"], n)
                    dve.wait_ge(S["pool_mixed"], i)
                    ch.link(v.tensor_copy(u[:, :, HIST:], B[6][:, :].rearrange("p (g t) -> p g t", t=P)))
                    E = HIST + P
                    ch.link(tt(w1[:, :, 1:E], u[:, :, 1:E], u[:, :, 0:E - 1], ALU.add))
                    ch.link(tt(w2[:, 1:4, 3:E], w1[:, 1:4, 3:E], w1[:, 1:4, 1:E - 2], ALU.add))
                    ch.link(tt(w1[:, 2:4, 7:E], w2[:, 2:4, 7:E], w2[:, 2:4, 3:E - 4], ALU.add))
                    ch.link(tt(w2[:, 3:4, 15:E], w1[:, 3:4, 15:E], w1[:, 3:4, 7:E - 8], ALU.add))
                    for g, full in enumerate((w1, w2, w1, w2)):
                        last = tt(w2[:, g, HIST:], full[:, g, HIST:], inv[:, g, :], ALU.mult)
                    last.then_inc(S["inv_used"], 1)
                    dve.wait_ge(S["inv_used"], n)
                    tt(w1[:, :, 0:P], w2[:, :, HIST:], u[:, :, HIST:], ALU.subtract).then_inc(S["pooled_ready"], 1)
                    dve.wait_ge(S["pooled_ready"], n)
                    ch.link(v.tensor_copy(u[:, :, 0:HIST], u[:, :, P:P + HIST]))
                    dve.wait_ge(S["zb_sigmoid"], n)
                    ch.link(tt(flat(zb[:, :, :]), B[7][:, :], flat(zb[:, :, :]), ALU.mult))
                    dve.wait_ge(S["za_sigmoid"], n)
                    tt(st[:, T_ZA:T_ZA + 512], B[5][:, :], st[:, T_ZA:T_ZA + 512], ALU.mult).then_inc(S["za_ready"], 1)
                    dve.wait_ge(S["k_turned"], n)
                    v.tensor_copy(st[:, T_KT:T_KT + 2 * P], B[5][:, 0:2 * P])
                    v.tensor_copy(st[:, T_QI:T_QI + 256], B[5][:, 256:512]).then_inc(S["kT_taken"], 1)
                    dve.wait_ge(S["pool_mixed"], n)
                    for g in range(POOL_GROUPS):
                        last = stt(st[:, T_BT + g * P:T_BT + (g + 1) * P], B[6][:, g * P:(g + 1) * P], pscale[:, g:g + 1], zb[:, g, :], ALU.mult, ALU.mult)
                    last.then_inc(S["bT_ready"], 1)
                    if tile.more:
                        take_h(n + 1, hTs[:, 1 - tile.b])
                    dve.wait_ge(S["inv_ready"], 16)
                    ch.start_over()
        S.close()
BLK = 512
GROUP = BLK // P
HALVINGS = 25
BIG = 8.0e30
LEAST = 1.0e-30


class Turn:

    def __init__(self, blocks, a, b, in_group, units_a, units_b):
        self.blocks, self.a, self.b, self.in_group = blocks, a, b, in_group
        self.units_a, self.units_b = units_a, units_b
        self.width = blocks * BLK


def turns(eng):
    yield Turn(1, 0, None, 0, 0, 0)
    units_a, units_b = 8, 0
    for g in range(TILES // GROUP):
        first = max(g * GROUP, 1)
        count, per = (g + 1) * GROUP - first, 8 * (g + 1)
        with eng.Fori(0, count) as i:
            yield Turn(g + 1, eng.snap(i + first), eng.snap(i + (first - 1)), i + (first - g * GROUP),
                       i * per + units_a, i * per + units_b)
        units_a, units_b = units_a + count * per, units_b + count * per
    yield Turn(TILES // GROUP, None, TILES - 1, 0, 0, units_b)


def attention(nc, A, x1, stage, out, const):
    ident = const["ident"]
    with ExitStack() as ctx:
        sb = lambda n, s: ctx.enter_context(nc.sbuf_tensor("at_" + n, s, F32))
        S = Signals(nc, "at")
        B = [ctx.enter_context(nc.psum_tensor(f"at_bank{i}", [P, 512], F32)) for i in range(8)]
        LOGIT, SCORE, TURNED, OUT = B[0:2], B[2:4], B[4:6], B[6]
        KT, KI, VC = sb("KT", [P, SEQ]), sb("KI", [P, SEQ]), sb("VC", [P, TILES, P])
        wa, wb, wo = sb("wa", [P, 4, D]), sb("wb", [P, 4, D]), sb("wo", [P, KD, D])
        halves, allowed = sb("halves", [P, HALVINGS]), sb("allowed", [P, BLK + 3 * P])
        ones = sb("ones", [P, 1])
        qi = sb("qi", [P, 272])
        qT, rest = sb("qT", [P, 4, P]), sb("rest", [P, T_KT - T_ZA])
        x = sb("x", [P, D])
        r = sb("r", [P, 4, BLK])
        acc, bias = sb("acc", [P, SEQ]), sb("bias", [P, SEQ])
        tie, over, run = sb("tie", [P, SEQ]), sb("over", [P, SEQ]), sb("run", [P, SEQ])
        mid, cnt, width = sb("mid", [P, 4]), sb("cnt", [P, 4]), sb("width", [P, HALVINGS])
        s = sb("s", [P, 2, SEQ])
        pT = sb("pT", [P, 2, TILES, P])
        mx, nm, den = sb("mx", [P, 2, 4]), sb("nm", [P, 8]), sb("den", [P, 8])
        at, aT = sb("a", [P, 512]), sb("aT", [P, 4, P])
        y, yT, o = sb("y", [P, D]), sb("yT", [P, KD, P]), sb("o", [P, D])
        za, bT = rest[:, 0:512], rest[:, T_BT - T_ZA:T_G - T_ZA]
        gates = rest[:, T_G - T_ZA:T_KT - T_ZA]
        flat = lambda ap: ap.rearrange("p a b -> p (a b)")
        rows_of = lambda t: bass.ds(t * P, P)
        FIRST_STEPS = 2
        tests = [0, 0] + [HALVINGS // 6 + (1 if e < HALVINGS % 6 else 0) for e in range(6)]

        with nc.Block() as block:
            @block.sync
            def _(sp):
                load = lambda dst, src: sp.dma_start(dst, src).then_inc(S["constants_loaded"], 16)
                by_tile = stage.rearrange("(t p) c -> p t c", p=P)
                load(KI[:, :].rearrange("p (t c) -> p t c", c=P), by_tile[:, :, T_KI:T_KI + P])
                load(halves[:, :], row(A["k_halves"]))
                load(allowed[:, :], A["k_allowed"])
                load(KT[:, :].rearrange("p (t c) -> p t c", c=P), by_tile[:, :, T_KT:T_KT + P])
                load(VC[:, :, :], by_tile[:, :, T_V:T_V + P])
                load(wa[:, :, :], A["w_branch_a_2"][0].rearrange("(k p) n -> p k n", p=P))
                load(wb[:, :, :], A["w_branch_b_2"][0].rearrange("(k p) n -> p k n", p=P))
                load(wo[:, :, :], A["w_out_2"][0].rearrange("(k p) n -> p k n", p=P))
                for t in turns(sp):
                    if t.a is not None:
                        sp.wait_ge(S["index_done"], t.a)
                        sp.dma_start(qi[:, :], stage[rows_of(t.a), T_QI:T_ZA]).then_inc(S["qi_loaded"], 16)
                    if t.b is not None:
                        sp.wait_ge(S["pv_done"], t.b * 8)
                        sp.dma_start(flat(qT[:, :, :]), stage[rows_of(t.b), T_QT:T_QT + 512]).then_inc(S["qT_loaded"], 16)
                        sp.wait_ge(S["out_ready"], t.b)
                        sp.dma_start(rest[:, :], stage[rows_of(t.b), T_ZA:T_KT]).then_inc(S["rest_loaded"], 16)
                        sp.dma_start(x[:, :], x1[rows_of(t.b), :]).then_inc(S["rest_loaded"], 16)

            N_CONST = 16 * 8

            @block.gpsimd
            def _(pool):
                ch = Chain(pool, S["pool_step"])
                nc.gpsimd.memset(bias[:, :], -BIG)
                ch.link(nc.gpsimd.memset(mid[:, :], 0.0))
                nc.gpsimd.memset(ones[:, :], 1.0).then_inc(S["setup_done"], 1)
                for t in turns(pool):
                    if t.b is not None:
                        pool.wait_ge(S["out_ready"], t.b + 1)
                        pool.dma_start(out[rows_of(t.b), :], o[:, :]).then_inc(S["out_stored"], 16)
                pool.wait_ge(S["out_stored"], 16 * TILES)

            @block.tensor
            def _(pe):
                mm, tr = nc.tensor.matmul, nc.tensor.transpose
                pe.wait_ge(S["constants_loaded"], N_CONST)
                for t in turns(pe):
                    n = t.blocks

                    def index_products(h):
                        rows_h = slice(32 * (h % 4), 32 * (h % 4) + 32)
                        for kb in range(n):
                            j = h * n + kb
                            if not (isinstance(t.units_a, int) and t.units_a + j < 2):
                                pe.wait_ge(S["relu_done"], t.units_a + (j - 1))
                            mm(LOGIT[j % 2][:, :], qi[rows_h, (h // 4) * P:(h // 4 + 1) * P], KI[rows_h, kb * BLK:(kb + 1) * BLK],
                               start=True, stop=True).then_inc(S["logits"], 1)

                    def score_products(h):
                        g = slice(64 * (h // 4), 64 * (h // 4) + 64)
                        for kb in range(n):
                            j = h * n + kb
                            pe.wait_ge(S["masked"], t.units_b + (j + 1))
                            mm(SCORE[j % 2][:, :], qT[g, h % 4, :], KT[g, kb * BLK:(kb + 1) * BLK], start=True, stop=True).then_inc(S["scores"], 1)

                    def turn_probabilities(h):
                        pe.wait_ge(S["probs"], t.b * 8 + (h + 1))
                        for kb in range(n):
                            j = h * n + kb
                            pe.wait_ge(S["pT_taken"], t.units_b + (j + 1))
                            for e in range(GROUP):
                                last = tr(TURNED[j % 2][:, e * P:(e + 1) * P], s[:, h % 2, kb * BLK + e * P:kb * BLK + (e + 1) * P], ident[:, :])
                            last.then_inc(S["probs_turned"], 1)

                    def values(h):
                        pe.wait_ge(S["pT_taken"], t.units_b + ((h + 1) * n + 2))
                        for kt in range(GROUP * n):
                            last = mm(OUT[:, h * 64:(h + 1) * 64], pT[:, h % 2, kt, :], VC[:, kt, 64 * (h // 4):64 * (h // 4) + 64],
                                      start=(kt == 0), stop=(kt == GROUP * n - 1))
                        last.then_inc(S["pv_done"], 1)

                    if t.a is not None:
                        pe.wait_ge(S["qi_loaded"], t.a * 16 + 16)
                    if t.b is not None:
                        pe.wait_ge(S["qT_loaded"], t.b * 16 + 16)
                        pe.wait_ge(S["out_ready"], t.b)
                        score_products(0)
                    for h in range(8):
                        if t.a is not None and h < FIRST_STEPS:
                            for e in range(4 * h, 4 * h + 4):
                                index_products(e)
                        if t.b is None:
                            continue
                        if h < 7:
                            score_products(h + 1)
                        turn_probabilities(h)
                        if h > 0:
                            values(h - 1)
                    if t.b is None:
                        continue
                    values(7)
                    pe.wait_ge(S["a_ready"], t.b + 1)
                    for c in range(4):
                        last = tr(TURNED[0][:, c * P:(c + 1) * P], at[:, c * P:(c + 1) * P], ident[:, :])
                    last.then_inc(S["a_turned"], 1)
                    pe.wait_ge(S["rest_loaded"], t.b * 32 + 32)
                    for half in range(2):
                        for k in range(4):
                            last = mm((B[7], TURNED[1])[half][:, :], bT[:, k * P:(k + 1) * P], wb[:, k, half * 512:(half + 1) * 512], start=(k == 0), stop=(k == 3))
                    pe.wait_ge(S["aT_ready"], t.b + 1)
                    for half in range(2):
                        for k in range(4):
                            last = mm(SCORE[half][:, :], aT[:, k, :], wa[:, k, half * 512:(half + 1) * 512], start=(k == 0), stop=(k == 3))
                    last.then_inc(S["branches_done"], 1)
                    pe.wait_ge(S["y_ready"], t.b + 1)
                    for k in range(KD):
                        last = tr(SCORE[k // 4][:, (k % 4) * P:(k % 4 + 1) * P], y[:, k * P:(k + 1) * P], ident[:, :])
                    last.then_inc(S["y_turned"], 1)
                    pe.wait_ge(S["yT_ready"], t.b + 1)
                    for half in range(2):
                        for k in range(KD):
                            last = mm(TURNED[half][:, :], yT[:, k, :], wo[:, k, half * 512:(half + 1) * 512], start=(k == 0), stop=(k == KD - 1))
                    last.then_inc(S["projected"], 1)

            @block.scalar
            def _(act):
                f = nc.scalar.activation
                act.sem_inc(S["pT_taken"], 2)
                for t in turns(act):
                    n = t.blocks
                    if t.a is not None:
                        act.wait_ge(S["qi_loaded"], t.a * 16 + 16)

                    def index_relu(h):
                        for kb in range(n):
                            j = h * n + kb
                            act.wait_ge(S["logits"], t.units_a + (j + 1))
                            if not (isinstance(t.units_a, int) and t.units_a + j < 4):
                                act.wait_ge(S["summed"], t.units_a + (j - 3))
                            f(r[:, j % 4, :], LOGIT[j % 2][:, :], ACT.Relu, scale=qi[:, 256 + h:257 + h]).then_inc(S["relu_done"], 1)

                    for h in range(8):
                        if t.b is not None:
                            act.wait_ge(S["row_max"], t.b * 8 + (h + 1))
                            f(s[:, h % 2, 0:t.width], s[:, h % 2, 0:t.width], ACT.Exp, bias=nm[:, h:h + 1], accum_out=den[:, h:h + 1]).then_inc(S["probs"], 1)
                        if t.a is not None and h < FIRST_STEPS:
                            for e in range(4 * h, 4 * h + 4):
                                index_relu(e)
                        if t.b is not None:
                            if h >= 2:
                                act.wait_ge(S["pv_done"], t.b * 8 + (h - 1))
                            for kb in range(n):
                                j = h * n + kb
                                act.wait_ge(S["probs_turned"], t.units_b + (j + 1))
                                f(flat(pT[:, h % 2, kb * GROUP:(kb + 1) * GROUP, :]), TURNED[j % 2][:, :], ACT.Copy).then_inc(S["pT_taken"], 1)
                    if t.b is not None:
                        act.wait_ge(S["a_turned"], t.b + 1)
                        f(flat(aT[:, :, :]), TURNED[0][:, :], ACT.Copy).then_inc(S["aT_ready"], 1)
                        act.wait_ge(S["y_turned"], t.b + 1)
                        f(flat(yT[:, 0:4, :]), SCORE[0][:, :], ACT.Copy)
                        f(flat(yT[:, 4:8, :]), SCORE[1][:, :], ACT.Copy).then_inc(S["yT_ready"], 1)

            @block.vector
            def _(dve):
                ch = Chain(dve, S["dve_step"])
                v = nc.vector
                tt, ts, stt = v.tensor_tensor, v.tensor_scalar, v.scalar_tensor_tensor
                dve.sem_inc(S["masked"], 2)
                dve.wait_ge(S["constants_loaded"], N_CONST)
                dve.wait_ge(S["setup_done"], 1)
                for t in turns(dve):
                    n, L = t.blocks, t.width

                    def index_sum(h):
                        sgn = qi[:, 264 + h:265 + h]
                        for kb in range(n):
                            j = h * n + kb
                            dve.wait_ge(S["relu_done"], t.units_a + (j + 1))
                            part = acc[:, kb * BLK:(kb + 1) * BLK]
                            if h == 0:
                                last = ts(part, r[:, j % 4, :], sgn, None, ALU.mult)
                            else:
                                dve.wait_ge(S["summed"], t.units_a + (j - n + 1))
                                last = stt(part, r[:, j % 4, :], sgn, part, ALU.mult, ALU.add)
                            last.then_inc(S["summed"], 1)

                    def search_range():
                        dve.wait_ge(S["summed"], t.units_a + 8 * n)
                        ch.link(v.tensor_reduce(cnt[:, 1:2], acc[:, 0:L], AX.X, ALU.max, apply_absolute_value=True))
                        ch.link(ts(cnt[:, 1:2].bitcast(I32), cnt[:, 1:2].bitcast(I32), 0x7f800000, None, ALU.bitwise_and))
                        ch.link(ts(cnt[:, 1:2], cnt[:, 1:2], 2.0, LEAST, ALU.mult, ALU.max))
                        ts(width[:, :], halves[:, :], cnt[:, 1:2], None, ALU.mult)
                        v.memset(mid[:, 0:1], 0.0)
                        start = t.in_group * (-P) + 3 * P
                        last_block = acc[:, L - BLK:L]
                        tt(last_block, last_block, allowed[:, bass.ds(start, BLK)], ALU.add).then_inc(S["index_done"], 1)
                        dve.wait_ge(S["index_done"], t.a + 1)

                    def halve(k):
                        ch.link(ts(run[:, 0:L], acc[:, 0:L], mid[:, 0:1], 0.0, ALU.is_ge, ALU.add, accum_out=cnt[:, 0:1]))
                        if k < HALVINGS - 1:
                            ch.link(ts(cnt[:, 2:3], cnt[:, 0:1], TOPK - 0.5, -0.5, ALU.is_ge, ALU.add))
                            ch.link(stt(mid[:, 0:1], cnt[:, 2:3], width[:, k:k + 1], mid[:, 0:1], ALU.mult, ALU.add))
                        else:
                            ch.link(ts(cnt[:, 2:3], cnt[:, 0:1], TOPK - 0.5, -1.0, ALU.is_ge, ALU.add))
                            ch.link(stt(mid[:, 1:2], cnt[:, 2:3], width[:, k:k + 1], mid[:, 0:1], ALU.mult, ALU.add))
                            ch.link(tt(mid[:, 2:3], mid[:, 1:2], width[:, k:k + 1], ALU.add))

                    def select():
                        lo, hi = mid[:, 1:2], mid[:, 2:3]
                        ts(tie[:, 0:L], acc[:, 0:L], lo, None, ALU.is_ge)
                        ch.link(ts(over[:, 0:L], acc[:, 0:L], hi, 0.0, ALU.is_ge, ALU.add, accum_out=cnt[:, 0:1]))
                        ch.link(tt(tie[:, 0:L], tie[:, 0:L], over[:, 0:L], ALU.subtract))
                        ts(cnt[:, 3:4], cnt[:, 0:1], -1.0, float(TOPK), ALU.mult, ALU.add)
                        ch.link(v.tensor_tensor_scan(run[:, 0:L], spread(ones[:, :], [P, L]), tie[:, 0:L], 0.0, ALU.mult, ALU.add))
                        ch.link(stt(tie[:, 0:L], run[:, 0:L], cnt[:, 3:4], tie[:, 0:L], ALU.is_le, ALU.mult))
                        ch.link(tt(tie[:, 0:L], tie[:, 0:L], over[:, 0:L], ALU.add))
                        ch.link(ts(bias[:, 0:L], tie[:, 0:L], BIG, -BIG, ALU.mult, ALU.add))

                    def mask(h):
                        if h >= 2:
                            dve.wait_ge(S["probs_turned"], t.units_b + (h - 1) * n)
                        for kb in range(n):
                            j = h * n + kb
                            c = slice(kb * BLK, (kb + 1) * BLK)
                            dve.wait_ge(S["scores"], t.units_b + (j + 1))
                            dve.sem_inc(S["score_seen"], 1)
                            v.tensor_tensor_reduce(out=s[:, h % 2, c], in0=SCORE[j % 2][:, :], in1=bias[:, c], scale=HEAD ** -0.5, scalar=-3.0e38,
                                                   op0=ALU.add, op1=ALU.max, accum_out=mx[:, h % 2, kb:kb + 1]).then_inc(S["masked"], 1)
                        dve.wait_ge(S["masked"], t.units_b + ((h + 1) * n + 2))
                        ch.link(v.tensor_reduce(nm[:, h:h + 1], mx[:, h % 2, 0:n], AX.X, ALU.max))
                        ts(nm[:, h:h + 1], nm[:, h:h + 1], -1.0, None, ALU.mult).then_inc(S["row_max"], 1)

                    if t.a is not None:
                        dve.wait_ge(S["qi_loaded"], t.a * 16 + 16)
                    done = 0
                    for h in range(8):
                        if t.b is not None:
                            mask(h)
                        if t.a is not None:
                            if h < FIRST_STEPS:
                                for e in range(4 * h, 4 * h + 4):
                                    index_sum(e)
                            if h == FIRST_STEPS:
                                search_range()
                            for _k in range(tests[h]):
                                halve(done)
                                done += 1
                    if t.b is not None:
                        dve.wait_ge(S["pv_done"], t.b * 8 + 8)
                        ch.link(v.reciprocal(den[:, :], den[:, :]))
                        hd = lambda ap: ap.rearrange("p (h d) -> p h d", d=HEAD)
                        ch.link(tt(hd(at[:, :]), hd(OUT[:, :]), spread(den[:, :].unsqueeze(2), [P, 8, HEAD]), ALU.mult))
                        dve.wait_ge(S["rest_loaded"], t.b * 32 + 32)
                        tt(at[:, :], at[:, :], za, ALU.mult).then_inc(S["a_ready"], 1)
                    if t.a is not None:
                        select()
                    if t.b is not None:
                        dve.wait_ge(S["branches_done"], t.b + 1)
                        dve.wait_ge(S["out_stored"], t.b * 16)
                        for half in range(2):
                            c = slice(half * 512, (half + 1) * 512)
                            tt(y[:, c], SCORE[half][:, :], gates[:, half * 512:(half + 1) * 512], ALU.mult)
                            last = tt(o[:, c], (B[7], TURNED[1])[half][:, :], gates[:, 1024 + half * 512:1024 + (half + 1) * 512], ALU.mult)
                        ch.link(last)
                        tt(y[:, :], y[:, :], o[:, :], ALU.add).then_inc(S["y_ready"], 1)
                        dve.wait_ge(S["y_ready"], t.b + 1)
                        dve.wait_ge(S["projected"], t.b + 1)
                        for half in range(2):
                            c = slice(half * 512, (half + 1) * 512)
                            last = tt(o[:, c], TURNED[half][:, :], x[:, c], ALU.add)
                        last.then_inc(S["out_ready"], 1)
                    ch.start_over()
        S.close()


def build(nc, A, out):
    with ExitStack() as ctx:
        sb = lambda n, s: ctx.enter_context(nc.sbuf_tensor(n, s, F32))
        dram = lambda n, s: nc.dram_tensor(n, s, F32, kind="Internal").ap()
        const = dict(ident=sb("ident", [P, P]))
        keep = dict(scale_ch=sb("scale_ch", [P, KD]), shift_ch=sb("shift_ch", [P, KD]), gate_row=dram("gate_row", (P, D)))
        stage1, mixed = dram("stage1", (SEQ, M_END)), dram("mixed", (SEQ, D))
        x1, stage = dram("x1", (SEQ, D)), dram("stage", (SEQ, T_END))
        identity_loaded, w_in_loaded, w_in_2_loaded = map(nc.alloc_semaphore, ("identity_loaded", "w_in_loaded", "w_in_2_loaded"))
        with nc.Block() as block:
            @block.sync
            def _(sp):
                sp.dma_start(const["ident"][:, :], A["k_ident"]).then_inc(identity_loaded, 16)
                sp.wait_ge(identity_loaded, 16)
        with nc.sbuf_tensor("w_in", [P, KD, IN1], F32) as w_in:
            adaptive_norm(nc, A, w_in, w_in_loaded, keep, const)
            mixer_projections(nc, A, w_in, w_in_loaded, stage1, keep, const)
        mixers(nc, A, stage1, mixed, const)
        with nc.sbuf_tensor("w_in_2", [P, KD, IN2], F32) as w_in_2:
            output_and_residual(nc, A, mixed, x1, w_in_2, w_in_2_loaded, keep, const)
            with nc.sbuf_tensor("tables", [P, TILES, 2, ROT + IDX_ROT], F32) as tables:
                rotary_tables(nc, A, tables)
                projections(nc, A, x1, w_in_2, w_in_2_loaded, stage, tables, const)
        attention(nc, A, x1, stage, out, const)


def shape_constants():
    s, t = np.arange(P)[:, None], np.arange(P)[None]
    masks = np.zeros((P, LEVELS, P), np.float32)
    for level in range(LEVELS):
        half = 1 << level
        masks[:, level] = (s // (2 * half) == t // (2 * half)) & (t // half % 2 == 1) & (s // half % 2 == 0)
    one_chunk = s // R_CHUNK == t // R_CHUNK
    tri = np.stack([(s < t) & one_chunk, (s <= t) & one_chunk], axis=1).astype(np.float32)
    quad = (s // G_KEY == np.arange(R_W)[None] // G_VAL).astype(np.float32)
    chunk_of = (s // R_CHUNK == np.arange(2)[None]).astype(np.float32)
    dist = np.arange(P)[:, None] - np.arange(2 * P)[None] + P
    slopes = (2.0 ** -np.arange(1, A_HEADS + 1)).astype(np.float32)
    alibi = np.where(((dist >= 0) & (dist < P))[:, None, :], -slopes[None, :, None] * dist[:, None, :].astype(np.float32), NEG)
    freq8 = ["0x1p+0", "0x1.8d275ep-3", "0x1.34119p-5", "0x1.ddee9cp-8", "0x1.72ba44p-10", "0x1.1f91fp-12", "0x1.be2188p-15", "0x1.5a0f4ep-17"]
    freq = np.array([[float.fromhex(f) for f in freq8 + freq8[::2]]], np.float32)
    inv = np.zeros((2, P, POOL_GROUPS, P), np.float32)
    for g, w in enumerate((2, 4, 8, 16)):
        inv[0, :, g], inv[1, :, g] = 1.0 / np.minimum(np.arange(P) + 1, w), 1.0 / w
    reach = np.arange(BLK + 3 * P)[None] - 3 * P
    allowed = np.where(reach < 64 * (np.arange(P)[:, None] >= 64) + 64, 0.0, NEG)
    return {
        "k_ident": np.eye(P, dtype=np.float32), "k_masks": masks, "k_tri": tri,
        "k_pair": (s // HEAD == t // HEAD).astype(np.float32), "k_quad": quad, "k_chunk_of": chunk_of,
        "k_alibi": alibi.astype(np.float32), "k_freq": freq, "k_inv": inv, "k_allowed": allowed.astype(np.float32),
        "k_halves": (2.0 ** -np.arange(HALVINGS))[None].astype(np.float32),
    }


def kernel(**inputs):
    import concourse.bacc as bacc
    from concourse.bass_utils import run_bass_kernel_spmd as run

    nc = bacc.Bacc("TRN2", target_bir_lowering=False, num_devices=1)
    arrays = {}
    by_column = ("c", "ada_b", "norm_pre", "gla_gk_b", "rwkv_mu_w", "rwkv_mu_a", "rwkv_mu_rkv", "norm_g_2", "pool_scale_2", "positions_2")
    only_so = ("c", "norm_pre", "gla_gk_b", "rwkv_mu_w", "rwkv_mu_a", "rwkv_mu_rkv", "norm_g_2", "pool_scale_2", "positions_2")
    for name, value in inputs.items():
        a = np.ascontiguousarray(value)
        if name in by_column:
            arrays[name + "_ch"] = np.ascontiguousarray(a.reshape(-1, P).T)
        if name not in only_so:
            arrays[name] = a
    arrays.update(shape_constants())
    A, fed = {}, {}
    for name, a in arrays.items():
        fed["in_" + name] = a
        A[name] = nc.dram_tensor("in_" + name, a.shape, mybir.dt.from_np(a.dtype), kind="ExternalInput").ap()
    out = nc.dram_tensor("out", (1, SEQ, D), F32, kind="ExternalOutput").ap()
    build(nc, A, out[0])
    return run(nc, [fed], core_ids=[0]).results[0]["out"]
```

```python
import concourse.bass as bass
from concourse import mybir
from contextlib import ExitStack
import numpy as np

F32 = mybir.dt.float32
I32 = mybir.dt.int32
U32 = mybir.dt.uint32
ALU = mybir.AluOpType
ACT = mybir.ActivationFunctionType
AX = mybir.AxisListType

P = 128
D = 1024
KD = D // P
SEQ = 2048
TILES = SEQ // P
HEAD = 64
EPS = 1e-6
NEG = -1.0e30

A_HEADS, A_KV = 8, 2
C_AQ, C_AK, C_AV, C_AG = 0, 512, 640, 768
C_RKV, C_RG = 1280, 2048
C_GQ, C_GK, C_GV, C_GG = 2304, 2432, 2560, 2816
IN1 = 3072
R_HEADS, R_W, R_CHUNK = 4, 256, 64
RWKV_LN_EPS = 64e-5
G_HEADS, G_KEY, G_VAL = 4, 32, 64
LEVELS = 7
INV_LEVELS = 6


class Signals(dict):

    def __init__(self, nc, phase):
        super().__init__()
        self.nc, self.phase = nc, phase

    def __missing__(self, name):
        self[name] = self.nc.alloc_semaphore(f"{self.phase}_{name}")
        return self[name]

    def close(self):
        self.nc.clear_and_free_semaphores(list(self.values()))
        self.nc.all_engine_barrier()


class Chain:

    def __init__(self, eng, sem):
        self.eng, self.sem, self.count = eng, sem, 0

    def link(self, ins):
        self.count += 1
        ins.then_inc(self.sem, 1)
        self.eng.wait_ge(self.sem, self.count)

    def start_over(self):
        self.eng.sem_clear(self.sem)
        self.count = 0


class Tile:

    def __init__(self, turn, t, n, b, more):
        self.turn, self.t, self.n, self.b, self.more = turn, t, n, b, more


def tile_pairs(eng):
    with eng.Fori(0, TILES // 2 - 1) as i:
        for b in range(2):
            yield Tile(i, eng.snap(2 * i + b), eng.snap(2 * i + (b + 1)), b, True)
    for b in range(2):
        yield Tile(TILES // 2 - 1, TILES - 2 + b, TILES - 1 + b, b, b == 0)


def row(ap_row, n=P):
    return ap_row.broadcast_to([n, ap_row.shape[1]])


def spread(ap, shape):
    return ap.broadcast_to(shape)


def adaptive_norm(nc, A, w_in, w_in_loaded, keep, const):
    g1, sh = keep["scale_ch"], keep["shift_ch"]
    with ExitStack() as ctx:
        sb = lambda n, s: ctx.enter_context(nc.sbuf_tensor("ad_" + n, s, F32))
        S = Signals(nc, "ad")
        ada = sb("w", [P, KD, 3 * D])
        cc, ce, ca = sb("c", [P, KD]), sb("ce", [P, KD]), sb("ca", [P, KD])
        cb = sb("cb", [P, KD, P])
        b_ch, npre = sb("b_ch", [P, 2 * KD]), sb("npre", [P, KD])
        gate_row, np_row = sb("gate_row", [P, D]), sb("np_row", [P, D])
        ps = ctx.enter_context(nc.psum_tensor("ad_ps", [P, 512], F32))
        pg = ctx.enter_context(nc.psum_tensor("ad_pg", [P, 1024], F32))
        with nc.Block() as block:
            @block.sync
            def _(sp):
                sp.dma_start(cc[:, :], A["c_ch"]).then_inc(S["c_loaded"], 16)
                src = A["ada_w"][0].rearrange("(k p) n -> p k n", p=P)
                for c in range(6):
                    cols = slice(c * 512, (c + 1) * 512)
                    sp.dma_start(ada[:, :, cols], src[:, :, cols]).then_inc(S[f"w_loaded{c}"], 16)
                sp.dma_start(b_ch[:, :], A["ada_b_ch"][:, 0:2 * KD]).then_inc(S["small_loaded"], 16)
                sp.dma_start(npre[:, :], A["norm_pre_ch"]).then_inc(S["small_loaded"], 16)
                sp.dma_start(gate_row[:, :], row(A["ada_b"][0:1, 2 * D:3 * D])).then_inc(S["small_loaded"], 16)
                sp.dma_start(np_row[:, :], row(A["norm_post"][0:1, :])).then_inc(S["small_loaded"], 16)
                wsrc = A["w_in"][0].rearrange("(k p) n -> p k n", p=P)
                for k in range(KD):
                    sp.dma_start(w_in[:, k, 512:], wsrc[:, k, 512:]).then_inc(w_in_loaded, 16)
                    for g in range(A_KV):
                        sp.dma_start(w_in[:, k, 0:512].rearrange("p (c g d) -> p g c d", g=2, d=HEAD)[:, g],
                                     wsrc[:, k, 256 * g:256 * g + 256].rearrange("p (c d) -> p c d", d=HEAD)).then_inc(w_in_loaded, 16)
                sp.wait_ge(S["gate_ready"], 1)
                sp.dma_start(keep["gate_row"], gate_row[:, :]).then_inc(S["gate_stored"], 16)
                sp.wait_ge(S["gate_stored"], 16)

            @block.scalar
            def _(act):
                act.wait_ge(S["c_loaded"], 16)
                nc.scalar.activation(ce[:, :], cc[:, :], ACT.Exp, scale=-1.0).then_inc(S["exp_done"], 1)

            @block.vector
            def _(dve):
                ch = Chain(dve, S["dve_step"])
                dve.wait_ge(S["exp_done"], 1)
                ch.link(nc.vector.tensor_scalar(ce[:, :], ce[:, :], 1.0, None, ALU.add))
                ch.link(nc.vector.reciprocal(ce[:, :], ce[:, :]))
                ch.link(nc.vector.tensor_tensor(ca[:, :], cc[:, :], ce[:, :], ALU.mult))
                nc.vector.tensor_copy(cb[:, :, :], spread(ca[:, :].unsqueeze(2), [P, KD, P])).then_inc(S["c_act_ready"], 1)
                dve.wait_ge(S["products_done"], 1)
                dve.wait_ge(S["small_loaded"], 64)
                nc.vector.tensor_tensor(sh[:, :], ps[:, 0:KD], b_ch[:, 0:KD], ALU.add)
                ch.link(nc.vector.tensor_tensor(ce[:, :], ps[:, KD:2 * KD], b_ch[:, KD:2 * KD], ALU.add))
                nc.vector.scalar_tensor_tensor(g1[:, :], ce[:, :], 1.0, npre[:, :], ALU.add, ALU.mult)
                ch.link(nc.vector.tensor_tensor(gate_row[:, :], pg[:, :], gate_row[:, :], ALU.add))
                nc.vector.tensor_tensor(gate_row[:, :], gate_row[:, :], np_row[:, :], ALU.mult).then_inc(S["gate_ready"], 1)

            @block.tensor
            def _(pe):
                pe.wait_ge(S["c_act_ready"], 1)
                for m in range(2 * KD):
                    if m % 4 == 0:
                        pe.wait_ge(S[f"w_loaded{m // 4}"], 16)
                    for k in range(KD):
                        nc.tensor.matmul(ps[:, m:m + 1], ada[:, k, m * P:(m + 1) * P], ca[:, k:k + 1],
                                         start=(k == 0), stop=(k == KD - 1))
                for half in range(2):
                    pe.wait_ge(S[f"w_loaded{4 + half}"], 16)
                    for k in range(KD):
                        last = nc.tensor.matmul(pg[:, half * 512:(half + 1) * 512], cb[:, k, :],
                                                ada[:, k, 2 * D + half * 512:2 * D + (half + 1) * 512],
                                                start=(k == 0), stop=(k == KD - 1))
                last.then_inc(S["products_done"], 1)
        S.close()


M_Q, M_K, M_V, M_SG, M_RKV, M_WA, M_GQ, M_GK, M_GB, M_GV, M_END = 0, 512, 640, 768, 1792, 2560, 3072, 3200, 3328, 3456, 3712


def mixer_projections(nc, A, w_in, w_in_loaded, stage1, keep, const):
    scale_ch, shift_ch = keep["scale_ch"], keep["shift_ch"]
    ident = const["ident"]
    with ExitStack() as ctx:
        sb = lambda n, s: ctx.enter_context(nc.sbuf_tensor("p1_" + n, s, F32))
        S = Signals(nc, "p1")
        B = [ctx.enter_context(nc.psum_tensor(f"p1_bank{i}", [P, 512], F32)) for i in range(8)]
        lora_cur, lora_prev = sb("lora_cur", [P, KD, P]), sb("lora_prev", [P, KD, P])
        gk1, gkb = sb("gk1", [P, KD, 16]), sb("gkb", [P, 1])
        mu_w, mu_a = sb("mu_w", [P, KD]), sb("mu_a", [P, KD])
        mu_rkv = sb("mu_rkv", [P, 6])
        wa2 = sb("wa2", [P, 2, R_W])
        lows = sb("lows", [P, 2 * R_W])
        gk2, wa0 = lows[0:16, 0:P], lows[32:33, :]
        ones, numbers = sb("ones", [P, P]), sb("numbers", [P, 3])
        xt, xn = sb("xt", [P, D]), sb("xn", [P, D])
        stat = sb("stat", [P, 2])
        hTs = sb("hT", [P, 2, KD, P + 1])
        loraT, gk1T = sb("loraT", [P, P]), sb("gk1T", [16, P])
        rkvT, mixT = sb("rkvT", [P, 6, P + 1]), sb("mixT", [P, 6, P])
        gz = sb("gz", [P, 2, P])
        st = sb("st", [P, 2, M_END])
        flat = lambda ap: ap.rearrange("p a b -> p (a b)")
        with nc.Block() as block:
            @block.sync
            def _(sp):
                load = lambda dst, src: sp.dma_start(dst, src).then_inc(S["weights_loaded"], 16)
                sp.dma_start(xt[:, :], A["x"][0][0:P, :]).then_inc(S["x_loaded"], 16)
                load(lora_cur[:, :, 0:64], A["rwkv_w1"][0].rearrange("(k p) n -> p k n", p=P))
                load(lora_cur[:, :, 64:128], A["rwkv_a1"][0].rearrange("(k p) n -> p k n", p=P))
                load(gk1[:, :, :], A["gla_gk1"][0].rearrange("(k p) n -> p k n", p=P))
                load(gk2[:, :], A["gla_gk2"][0])
                load(gkb[:, :], A["gla_gk_b_ch"])
                load(mu_w[:, :], A["rwkv_mu_w_ch"])
                load(mu_a[:, :], A["rwkv_mu_a_ch"])
                load(mu_rkv[:, :], A["rwkv_mu_rkv_ch"])
                load(wa2[0:64, 0, :], A["rwkv_w2"][0])
                load(wa2[64:128, 1, :], A["rwkv_a2"][0])
                load(wa0[:, 0:R_W], A["rwkv_w0"][0:1, :])
                load(wa0[:, R_W:], A["rwkv_a0"][0:1, :])
                for tile in tile_pairs(sp):
                    i, n = tile.t, tile.n
                    if tile.more:
                        sp.wait_ge(S["xn_ready"], n)
                        sp.dma_start(xt[:, :], A["x"][0][bass.ds(n * P, P), :]).then_inc(S["x_loaded"], 16)
                    sp.wait_ge(S["act_staged"], n)
                    sp.wait_ge(S["dve_staged"], n)
                    sp.dma_start(stage1[bass.ds(i * P, P), :], st[:, tile.b, :]).then_inc(S[f"stage_stored{tile.b}"], 16)
                for b in range(2):
                    sp.wait_ge(S[f"stage_stored{b}"], 16 * TILES // 2)

            N_WEIGHTS = 16 * 12

            @block.gpsimd
            def _(pool):
                ch = Chain(pool, S["pool_step"])
                for at, value in enumerate((-0.5, 1.0 / D, EPS)):
                    nc.gpsimd.memset(numbers[:, at:at + 1], value)
                nc.gpsimd.memset(ones[:, :], 1.0)
                nc.gpsimd.memset(hTs[:, 0, :, 0:1], 0.0)
                nc.gpsimd.memset(rkvT[:, :, P:P + 1], 0.0)
                ch.link(nc.gpsimd.memset(wa2[0:64, 1, :], 0.0))

                def x_norm(n):
                    pool.wait_ge(S["x_squares"], n)
                    ch.link(nc.gpsimd.tensor_tensor(stat[:, 0:1], stat[:, 0:1], numbers[:, 1:2], ALU.mult))
                    ch.link(nc.gpsimd.tensor_tensor(stat[:, 0:1], stat[:, 0:1], numbers[:, 2:3], ALU.add))
                    nc.gpsimd.tensor_tensor(stat[:, 1:2], stat[:, 0:1], numbers[:, 0:1], ALU.pow).then_inc(S["x_rstd"], 1)

                x_norm(1)
                pool.wait_ge(S["weights_loaded"], N_WEIGHTS)
                for mu_ch, hs in ((mu_w, slice(0, 64)), (mu_a, slice(64, 128))):
                    mu = spread(mu_ch[:, :].unsqueeze(2), [P, KD, 64])
                    ch.link(nc.gpsimd.tensor_tensor(lora_prev[:, :, hs], lora_cur[:, :, hs], mu, ALU.mult))
                    ch.link(nc.gpsimd.tensor_tensor(lora_cur[:, :, hs], lora_cur[:, :, hs], lora_prev[:, :, hs], ALU.subtract))
                nc.gpsimd.memset(wa2[64:128, 0, :], 0.0).then_inc(S["setup_done"], 1)
                ch.start_over()
                for tile in tile_pairs(pool):
                    if tile.more:
                        x_norm(tile.n + 1)
                    ch.start_over()

            @block.tensor
            def _(pe):
                mm, tr = nc.tensor.matmul, nc.tensor.transpose

                def turn_x(n):
                    pe.wait_ge(S["xn_ready"], n)
                    for k in range(KD):
                        last = tr(B[k // 4][:, (k % 4) * P:(k % 4 + 1) * P], xn[:, k * P:(k + 1) * P], ident[:, :])
                    last.then_inc(S["x_turned"], 1)

                turn_x(1)
                pe.wait_ge(w_in_loaded, 16 * 3 * KD)
                pe.wait_ge(S["setup_done"], 1)
                for tile in tile_pairs(pe):
                    i, n, hT = tile.t, tile.n, hTs[:, tile.b]

                    def channels(out, c):
                        for k in range(KD):
                            last = mm(out, w_in[:, k, c:c + P], hT[:, k, 1:P + 1], start=(k == 0), stop=(k == KD - 1))
                        return last

                    def tokens(out, c, width):
                        for k in range(KD):
                            last = mm(out, hT[:, k, 1:P + 1], w_in[:, k, c:c + width], start=(k == 0), stop=(k == KD - 1))
                        return last

                    pe.wait_ge(S["hT_act"], n)
                    pe.wait_ge(S["hT_dve"], n)
                    pe.wait_ge(S["gate_biased"], i)
                    for k in range(KD):
                        mm(B[3][:, 3 * P:4 * P], lora_cur[:, k, :], hT[:, k, 1:P + 1], start=(k == 0), stop=False)
                    for k in range(KD):
                        last = mm(B[3][:, 3 * P:4 * P], lora_prev[:, k, :], hT[:, k, 0:P], start=False, stop=(k == KD - 1))
                    for spot, c in enumerate((C_AK, C_GQ, C_GK)):
                        last = channels(B[3][:, spot * P:(spot + 1) * P], c)
                    last.then_inc(S["k_lora_proj"], 1)
                    pe.wait_ge(S["tok_taken"], i)
                    for c in range(4):
                        last = channels(B[4][:, c * P:(c + 1) * P], C_RKV + P * c)
                    last.then_inc(S["rk_proj"], 1)
                    for c in range(2):
                        channels(B[5][:, c * P:(c + 1) * P], C_RKV + P * (4 + c))
                    for k in range(KD):
                        last = mm(B[5][0:16, 2 * P:3 * P], gk1[:, k, :], hT[:, k, 1:P + 1], start=(k == 0), stop=(k == KD - 1))
                    last.then_inc(S["v_gk1_proj"], 1)
                    tokens(B[0][:, :], C_GV, 512).then_inc(S["gv_gg_proj"], 1)
                    pe.wait_ge(S["lora_ready"], n)
                    mm(B[1][:, :], loraT[:, :], flat(wa2[:, :, :]), start=True, stop=False)
                    mm(B[1][:, :], ones[32:33, :], wa0[:, :], start=False, stop=True).then_inc(S["wa_proj"], 1)
                    pe.wait_ge(S["q_taken"], i)
                    for c in range(4):
                        last = channels(B[2][:, c * P:(c + 1) * P], c * P)
                    last.then_inc(S["q_proj"], 1)
                    pe.wait_ge(S["raw_taken"], n)
                    pe.wait_ge(S["bank3_taken"], n)
                    mm(B[3][:, 0:P], gk2[:, :], gk1T[:, :], start=True, stop=True).then_inc(S["gate_proj"], 1)
                    pe.wait_ge(S["mix_ready"], n)
                    for c in range(6):
                        bank, spot = (4, c) if c < 4 else (5, c - 4)
                        last = tr(B[bank][:, spot * P:(spot + 1) * P], mixT[:, c, :], ident[:, :])
                    last.then_inc(S["rkv_turned"], 1)
                    if tile.more:
                        pe.wait_ge(S["gg_taken"], n)
                        pe.wait_ge(S["wa_taken"], n)
                        turn_x(n + 1)
                    pe.wait_ge(S["dve_staged"], i)
                    tokens(B[7][:, :], C_AG, 512).then_inc(S["ag_proj"], 1)
                    tokens(B[6][:, 0:P], C_AV, P)
                    tokens(B[6][:, P:P + 256], C_RG, 256).then_inc(S["av_rg_proj"], 1)

            @block.scalar
            def _(act):
                ch = Chain(act, S["act_step"])
                f = nc.scalar.activation

                def norm_x(n, t):
                    act.wait_ge(S["x_loaded"], n * 16)
                    act.wait_ge(S["x_turned"], t)
                    f(xn[:, :], xt[:, :], ACT.Square, accum_out=stat[:, 0:1]).then_inc(S["x_squares"], 1)
                    act.wait_ge(S["x_rstd"], n)
                    f(xn[:, :], xt[:, :], ACT.Copy, scale=stat[:, 1:2]).then_inc(S["xn_ready"], 1)

                def take_h(n, hT):
                    act.wait_ge(S["x_turned"], n)
                    for k in range(4):
                        last = f(hT[:, k, 1:P + 1], B[0][:, k * P:(k + 1) * P], ACT.Identity, bias=shift_ch[:, k:k + 1], scale=scale_ch[:, k:k + 1])
                    last.then_inc(S["hT_act"], 1)

                norm_x(1, 0)
                act.wait_ge(S["setup_done"], 1)
                take_h(1, hTs[:, 0])
                for tile in tile_pairs(act):
                    n = tile.n
                    out = lambda a, b: st[:, tile.b, a:b]
                    act.wait_ge(S[f"stage_stored{tile.b}"], tile.turn * 16)
                    act.wait_ge(S["k_lora_proj"], n)
                    f(loraT[0:64, :], B[3][0:64, 3 * P:4 * P], ACT.Tanh)
                    f(loraT[64:128, :], B[3][64:128, 3 * P:4 * P], ACT.Copy).then_inc(S["lora_ready"], 1)
                    f(out(M_GQ, M_GK), B[3][:, P:2 * P], ACT.Copy, scale=G_KEY ** -0.5)
                    f(out(M_GK, M_GB), B[3][:, 2 * P:3 * P], ACT.Copy)
                    f(out(M_K, M_V), B[3][:, 0:P], ACT.Copy).then_inc(S["bank3_taken"], 1)
                    act.wait_ge(S["gv_gg_proj"], n)
                    f(out(M_GV, M_END), B[0][:, 0:256], ACT.Copy)
                    f(out(M_SG + 768, M_SG + 1024), B[0][:, 256:512], ACT.Sigmoid).then_inc(S["gg_sigmoid"], 1)
                    act.wait_ge(S["wa_proj"], n)
                    f(out(M_WA, M_GQ), B[1][:, :], ACT.Sigmoid).then_inc(S["wa_taken"], 1)
                    if tile.more:
                        norm_x(n + 1, n)
                    act.wait_ge(S["q_proj"], n)
                    f(out(M_Q, M_K), B[2][:, :], ACT.Copy).then_inc(S["q_taken"], 1)
                    act.wait_ge(S["rkv_turned"], n)
                    f(out(M_RKV, M_RKV + 512), B[4][:, :], ACT.Copy)
                    f(out(M_RKV + 512, M_WA), B[5][:, 0:256], ACT.Copy).then_inc(S["tok_taken"], 1)
                    if tile.more:
                        take_h(n + 1, hTs[:, 1 - tile.b])
                    act.wait_ge(S["gate_abs"], n)
                    ch.link(f(gz[:, 1, :], gz[:, 1, :], ACT.Exp, scale=-1.0))
                    f(gz[:, 1, :], gz[:, 1, :], ACT.Ln, bias=1.0).then_inc(S["gate_ln"], 1)
                    act.wait_ge(S["ag_proj"], n)
                    f(out(M_SG, M_SG + 512), B[7][:, :], ACT.Sigmoid).then_inc(S["ag_sigmoid"], 1)
                    act.wait_ge(S["av_rg_proj"], n)
                    f(out(M_V, M_SG), B[6][:, 0:P], ACT.Copy)
                    f(out(M_SG + 512, M_SG + 768), B[6][:, P:P + 256], ACT.Sigmoid).then_inc(S["act_staged"], 1)
                    ch.start_over()

            @block.vector
            def _(dve):
                ch = Chain(dve, S["dve_step"])
                v = nc.vector
                tt, ts, stt = v.tensor_tensor, v.tensor_scalar, v.scalar_tensor_tensor

                def take_h(n, hT):
                    dve.wait_ge(S["x_turned"], n)
                    for k in range(4, 8):
                        last = ts(hT[:, k, 1:P + 1], B[1][:, (k - 4) * P:(k - 3) * P], scale_ch[:, k:k + 1], shift_ch[:, k:k + 1], ALU.mult, ALU.add)
                    return last

                dve.wait_ge(S["setup_done"], 1)
                take_h(1, hTs[:, 0]).then_inc(S["hT_dve"], 1)
                for tile in tile_pairs(dve):
                    n = tile.n
                    out = lambda a, b: st[:, tile.b, a:b]
                    ch.link(v.tensor_copy(rkvT[:, :, 0:1], rkvT[:, :, P:P + 1]))
                    dve.wait_ge(S["rk_proj"], n)
                    v.tensor_copy(rkvT[:, 0:4, 1:P + 1], B[4][:, :].rearrange("p (a b) -> p a b", b=P))
                    dve.wait_ge(S["v_gk1_proj"], n)
                    v.tensor_copy(gk1T[:, :], B[5][0:16, 2 * P:3 * P])
                    v.tensor_copy(rkvT[:, 4:6, 1:P + 1], B[5][:, 0:2 * P].rearrange("p (a b) -> p a b", b=P)).then_inc(S["raw_taken"], 1)
                    dve.wait_ge(S["raw_taken"], n)
                    ch.link(tt(mixT[:, :, :], rkvT[:, :, 0:P], rkvT[:, :, 1:P + 1], ALU.subtract))
                    for c in range(6):
                        last = stt(mixT[:, c, :], mixT[:, c, :], mu_rkv[:, c:c + 1], rkvT[:, c, 1:P + 1], ALU.mult, ALU.add)
                    last.then_inc(S["mix_ready"], 1)
                    dve.wait_ge(S["gg_sigmoid"], n)
                    tt(out(M_SG + 768, M_SG + 1024), B[0][:, 256:512], out(M_SG + 768, M_SG + 1024), ALU.mult).then_inc(S["gg_taken"], 1)
                    dve.wait_ge(S["gate_proj"], n)
                    ts(gz[:, 0, :], B[3][:, 0:P], gkb[:, 0:1], None, ALU.add).then_inc(S["gate_biased"], 1)
                    dve.wait_ge(S["gate_biased"], n)
                    stt(gz[:, 1, :], gz[:, 0, :], -1.0, gz[:, 0, :], ALU.mult, ALU.max).then_inc(S["gate_abs"], 1)
                    ch.link(ts(gz[:, 0, :], gz[:, 0, :], 0.0, None, ALU.min))
                    if tile.more:
                        take_h(n + 1, hTs[:, 1 - tile.b])
                        dve.wait_ge(S["hT_act"], n)
                        v.tensor_copy(hTs[:, 1 - tile.b, :, 0:1], hTs[:, tile.b, :, P:P + 1]).then_inc(S["hT_dve"], 1)
                    dve.wait_ge(S["gate_ln"], n)
                    ch.link(tt(gz[:, 0, :], gz[:, 0, :], gz[:, 1, :], ALU.subtract))
                    ch.link(ts(gz[:, 0, :], gz[:, 0, :], 1.0 / 16.0, None, ALU.mult))
                    v.tensor_tensor_scan(out(M_GB, M_GV), ones[:, :], gz[:, 0, :], 0.0, ALU.mult, ALU.add)
                    dve.wait_ge(S["ag_sigmoid"], n)
                    tt(out(M_SG, M_SG + 512), B[7][:, :], out(M_SG, M_SG + 512), ALU.mult)
                    dve.wait_ge(S["act_staged"], n)
                    tt(out(M_SG + 512, M_SG + 768), B[6][:, P:P + 256], out(M_SG + 512, M_SG + 768), ALU.mult).then_inc(S["dve_staged"], 1)
                    ch.start_over()
        S.close()


def mixers(nc, A, stage1, mixed, const):
    ident = const["ident"]
    with ExitStack() as ctx:
        sb = lambda n, s: ctx.enter_context(nc.sbuf_tensor("b1_" + n, s, F32))
        S = Signals(nc, "b1")
        banks8 = ctx.enter_context(nc.psum_tensor("b1_banks", [P, 8, 512], F32))
        B = [banks8[:, i, :] for i in range(8)]
        rows = sb("rows", [P, 6, R_W])
        KK_, KA_, OMKA, RK_, LNW, LNB = range(6)
        gnorm, sinks = sb("gnorm", [P, G_VAL]), sb("sinks", [P, A_HEADS])
        masks = sb("masks", [P, LEVELS, P])
        tri = sb("tri", [P, 2, P])
        pair = sb("pair", [P, P])
        quad = sb("quad", [P, R_W])
        chunk_of = sb("chunk_of", [P, 2])
        alibi = sb("alibi", [P, A_HEADS, 2 * P])
        numbers = sb("numbers", [P, 6, 4])
        NEG_HALF, PER_D, PER_HEAD, EPS_X, EPS_GLA, EPS_RWKV = range(6)
        tile_in = sb("tile_in", [P, 2, M_END])
        ys = sb("y", [P, 2, D])
        kT = sb("kT", [P, 2, P])
        vt = sb("vt", [P, 2, P])
        s = sb("s", [P, A_HEADS, 2 * P])
        pT = sb("pT", [P, 4, 4, P])
        am, nm, den = sb("am", [P, A_HEADS]), sb("nm", [P, A_HEADS]), sb("den", [P, A_HEADS])
        lw = sb("lw", [P, R_W])
        ex = sb("ex", [P, 3, R_W])
        pends, bonuses = sb("pend", [P, 2, 4]), sb("bonus", [P, 2, 4])
        kk, kka, kn, pr = sb("kk", [P, R_W]), sb("kka", [P, R_W]), sb("kn", [P, R_W]), sb("pr", [P, R_W])
        hk = sb("hk", [P, 2, 4])
        t1, t2, t3 = sb("t1", [P, R_W]), sb("t2", [P, R_W]), sb("t3", [P, R_W])
        h4 = sb("h4", [P, 4, 4])
        X4s = sb("X4", [P, 2, 4, R_W])
        X4T = sb("X4T", [P, 4, 2, P])
        GB, GK = sb("GB", [P, 4, 2, P]), sb("GK", [P, 4, 2, P])
        cT = sb("cT", [P, 2, 4, P])
        XY = sb("XY", [P, 2, 2, 2, P])
        X, Y = (lambda h: XY[:, h // 2, 0, h % 2, :]), (lambda h: XY[:, h // 2, 1, h % 2, :])
        Zs = sb("Zs", [P, 2, 2, P])
        Z_BANK, XY_BANK = (B[0], B[3]), (B[1], B[2])
        akv, U = sb("akv", [P, R_W]), sb("U", [P, R_W])
        WT = sb("WT", [P, 2, P])
        SA, M = sb("SA", [P, R_W]), sb("M", [P, 2, P])
        yR = sb("yR", [P, R_W])
        ge = sb("ge", [P, LEVELS, P])
        gql, gkl = sb("gql", [P, LEVELS * P]), sb("gkl", [P, LEVELS * P])
        geb = sb("geb", [P, 3, P])
        gA, gS = sb("gA", [P, 4, P]), sb("gS", [P, R_W])
        ke_tok, g1, g4 = sb("ke_tok", [P, P]), sb("g1", [P, R_W]), sb("g4", [P, 4, 4])

        def s3(ap):
            return ap.rearrange("p (l t) -> p l t", t=P)

        class Staged:

            def __init__(self, b):
                part = lambda a, e: tile_in[:, b, a:e]
                self.qT = part(M_Q, M_K).rearrange("p (c t) -> p c t", t=P)
                self.k, self.v = part(M_K, M_V), part(M_V, M_SG)
                self.sg = part(M_SG, M_RKV)
                self.tok = part(M_RKV, M_WA).rearrange("p (e c) -> p e c", c=R_W)
                self.wa = part(M_WA, M_GQ).rearrange("p (e c) -> p e c", c=R_W)
                self.gqT, self.gkT, self.gb, self.gv = part(M_GQ, M_GK), part(M_GK, M_GB), part(M_GB, M_GV), part(M_GV, M_END)

        SAG, SRG, SGG = 0, 512, 768
        SCORES_FIRST = 4

        with nc.Block() as block:
            @block.sync
            def _(sp):
                load = lambda dst, src: sp.dma_start(dst, src).then_inc(S["weights_loaded"], 16)
                fetch = lambda t, b: sp.dma_start(tile_in[:, b, :], stage1[bass.ds(t * P, P), :]).then_inc(S[f"tile_loaded{b}"], 16)
                store = lambda t, b: sp.dma_start(mixed[bass.ds(t * P, P), :], ys[:, b, :]).then_inc(S[f"y_stored{b}"], 16)
                fetch(0, 0)
                for n, name in ((KK_, "rwkv_k_k"), (KA_, "rwkv_k_a"), (LNW, "rwkv_ln_w"), (LNB, "rwkv_ln_b")):
                    load(rows[:, n, :], row(A[name][0:1, :]))
                load(rows[:, RK_, :], row(A["rwkv_r_k"].rearrange("a h d -> a (h d)")))
                load(gnorm[:, :], row(A["gla_norm_w"][0:1, :]))
                load(sinks[:, :], row(A["attn_sinks"][0:1, :]))
                load(masks[:, :, :], A["k_masks"])
                load(tri[:, :, :], A["k_tri"])
                load(pair[:, :], A["k_pair"])
                load(quad[:, :], A["k_quad"])
                load(chunk_of[:, :], A["k_chunk_of"])
                load(alibi[:, :, P:], A["k_alibi"][:, :, P:])
                fetch(1, 1)
                sp.wait_ge(S["scores_done"], 1)
                sp.dma_start(alibi[:, :, 0:P], A["k_alibi"][:, :, 0:P]).then_inc(S["alibi_ready"], 16)
                with sp.Fori(0, TILES // 2 - 1) as i:
                    for b in range(2):
                        sp.wait_ge(S["y_ready"], 2 * i + (b + 1))
                        fetch(2 * i + (b + 2), b)
                        store(2 * i + b, b)
                for b in range(2):
                    sp.wait_ge(S["y_ready"], TILES - 1 + b)
                    store(TILES - 2 + b, b)
                for b in range(2):
                    sp.wait_ge(S[f"y_stored{b}"], 16 * TILES // 2)

            N_WEIGHTS = 16 * (4 + 3 + 6)

            @block.gpsimd
            def _(pool):
                ch = Chain(pool, S["pool_step"])
                for at, value in enumerate((-0.5, 1.0 / D, 1.0 / HEAD, EPS, 1e-5, RWKV_LN_EPS)):
                    nc.gpsimd.memset(numbers[:, at, :], value)
                nc.gpsimd.memset(alibi[:, :, 0:P], NEG)
                nc.gpsimd.memset(kT[:, :, :], 0.0)
                nc.gpsimd.memset(vt[:, :, :], 0.0)
                nc.gpsimd.memset(M[:, :, :], 0.0)
                nc.gpsimd.memset(gS[:, :], 0.0)
                ch.link(nc.gpsimd.memset(pends[:, :, :], 0.0))
                pool.wait_ge(S["weights_loaded"], N_WEIGHTS)
                nc.gpsimd.tensor_scalar(rows[:, OMKA, :], rows[:, KA_, :], -1.0, 1.0, ALU.mult, ALU.add).then_inc(S["setup_done"], 1)
                ch.start_over()

                def inv_sqrt(out, sums, n, per, eps):
                    ch.link(nc.gpsimd.tensor_tensor(sums, sums, numbers[:, per, 0:n], ALU.mult))
                    ch.link(nc.gpsimd.tensor_tensor(sums, sums, numbers[:, eps, 0:n], ALU.add))
                    return nc.gpsimd.tensor_tensor(out, sums, numbers[:, NEG_HALF, 0:n], ALU.pow)

                def kk_length(n):
                    pool.wait_ge(S["kk_squares"], n)
                    nc.gpsimd.tensor_tensor(hk[:, 1, :], hk[:, 0, :], numbers[:, NEG_HALF, :], ALU.pow).then_inc(S["kk_rnorm"], 1)

                kk_length(1)
                for tile in tile_pairs(pool):
                    n = tile.n
                    pool.wait_ge(S["gla_squares"], n)
                    inv_sqrt(g4[:, 1, :], g4[:, 0, :], 4, PER_HEAD, EPS_GLA).then_inc(S["gla_rstd"], 1)
                    if tile.more:
                        kk_length(n + 1)
                    pool.wait_ge(S["rwkv_squares"], n)
                    inv_sqrt(h4[:, 3, :], h4[:, 2, :], 4, PER_HEAD, EPS_RWKV).then_inc(S["rwkv_rstd"], 1)
                    ch.start_over()

            @block.tensor
            def _(pe):
                pe.wait_ge(S["setup_done"], 1)
                mm, tr = nc.tensor.matmul, nc.tensor.transpose

                def running_sums(n):
                    pe.wait_ge(S["lw_ready"], n)
                    mm(B[6][:, 0:R_W], tri[:, 1, :], lw[:, :], start=True, stop=True)
                    for p in range(2):
                        last = mm(B[6][:, R_W + 2 * p:R_W + 2 * p + 2], lw[:, p * P:(p + 1) * P], chunk_of[:, :], start=True, stop=True)
                    last.then_inc(S["cum_done"], 1)

                running_sums(1)
                for tile in tile_pairs(pe):
                    i, n, T, X4 = tile.t, tile.n, Staged(tile.b), X4s[:, tile.b]

                    def Z_products(l):
                        pe.wait_ge(S["cT_ready"], i * INV_LEVELS + (l + 1))
                        for half in range(2):
                            if l > 0:
                                pe.wait_ge(S[f"XY_ready{half}"], i * INV_LEVELS + l)
                            elif half == 1:
                                pe.wait_ge(S["GK_ready"], n)
                            for h in range(2 * half, 2 * half + 2):
                                last = mm(Z_BANK[half][:, (h % 2) * P:(h % 2 + 1) * P], cT[:, l % 2, h, :],
                                          ident[:, :] if l == 0 else X(h), start=True, stop=True)
                            last.then_inc(S[f"Z_done{half}"], 1)

                    def XY_products(l):
                        for half in range(2):
                            pe.wait_ge(S[f"Z_taken{half}"], i * (INV_LEVELS - 1) + l)
                            for h in range(2 * half, 2 * half + 2):
                                last = mm(XY_BANK[half][:, (2 + h % 2) * P:(3 + h % 2) * P], Zs[:, half, h % 2, :], Y(h), start=True, stop=True)
                            if l < INV_LEVELS - 1:
                                for h in range(2 * half, 2 * half + 2):
                                    last = mm(XY_BANK[half][:, (h % 2) * P:(h % 2 + 1) * P], Y(h), Zs[:, half, h % 2, :], start=True, stop=True)
                            last.then_inc(S[f"XY_done{half}"], 1)

                    def gla_levels(first, last_one):
                        for l in range(first, last_one + 1):
                            for h in range(4):
                                r = slice(32 * h, 32 * h + 32)
                                a, b = (T.gkT[r, :], T.gqT[r, :]) if l == 0 else (s3(gkl[r, :])[:, l - 1, :], s3(gql[r, :])[:, l - 1, :])
                                last = mm(B[4 + h][:, (l % 4) * P:(l % 4 + 1) * P], a, b, start=True, stop=True)
                        if last_one % 4 == 3:
                            last.then_inc(S[f"gla_round{last_one // 4}"], 1)

                    pe.wait_ge(S["X4_ready"], n)
                    pe.wait_ge(S["rwkv_taken"], i)
                    for c in range(8):
                        last = tr(B[2 + c // 4][:, (c % 4) * P:(c % 4 + 1) * P], X4[:, c // 2, (c % 2) * P:(c % 2 + 1) * P], ident[:, :])
                    last.then_inc(S["X4_turned"], 1)
                    pe.wait_ge(S["X4T_ready"], n)
                    for what, banks, name in ((2, (0, 1), "gram_b"), (3, (2, 3), "gram_k")):
                        for h in range(4):
                            r, p = slice(64 * (h % 2), 64 * (h % 2) + 64), h // 2
                            last = mm(B[banks[h % 2]][:, p * 256:p * 256 + 256], X4T[r, what, p, :],
                                      X4T[r, 0:2, p, :], start=True, stop=True)
                        last.then_inc(S[name], 1)
                    pe.wait_ge(S["kept"], n)
                    pe.wait_ge(S["cum_taken"], n)
                    for h in range(A_HEADS):
                        g = h // 4
                        last = mm(B[4 + h // 2][:, (h % 2) * 256:(h % 2) * 256 + 256], T.qT[64 * g:64 * g + 64, h % 4, :],
                                  kT[64 * g:64 * g + 64, :, :].rearrange("p a b -> p (a b)"), start=True, stop=True)
                        if h % 2:
                            last.then_inc(S[f"scores{h // 2}"], 1)
                        if h == SCORES_FIRST - 1:
                            Z_products(0)
                    Z_products(1)
                    XY_products(1)
                    Z_products(2)
                    XY_products(2)
                    for j in range(4):
                        if j == 2:
                            Z_products(3)
                        pe.wait_ge(S[f"probs{j}"], n)
                        for e in range(4):
                            last = tr(B[4 + j][:, e * P:(e + 1) * P], s[:, 2 * j + e // 2, (e % 2) * P:(e % 2 + 1) * P], ident[:, :])
                        last.then_inc(S[f"probs_turned{j}"], 1)
                    XY_products(3)
                    Z_products(4)
                    pe.wait_ge(S["pT_dve"], n)
                    pe.wait_ge(S["pT_act"], n)
                    for h in range(A_HEADS):
                        for half in range(2):
                            last = mm(B[4][:, h * 64:(h + 1) * 64], pT[:, h // 2, (h % 2) * 2 + half, :],
                                      vt[:, half, 64 * (h // 4):64 * (h // 4) + 64], start=(half == 0), stop=(half == 1))
                    last.then_inc(S["attended"], 1)
                    pe.wait_ge(S["gla_scaled"], n)
                    tr(B[5][:, 0:P], geb[:, 2, :], ident[:, :]).then_inc(S["ke_turned"], 1)
                    XY_products(4)
                    pe.wait_ge(S["attn_out"], n)
                    pe.wait_ge(S["ke_ready"], n)
                    gla_levels(0, 1)
                    Z_products(5)
                    gla_levels(2, 3)
                    XY_products(5)
                    for h in range(4):
                        last = mm(B[3][:, h * 64:(h + 1) * 64], GK[:, h, 0, :], T.tok[:, 2, h * 64:(h + 1) * 64], start=True, stop=True)
                    last.then_inc(S["akv_done"], 1)
                    for half in range(2):
                        pe.wait_ge(S[f"XY_ready{half}"], i * INV_LEVELS + INV_LEVELS)
                    for h in range(4):
                        last = mm(B[1][64 * (h % 2):64 * (h % 2) + 64, (h // 2) * P:(h // 2 + 1) * P], X4[:, 0, h * 64:(h + 1) * 64], Y(h), start=True, stop=True)
                    last.then_inc(S["WT_done"], 1)
                    pe.wait_ge(S["akv_ready"], n)
                    for h in range(4):
                        last = mm(B[0][:, h * 64:(h + 1) * 64], Y(h), akv[:, h * 64:(h + 1) * 64], start=True, stop=True)
                    last.then_inc(S["U_done"], 1)
                    pe.wait_ge(S["gla_levels_used"], n)
                    gla_levels(4, 7)

                    def state_products(c):
                        r = slice(64 * c, 64 * c + 64)
                        for p in range(2):
                            mm(B[2][r, p * P:(p + 1) * P], WT[:, p, r], M[:, p, :], start=True, stop=True)
                        for p in range(2):
                            last = mm(B[1][r, 256 + p * P:256 + (p + 1) * P], X4T[:, 1, p, r], M[:, p, :], start=True, stop=True)
                        last.then_inc(S[f"sa_done{c}"], 1)

                    def state_addition(c):
                        r = slice(64 * c, 64 * c + 64)
                        pe.wait_ge(S[f"sa_ready{c}"], n)
                        for p in range(2):
                            mm(B[3][:, 256 + p * P:256 + (p + 1) * P], X4[r, 2, p * P:(p + 1) * P], SA[r, p * P:(p + 1) * P], start=True, stop=False)
                            last = mm(B[3][:, 256 + p * P:256 + (p + 1) * P], X4[r, 3, p * P:(p + 1) * P], T.tok[r, 2, p * P:(p + 1) * P], start=False, stop=True)
                        last.then_inc(S[f"dM_done{c}"], 1)

                    pe.wait_ge(S["WT_ready"], n)
                    state_products(0)
                    state_addition(0)
                    pe.wait_ge(S["gA_ready"], n)
                    if tile.more:
                        running_sums(n + 1)
                    for h in range(4):
                        c = slice(h * 64, (h + 1) * 64)
                        mm(B[4][:, c], geb[:, 1, :], gS[:, c], start=True, stop=False)
                        mm(B[4][:, c], gA[:, h, :], T.gv[:, c], start=False, stop=True)
                    mm(B[5][:, 256:512], ke_tok[:, :], T.gv[:, :], start=True, stop=True).then_inc(S["gla_out"], 1)
                    pe.wait_ge(S["M_ready0"], n)
                    state_products(1)
                    state_addition(1)
                    for h in range(4):
                        c = slice(h * 64, (h + 1) * 64)
                        mm(B[0][:, 256 + h * 64:256 + (h + 1) * 64], GB[:, h, 1, :], SA[:, c], start=True, stop=False)
                        last = mm(B[0][:, 256 + h * 64:256 + (h + 1) * 64], GK[:, h, 1, :], T.tok[:, 2, c], start=False, stop=True)
                    last.then_inc(S["rwkv_out"], 1)

            @block.scalar
            def _(act):
                f = nc.scalar.activation

                def decays(n, b):
                    act.wait_ge(S["cum_less"], n)
                    f(ex[:, 1, :], B[6][:, 0:R_W], ACT.Exp)
                    f(ex[:, 2, :], B[6][:, 0:R_W], ACT.Exp, scale=-1.0)
                    f(pends[:, b, :], B[6][:, R_W:R_W + 4], ACT.Exp).then_inc(S["cum_taken"], 1)
                    f(ex[:, 0, :], ex[:, 0, :], ACT.Exp).then_inc(S["ex_ready"], 1)

                decays(1, 0)
                for tile in tile_pairs(act):
                    i, n, T = tile.t, tile.n, Staged(tile.b)

                    def Z_copy(l):
                        for half in range(2):
                            act.wait_ge(S[f"Z_done{half}"], i * INV_LEVELS + (l + 1))
                            f(Zs[:, half, :, :].rearrange("p a b -> p (a b)"), Z_BANK[half][:, 0:2 * P], ACT.Copy).then_inc(S[f"Z_taken{half}"], 1)

                    act.wait_ge(S["X4_turned"], n)
                    f(X4T[:, 0:2, :, :].rearrange("p a b c -> p (a b c)"), B[2][:, :], ACT.Copy)
                    f(X4T[:, 2:4, :, :].rearrange("p a b c -> p (a b c)"), B[3][:, :], ACT.Copy).then_inc(S["X4T_ready"], 1)
                    Z_copy(1)
                    act.wait_ge(S["levels_ready"], n)
                    f(ge[:, :, :], ge[:, :, :], ACT.Exp)
                    f(geb[:, 1, :], T.gb, ACT.Exp)
                    f(geb[:, 2, :], T.gb, ACT.Exp, scale=-1.0, bias=T.gb[:, P - 1:P]).then_inc(S["levels_exp"], 1)
                    Z_copy(2)
                    act.wait_ge(S["max_ready"], n)
                    for h in range(A_HEADS):
                        last = f(s[:, h, :], s[:, h, :], ACT.Exp, bias=nm[:, h:h + 1], accum_out=den[:, h:h + 1])
                        if h % 2:
                            last.then_inc(S[f"probs{h // 2}"], 1)
                    f(am[:, :], am[:, :], ACT.Exp).then_inc(S["sink_exp"], 1)
                    Z_copy(3)
                    for j in (0, 2):
                        act.wait_ge(S[f"probs_turned{j}"], n)
                        last = f(pT[:, j, :, :].rearrange("p a b -> p (a b)"), B[4 + j][:, :], ACT.Copy)
                    last.then_inc(S["pT_act"], 1)
                    Z_copy(4)
                    act.wait_ge(S["ke_turned"], n)
                    f(ke_tok[:, :], B[5][:, 0:P], ACT.Copy).then_inc(S["ke_ready"], 1)
                    Z_copy(5)
                    act.wait_ge(S["akv_done"], n)
                    f(akv[:, :], B[3][:, 0:R_W], ACT.Copy).then_inc(S["akv_ready"], 1)
                    act.wait_ge(S["WT_done"], n)
                    f(WT[:, :, :].rearrange("p a b -> p (a b)"), B[1][:, 0:R_W], ACT.Copy)
                    act.wait_ge(S["U_done"], n)
                    f(U[:, :], B[0][:, 0:R_W], ACT.Copy).then_inc(S["WT_ready"], 1)
                    act.wait_ge(S["sa_done0"], n)
                    f(yR[0:64, :], B[1][0:64, 256:512], ACT.Copy)
                    if tile.more:
                        decays(n + 1, 1 - tile.b)
                    act.wait_ge(S["sa_done1"], n)
                    f(yR[64:128, :], B[1][64:128, 256:512], ACT.Copy).then_inc(S["yR_ready"], 1)

            @block.vector
            def _(dve):
                ch = Chain(dve, S["dve_step"])
                v = nc.vector
                tt, ts, stt = v.tensor_tensor, v.tensor_scalar, v.scalar_tensor_tensor
                idn = ident[:, :].unsqueeze(1)

                def heads(ap, d=HEAD):
                    return ap.rearrange("p (h d) -> p h d", d=d)

                def log_decay(N):
                    ts(lw[:, :], N.wa[:, 0, :], -float(np.exp(-0.5)), None, ALU.mult).then_inc(S["lw_ready"], 1)

                def keep_k_v(N):
                    ch.link(v.tensor_copy(kT[:, 0, :], kT[:, 1, :]))
                    ch.link(v.tensor_copy(vt[:, 0, :], vt[:, 1, :]))
                    v.tensor_copy(kT[:, 1, :], N.k)
                    v.tensor_copy(vt[:, 1, :], N.v).then_inc(S["kept"], 1)

                def sums_less(n):
                    dve.wait_ge(S["cum_done"], n)
                    dve.wait_ge(S["lw_ready"], n)
                    tt(ex[:, 0, :], B[6][:, 0:R_W], lw[:, :], ALU.subtract).then_inc(S["cum_less"], 1)

                def kk_squares(N):
                    ch.link(tt(kk[:, :], N.tok[:, 1, :], rows[:, KK_, :], ALU.mult))
                    ch.link(tt(pr[:, :], kk[:, :], kk[:, :], ALU.mult))
                    ch.link(v.tensor_reduce(hk[:, 0, :], heads(pr[:, :]), AX.X, ALU.add))
                    ts(hk[:, 0, :], hk[:, 0, :], 1e-24, None, ALU.max).then_inc(S["kk_squares"], 1)

                def key_and_bonus(N, b):
                    ch.link(tt(kn[:, :], N.wa[:, 1, :], rows[:, KA_, :], ALU.mult))
                    ch.link(tt(kn[:, :], kn[:, :], rows[:, OMKA, :], ALU.add))
                    ch.link(tt(kn[:, :], kn[:, :], N.tok[:, 1, :], ALU.mult))
                    ch.link(tt(pr[:, :], N.tok[:, 0, :], kn[:, :], ALU.mult))
                    ch.link(tt(pr[:, :], pr[:, :], rows[:, RK_, :], ALU.mult))
                    ch.link(v.tensor_reduce(bonuses[:, b, :], heads(pr[:, :]), AX.X, ALU.add))

                def scaled_vectors(N, n, b):
                    dve.wait_ge(S["kk_rnorm"], n)
                    ch.link(tt(heads(kk[:, :]), heads(kk[:, :]), spread(hk[:, 1, :].unsqueeze(2), [P, 4, HEAD]), ALU.mult))
                    ch.link(tt(kka[:, :], kk[:, :], N.wa[:, 1, :], ALU.mult))
                    dve.wait_ge(S["ex_ready"], n)
                    tt(X4s[:, b, 0, :], kk[:, :], ex[:, 0, :], ALU.mult)
                    tt(X4s[:, b, 1, :], N.tok[:, 0, :], ex[:, 1, :], ALU.mult)
                    tt(X4s[:, b, 2, :], kka[:, :], ex[:, 2, :], ALU.mult)
                    tt(X4s[:, b, 3, :], kn[:, :], ex[:, 2, :], ALU.mult).then_inc(S["X4_ready"], 1)

                dve.wait_ge(S["setup_done"], 1)
                ch.link(v.memset(am[:, :], 0.0))
                dve.wait_ge(S["tile_loaded0"], 16)
                first = Staged(0)
                log_decay(first)
                keep_k_v(first)
                sums_less(1)
                kk_squares(first)
                key_and_bonus(first, 0)
                scaled_vectors(first, 1, 0)
                ch.start_over()
                for tile in tile_pairs(dve):
                    i, n, y, T, N = tile.t, tile.n, ys[:, tile.b], Staged(tile.b), Staged(1 - tile.b)
                    at = i * INV_LEVELS

                    def lower(l):
                        tt(cT[:, l % 2, :, :], GB[:, :, 0, :], spread(masks[:, l, :].unsqueeze(1), [P, 4, P]), ALU.mult).then_inc(S["cT_ready"], 1)

                    def join(l):
                        for half in range(2):
                            dve.wait_ge(S[f"XY_done{half}"], i * (INV_LEVELS - 1) + l)
                            dve.wait_ge(S[f"XY_ready{half}"], at + l)
                            if l < INV_LEVELS - 1:
                                mine = XY[:, half, :, :, :].rearrange("p a b c -> p (a b c)")
                                tt(mine, mine, XY_BANK[half][:, :], ALU.subtract).then_inc(S[f"XY_ready{half}"], 1)
                            else:
                                mine = XY[:, half, 1, :, :].rearrange("p a b -> p (a b)")
                                tt(mine, mine, XY_BANK[half][:, 2 * P:4 * P], ALU.subtract).then_inc(S[f"XY_ready{half}"], 1)

                    def gla_level(l):
                        src = banks8[:, 4:8, (l % 4) * P:(l % 4 + 1) * P]
                        if l == 0:
                            return tt(gA[:, :, :], src, spread(idn, [P, 4, P]), ALU.mult)
                        return v.copy_predicated(gA[:, :, :], spread(masks[:, l - 1, :].bitcast(U32).unsqueeze(1), [P, 4, P]), src)

                    for name, banks, dst in (("gram_b", (0, 1), GB), ("gram_k", (2, 3), GK)):
                        dve.wait_ge(S[name], n)
                        for j in range(2):
                            last = tt(dst[:, :, :, :].rearrange("p (q j) a b -> p j q (a b)", j=2)[:, j],
                                      B[banks[j]][:, :].rearrange("p (h a) -> p h a", h=2),
                                      spread(tri[:, :, :].rearrange("p a b -> p (a b)").unsqueeze(1), [P, 2, 2 * P]), ALU.mult)
                        if name == "gram_b":
                            ch.link(last)
                            lower(0)
                        else:
                            last.then_inc(S["GK_ready"], 1)
                    lower(1)
                    dve.wait_ge(S["cT_ready"], at + 1)
                    for half in range(2):
                        last = tt(XY[:, half, 1, :, :], spread(idn, [P, 2, P]), cT[:, 0, 2 * half:2 * half + 2, :], ALU.subtract)
                    ch.link(last)
                    for half in range(2):
                        dve.wait_ge(S[f"Z_done{half}"], at + 1)
                        tt(XY[:, half, 0, :, :], spread(idn, [P, 2, P]), Z_BANK[half][:, 0:2 * P].rearrange("p (h t) -> p h t", t=P), ALU.subtract).then_inc(S[f"XY_ready{half}"], 1)
                    for l in range(LEVELS):
                        half = 1 << l
                        blocks = lambda ap: ap.rearrange("p (m w) -> p m w", w=2 * half)
                        mid = spread(blocks(T.gb)[:, :, half - 1:half], [P, P // (2 * half), 2 * half])
                        last = tt(blocks(ge[:, l, :]), blocks(T.gb), mid, ALU.subtract)
                    ch.link(last)
                    stt(ge[:, :, :], ge[:, :, :], -1.0, ge[:, :, :], ALU.mult, ALU.min).then_inc(S["levels_ready"], 1)
                    lower(2)
                    join(1)
                    for j in range(4):
                        dve.wait_ge(S[f"scores{j}"], n)
                        last = stt(s[:, 2 * j:2 * j + 2, :].rearrange("p a b -> p (a b)"), B[4 + j][:, :], HEAD ** -0.5,
                                   alibi[:, 2 * j:2 * j + 2, :].rearrange("p a b -> p (a b)"), ALU.mult, ALU.add)
                    last.then_inc(S["scores_done"], 1)
                    dve.wait_ge(S["scores_done"], n)
                    ch.link(v.tensor_reduce(am[:, :], s[:, :, :], AX.X, ALU.max))
                    ch.link(tt(am[:, :], am[:, :], sinks[:, :], ALU.max))
                    ch.link(ts(nm[:, :], am[:, :], -1.0, None, ALU.mult))
                    tt(am[:, :], sinks[:, :], nm[:, :], ALU.add).then_inc(S["max_ready"], 1)
                    lower(3)
                    join(2)
                    dve.wait_ge(S["levels_exp"], n)
                    tt(s3(gql[:, :]), ge[:, :, :], spread(T.gqT.unsqueeze(1), [P, LEVELS, P]), ALU.mult)
                    tt(s3(gkl[:, :]), ge[:, :, :], spread(T.gkT.unsqueeze(1), [P, LEVELS, P]), ALU.mult)
                    v.tensor_copy(g4[:, 3, 0:1], geb[:, 1, P - 1:P])
                    ch.link(tt(geb[:, 2, :], geb[:, 2, :], T.gkT, ALU.mult))
                    tt(geb[:, 1, :], geb[:, 1, :], T.gqT, ALU.mult).then_inc(S["gla_scaled"], 1)
                    lower(4)
                    join(3)
                    for j in (1, 3):
                        dve.wait_ge(S[f"probs_turned{j}"], n)
                        last = v.tensor_copy(pT[:, j, :, :].rearrange("p a b -> p (a b)"), B[4 + j][:, :])
                    last.then_inc(S["pT_dve"], 1)
                    dve.wait_ge(S["sink_exp"], n)
                    ch.link(tt(den[:, :], den[:, :], am[:, :], ALU.add))
                    ch.link(v.reciprocal(den[:, :], den[:, :]))
                    lower(5)
                    join(4)
                    dve.wait_ge(S["attended"], n)
                    dve.wait_ge(S[f"y_stored{tile.b}"], tile.turn * 16)
                    tt(heads(y[:, 0:512]), heads(B[4][:, :]), spread(den[:, :].unsqueeze(2), [P, A_HEADS, HEAD]), ALU.mult).then_inc(S["attn_out"], 1)
                    dve.wait_ge(S["attn_out"], n)
                    ch.link(tt(y[:, 0:512], y[:, 0:512], T.sg[:, 0:512], ALU.mult))
                    if tile.more:
                        dve.wait_ge(S[f"tile_loaded{1 - tile.b}"], (tile.turn + tile.b) * 16 + 16)
                        log_decay(N)
                        keep_k_v(N)
                    join(5)
                    dve.wait_ge(S["gla_round0"], n)
                    for l in range(4):
                        last = gla_level(l)
                        if l < 3:
                            ch.link(last)
                    last.then_inc(S["gla_levels_used"], 1)
                    dve.wait_ge(S["gla_levels_used"], n)
                    if tile.more:
                        kk_squares(N)
                        key_and_bonus(N, 1 - tile.b)
                    dve.wait_ge(S["WT_ready"], n)

                    def sa(c):
                        r = slice(64 * c, 64 * c + 64)
                        dve.wait_ge(S[f"sa_done{c}"], n)
                        stt(SA[r, :], B[2][r, 0:R_W], -1.0, U[r, :], ALU.mult, ALU.subtract).then_inc(S[f"sa_ready{c}"], 1)

                    def next_state(c):
                        dve.wait_ge(S[f"dM_done{c}"], n)
                        dM = t1[:, :].rearrange("p (a b) -> p a b", b=P)
                        ch.link(tt(dM, B[3][:, 256:512].rearrange("p (a b) -> p a b", b=P), spread(pair[:, :].unsqueeze(1), [P, 2, P]), ALU.mult))
                        ch.link(tt(M[:, :, :], M[:, :, :], dM, ALU.add))
                        ts(M[:, 0, :], M[:, 0, :], pends[:, tile.b, c:c + 1], None, ALU.mult)
                        ts(M[:, 1, :], M[:, 1, :], pends[:, tile.b, 2 + c:3 + c], None, ALU.mult).then_inc(S[f"M_ready{c}"], 1)

                    sa(0)
                    dve.wait_ge(S["gla_round1"], n)
                    dve.sem_inc(S["round_seen"], 1)
                    for l in range(4, 8):
                        last = gla_level(l)
                        if l < 7:
                            ch.link(last)
                    last.then_inc(S["gA_ready"], 1)
                    next_state(0)
                    if tile.more:
                        sums_less(n + 1)
                    dve.wait_ge(S["gla_out"], n)
                    ch.link(tt(g1[:, :], B[5][:, 256:512], quad[:, :], ALU.mult))
                    ch.link(stt(gS[:, :], gS[:, :], g4[:, 3, 0:1], g1[:, :], ALU.mult, ALU.add))
                    sa(1)
                    ch.link(v.tensor_copy(y[:, 768:1024], B[4][:, 0:R_W]))
                    ch.link(tt(g1[:, :], y[:, 768:1024], y[:, 768:1024], ALU.mult))
                    v.tensor_reduce(g4[:, 0, :], heads(g1[:, :]), AX.X, ALU.add).then_inc(S["gla_squares"], 1)
                    next_state(1)
                    if tile.more:
                        scaled_vectors(N, n + 1, 1 - tile.b)
                    dve.wait_ge(S["yR_ready"], n)
                    dve.wait_ge(S["rwkv_out"], n)
                    yr = heads(t1[:, :])
                    dve.wait_ge(S["M_ready1"], n)
                    tt(t1[:, :], B[0][:, 256:512], yR[:, :], ALU.add).then_inc(S["rwkv_taken"], 1)
                    dve.wait_ge(S["rwkv_taken"], n)
                    ch.link(v.tensor_reduce(h4[:, 0, :], yr, AX.X, ALU.add))
                    ch.link(ts(h4[:, 0, :], h4[:, 0, :], 1.0 / HEAD, None, ALU.mult))
                    ch.link(tt(yr, yr, spread(h4[:, 0, :].unsqueeze(2), [P, 4, HEAD]), ALU.subtract))
                    ch.link(tt(t2[:, :], t1[:, :], t1[:, :], ALU.mult))
                    v.tensor_reduce(h4[:, 2, :], heads(t2[:, :]), AX.X, ALU.add).then_inc(S["rwkv_squares"], 1)
                    ch.link(tt(heads(t3[:, :]), heads(T.tok[:, 2, :]), spread(bonuses[:, tile.b, :].unsqueeze(2), [P, 4, HEAD]), ALU.mult))
                    dve.wait_ge(S["gla_rstd"], n)
                    yg = heads(y[:, 768:1024])
                    ch.link(tt(yg, yg, spread(g4[:, 1, :].unsqueeze(2), [P, 4, HEAD]), ALU.mult))
                    ch.link(tt(yg, yg, spread(gnorm[:, :].unsqueeze(1), [P, 4, HEAD]), ALU.mult))
                    ch.link(tt(y[:, 768:1024], y[:, 768:1024], T.sg[:, SGG:SGG + 256], ALU.mult))
                    dve.wait_ge(S["rwkv_rstd"], n)
                    ch.link(tt(yr, yr, spread(h4[:, 3, :].unsqueeze(2), [P, 4, HEAD]), ALU.mult))
                    ch.link(tt(t1[:, :], t1[:, :], rows[:, LNW, :], ALU.mult))
                    ch.link(tt(t1[:, :], t1[:, :], rows[:, LNB, :], ALU.add))
                    ch.link(tt(t1[:, :], t1[:, :], t3[:, :], ALU.add))
                    dve.wait_ge(S["alibi_ready"], 16)
                    tt(y[:, 512:768], t1[:, :], T.sg[:, SRG:SRG + 256], ALU.mult).then_inc(S["y_ready"], 1)
                    ch.start_over()
        S.close()


def output_and_residual(nc, A, mixed, x1, w_in_2, w_in_2_loaded, keep, const):
    ident = const["ident"]
    with ExitStack() as ctx:
        sb = lambda n, s: ctx.enter_context(nc.sbuf_tensor("o1_" + n, s, F32))
        S = Signals(nc, "o1")
        B = [ctx.enter_context(nc.psum_tensor(f"o1_bank{i}", [P, 512], F32)) for i in range(8)]
        w, gate_row = sb("w", [P, KD, D]), sb("gate_row", [P, D])
        y, x, r = sb("y", [P, 2, D]), sb("x", [P, 2, D]), sb("r", [P, 2, D])
        yT = w_in_2[:, KD - 1, 0:2 * D].rearrange("p (b k t) -> p b k t", b=2, t=P)
        sq = w_in_2[:, KD - 1, 2 * D:2 * D + 512]
        st, neg_half = sb("st", [P, 2, 4]), sb("neg_half", [P, 1])
        PAIRS = TILES // 2
        assert PAIRS == KD

        with nc.Block() as block:
            @block.sync
            def _(sp):
                src = A["w_out"][0].rearrange("(k p) n -> p k n", p=P)
                for k in range(KD):
                    sp.dma_start(w[:, k, :], src[:, k, :]).then_inc(S["w_loaded"], 16)
                sp.dma_start(gate_row[:, :], keep["gate_row"]).then_inc(S["gate_loaded"], 16)
                src = A["w_in_2"][0].rearrange("(k p) n -> p k n", p=P)

                def fetch(i):
                    for b in range(2):
                        sp.wait_ge(S[f"y_turned{b}"], i)
                        sp.dma_start(y[:, b, :], mixed[bass.ds((2 * i + b) * P, P), :]).then_inc(S[f"y_loaded{b}"], 16)
                    for b in range(2):
                        sp.wait_ge(S[f"x_used{b}"], i)
                        sp.dma_start(x[:, b, :], A["x"][0][bass.ds((2 * i + b) * P, P), :]).then_inc(S[f"x_loaded{b}"], 16)

                with sp.Fori(0, PAIRS - 1) as i:
                    fetch(i)
                    sp.dma_start(w_in_2[:, bass.ds(i, 1), :], src[:, bass.ds(i, 1), :]).then_inc(w_in_2_loaded, 16)
                fetch(PAIRS - 1)

            @block.gpsimd
            def _(pool):
                ch = Chain(pool, S["pool_step"])
                ch.link(nc.gpsimd.memset(neg_half[:, :], -0.5))
                ch.start_over()
                with pool.Fori(0, PAIRS) as i:
                    n = pool.snap(i + 1)
                    for b in range(2):
                        pool.wait_ge(S[f"squares{b}"], n)
                        ch.link(nc.gpsimd.tensor_tensor(st[:, b, 0:1], st[:, b, 0:1], st[:, b, 1:2], ALU.add))
                        ch.link(nc.gpsimd.tensor_scalar(st[:, b, 0:1], st[:, b, 0:1], 1.0 / D, EPS, ALU.mult, ALU.add))
                        nc.gpsimd.tensor_tensor(st[:, b, 2:3], st[:, b, 0:1], neg_half[:, :], ALU.pow).then_inc(S[f"rstd{b}"], 1)
                    ch.start_over()

            @block.tensor
            def _(pe):
                def turn_y(b, n):
                    pe.wait_ge(S[f"y_loaded{b}"], n * 16)
                    for k in range(KD):
                        last = nc.tensor.transpose(B[2 * b + k // 4][:, (k % 4) * P:(k % 4 + 1) * P], y[:, b, k * P:(k + 1) * P], ident[:, :])
                    last.then_inc(S[f"y_turned{b}"], 1)

                turn_y(0, 1)
                pe.wait_ge(S["w_loaded"], 16 * KD)
                for tile in tile_pairs(pe):
                    b, n = tile.b, tile.turn + 1
                    if tile.more:
                        turn_y(1 - b, n + b)
                    pe.wait_ge(S[f"yT_act{b}"], n)
                    pe.wait_ge(S[f"yT_dve{b}"], n)
                    pe.wait_ge(S[f"scaled{b}"], tile.turn)
                    for half in range(2):
                        for k in range(KD):
                            last = nc.tensor.matmul(B[4 + 2 * b + half][:, :], yT[:, b, k, :], w[:, k, half * 512:(half + 1) * 512], start=(k == 0), stop=(k == KD - 1))
                    last.then_inc(S[f"projected{b}"], 1)

            @block.scalar
            def _(act):
                def take_y(b, n):
                    act.wait_ge(S[f"y_turned{b}"], n)
                    nc.scalar.activation(yT[:, b, 0:4, :].rearrange("p a b -> p (a b)"), B[2 * b][:, :], ACT.Copy).then_inc(S[f"yT_act{b}"], 1)

                take_y(0, 1)
                for tile in tile_pairs(act):
                    b, n = tile.b, tile.turn + 1
                    if tile.more:
                        take_y(1 - b, n + b)
                    act.wait_ge(S[f"projected{b}"], n)
                    act.wait_ge(S[f"rstd{b}"], tile.turn)
                    nc.scalar.activation(sq, B[4 + 2 * b][:, :], ACT.Square, accum_out=st[:, b, 0:1]).then_inc(S["act_step"], 1)
                    act.wait_ge(S["act_step"], 1)
                    act.sem_clear(S["act_step"])
                    nc.scalar.activation(sq, B[5 + 2 * b][:, :], ACT.Square, accum_out=st[:, b, 1:2]).then_inc(S[f"squares{b}"], 1)
                    act.wait_ge(S[f"squares{b}"], n)
                    act.wait_ge(S[f"x_used{b}"], n)
                    act.dma_start(x1[bass.ds(tile.t * P, P), :], r[:, b, :]).then_inc(S[f"x1_stored{b}"], 16)
                for b in range(2):
                    act.wait_ge(S[f"x1_stored{b}"], 16 * PAIRS)

            @block.vector
            def _(dve):
                def take_y(b, n):
                    dve.wait_ge(S[f"y_turned{b}"], n)
                    nc.vector.tensor_copy(yT[:, b, 4:8, :].rearrange("p a b -> p (a b)"), B[2 * b + 1][:, :]).then_inc(S[f"yT_dve{b}"], 1)

                dve.wait_ge(S["gate_loaded"], 16)
                take_y(0, 1)
                for tile in tile_pairs(dve):
                    b, n = tile.b, tile.turn + 1
                    if tile.more:
                        take_y(1 - b, n + b)
                    dve.wait_ge(S[f"rstd{b}"], n)
                    dve.wait_ge(S[f"x1_stored{b}"], tile.turn * 16)
                    for half in range(2):
                        c = slice(half * 512, (half + 1) * 512)
                        last = nc.vector.scalar_tensor_tensor(r[:, b, c], B[4 + 2 * b + half][:, :], st[:, b, 2:3], gate_row[:, c], ALU.mult, ALU.mult)
                    last.then_inc(S[f"scaled{b}"], 1)
                    dve.wait_ge(S[f"scaled{b}"], n)
                    dve.wait_ge(S[f"x_loaded{b}"], n * 16)
                    nc.vector.tensor_tensor(r[:, b, :], r[:, b, :], x[:, b, :], ALU.add).then_inc(S[f"x_used{b}"], 1)
        S.close()


A2_HEADS, A2_KV = 8, 2
IDX_HEADS, IDX_DIM = 8, 32
ROT, IDX_ROT = 8, 4
TOPK = 256
POOL_GROUPS = 4
HIST = 16
C2_Q, C2_K, C2_V, C2_QI, C2_KI, C2_ZA, C2_U, C2_ZB, C2_GATES = 0, 512, 640, 768, 1024, 1064, 1576, 2088, 2600
IN2 = 4648
T_QT, T_QI, T_W, T_ZA, T_BT, T_G, T_KT, T_KI, T_V, T_END = 0, 512, 768, 784, 1296, 1808, 3856, 3984, 4112, 4240


def rotary_tables(nc, A, tables):
    NF = ROT + IDX_ROT
    N = TILES * NF
    TWO_PI = 2 * np.pi
    part1 = float(np.float32(6.28125))
    part2 = float(np.float32(int((TWO_PI - part1) * 2 ** 21) / 2 ** 21))
    part3 = float(np.float32(TWO_PI - part1 - part2))
    MAGIC = float(1.5 * 2 ** 23)
    with ExitStack() as ctx:
        sb = lambda n, s, d=F32: ctx.enter_context(nc.sbuf_tensor("ro_" + n, s, d))
        S = Signals(nc, "ro")
        pos_i, pos, freq = sb("pos_i", [P, TILES], I32), sb("pos", [P, TILES]), sb("freq", [P, NF])
        ang, turns, red = sb("ang", [P, TILES, NF]), sb("turns", [P, TILES, NF]), sb("red", [P, 2, TILES, NF])
        with nc.Block() as block:
            @block.sync
            def _(sp):
                sp.dma_start(pos_i[:, :], A["positions_2_ch"]).then_inc(S["loaded"], 16)
                sp.dma_start(freq[:, :], row(A["k_freq"])).then_inc(S["loaded"], 16)

            @block.vector
            def _(dve):
                ch = Chain(dve, S["dve_step"])
                v = nc.vector
                dve.wait_ge(S["loaded"], 32)
                ch.link(v.tensor_copy(pos[:, :], pos_i[:, :]))
                ch.link(v.tensor_tensor(ang[:, :, :], spread(pos[:, :].unsqueeze(2), [P, TILES, NF]),
                                        spread(freq[:, :].unsqueeze(1), [P, TILES, NF]), ALU.mult))
                for which, quarter in ((0, 0.25), (1, 0.0)):
                    r = red[:, which, :, :]
                    ch.link(v.tensor_scalar(turns[:, :, :], ang[:, :, :], 1.0 / TWO_PI, quarter, ALU.mult, ALU.add))
                    ch.link(v.tensor_scalar(turns[:, :, :], turns[:, :, :], MAGIC, None, ALU.add))
                    ch.link(v.tensor_scalar(turns[:, :, :], turns[:, :, :], MAGIC, None, ALU.subtract))
                    ch.link(v.scalar_tensor_tensor(r, turns[:, :, :], -part1, ang[:, :, :], ALU.mult, ALU.add))
                    ch.link(v.scalar_tensor_tensor(r, turns[:, :, :], -part2, r, ALU.mult, ALU.add))
                    ch.link(v.scalar_tensor_tensor(r, turns[:, :, :], -part3, r, ALU.mult, ALU.add))
                    ch.link(v.tensor_scalar(r, r, quarter * TWO_PI, None, ALU.add))
                    for beyond, bound in ((ALU.is_gt, np.pi), (ALU.is_lt, -np.pi)):
                        ch.link(v.tensor_scalar(turns[:, :, :], r, float(bound), -2.0 * float(bound), beyond, ALU.mult))
                        ch.link(v.tensor_tensor(r, r, turns[:, :, :], ALU.add))
                    ch.link(v.tensor_scalar(r, r, 3.1415925, -3.1415925, ALU.min, ALU.max))
                v.memset(pos[:, :], 0.0).then_inc(S["reduced"], 1)

            @block.scalar
            def _(act):
                act.wait_ge(S["reduced"], 1)
                for which in range(2):
                    nc.scalar.activation(tables[:, :, which, :], red[:, which, :, :], ACT.Sin)
        S.close()


def projections(nc, A, x1, w, w_loaded, stage, tables, const):
    ident = const["ident"]
    with ExitStack() as ctx:
        sb = lambda n, s: ctx.enter_context(nc.sbuf_tensor("p2_" + n, s, F32))
        S = Signals(nc, "p2")
        B = [ctx.enter_context(nc.psum_tensor(f"p2_bank{i}", [P, 512], F32)) for i in range(8)]
        g_ch, pscale = sb("g_ch", [P, KD]), sb("pscale", [P, POOL_GROUPS])
        pw = sb("pw", [P, POOL_GROUPS, P])
        mb = sb("mb", [P, 512])
        ones = sb("ones", [P, P])
        qk_g = sb("qk_g", [P, 10, HEAD])
        xt, xn, hTs = sb("xt", [P, D]), sb("xn", [P, D]), sb("hT", [P, 2, KD, P])
        stat, numbers = sb("stat", [P, 2]), sb("numbers", [P, 4, 10])
        NEG_HALF, PER_D, PER_HEAD, EPS_ = range(4)
        pr = sb("pr", [P, C2_ZA])
        qk = sb("qk", [P, 10, HEAD])
        ssq, rsq = sb("ssq", [P, 10]), sb("rsq", [P, 10])
        cs = sb("cs", [P, 2, ROT + IDX_ROT])
        r4 = sb("r4", [P, 4, 10, ROT])
        ki4 = sb("ki4", [P, 4, IDX_DIM])
        u = sb("u", [P, POOL_GROUPS, HIST + P])
        w1, w2 = sb("w1", [P, POOL_GROUPS, HIST + P]), sb("w2", [P, POOL_GROUPS, HIST + P])
        inv = sb("inv", [P, POOL_GROUPS, P])
        zb = sb("zb", [P, POOL_GROUPS, P])
        st = sb("st", [P, T_END])
        flat = lambda ap: ap.rearrange("p a b -> p (a b)")
        with nc.Block() as block:
            @block.sync
            def _(sp):
                load = lambda dst, src: sp.dma_start(dst, src).then_inc(S["weights_loaded"], 16)
                sp.dma_start(xt[:, :], x1[0:P, :]).then_inc(S["x_loaded"], 16)
                k = KD - 1
                sp.dma_start(w[:, k, :], A["w_in_2"][0].rearrange("(k p) n -> p k n", p=P)[:, k, :]).then_inc(w_loaded, 16)
                load(g_ch[:, :], A["norm_g_2_ch"])
                load(pscale[:, :], A["pool_scale_2_ch"])
                load(pw[:, :, :], A["pool_w_2"][0].rearrange("g c d -> c g d"))
                for r in range(4):
                    load(mb[32 * r:32 * r + 1, :], A["merge_bias_2"][0, r // 2:r // 2 + 1, (r % 2) * 512:(r % 2) * 512 + 512])
                load(qk_g[:, 0:8, :], A["q_norm_g_2"].unsqueeze(1).broadcast_to([P, 8, HEAD]))
                load(qk_g[:, 8:10, :], A["k_norm_g_2"].unsqueeze(1).broadcast_to([P, 2, HEAD]))
                load(inv[:, :, :], A["k_inv"][0])
                sp.wait_ge(S["xn_ready"], 1)
                sp.dma_start(xt[:, :], x1[P:2 * P, :]).then_inc(S["x_loaded"], 16)
                sp.wait_ge(S["inv_used"], 1)
                sp.dma_start(inv[:, :, :], A["k_inv"][1]).then_inc(S["inv_ready"], 16)

                def store(t):
                    sp.wait_ge(S["bT_ready"], t + 1)
                    sp.wait_ge(S["gates23_taken"], t + 1)
                    sp.dma_start(stage[bass.ds(t * P, P), :], st[:, :]).then_inc(S["stage_stored"], 16)

                with sp.Fori(0, TILES - 2) as i:
                    store(i)
                    sp.wait_ge(S["xn_ready"], i + 2)
                    sp.dma_start(xt[:, :], x1[bass.ds((i + 2) * P, P), :]).then_inc(S["x_loaded"], 16)
                for t in (TILES - 2, TILES - 1):
                    store(t)
                sp.wait_ge(S["stage_stored"], 16 * TILES)

            N_WEIGHTS = 16 * (3 + 4 + 3)

            @block.gpsimd
            def _(pool):
                ch = Chain(pool, S["pool_step"])
                for at, value in enumerate((-0.5, 1.0 / D, 1.0 / HEAD, EPS)):
                    nc.gpsimd.memset(numbers[:, at, :], value)
                nc.gpsimd.memset(u[:, :, :], 0.0)
                nc.gpsimd.memset(w1[:, :, :], 0.0)
                nc.gpsimd.memset(w2[:, :, :], 0.0)
                ch.link(nc.gpsimd.memset(stat[:, :], 0.0))
                nc.gpsimd.memset(ones[:, :], 1.0).then_inc(S["setup_done"], 1)
                ch.start_over()

                def inv_sqrt(out, sums, n, per):
                    ch.link(nc.gpsimd.tensor_tensor(sums, sums, numbers[:, per, 0:n], ALU.mult))
                    ch.link(nc.gpsimd.tensor_tensor(sums, sums, numbers[:, EPS_, 0:n], ALU.add))
                    return nc.gpsimd.tensor_tensor(out, sums, numbers[:, NEG_HALF, 0:n], ALU.pow)

                def x_norm(n):
                    pool.wait_ge(S["x_squares"], n)
                    inv_sqrt(stat[:, 1:2], stat[:, 0:1], 1, PER_D).then_inc(S["x_rstd"], 1)

                x_norm(1)
                ch.start_over()
                for tile in tile_pairs(pool):
                    n = tile.n
                    if tile.more:
                        x_norm(n + 1)
                    pool.wait_ge(S["qk_squares"], n)
                    inv_sqrt(rsq[:, :], ssq[:, :], 10, PER_HEAD).then_inc(S["qk_rstd"], 1)
                    ch.start_over()

            @block.tensor
            def _(pe):
                mm, tr = nc.tensor.matmul, nc.tensor.transpose
                pe.wait_ge(S["setup_done"], 1)

                def turn_x(n):
                    pe.wait_ge(S["xn_ready"], n)
                    for k in range(KD):
                        last = tr(B[k // 4][:, (k % 4) * P:(k % 4 + 1) * P], xn[:, k * P:(k + 1) * P], ident[:, :])
                    last.then_inc(S["x_turned"], 1)

                turn_x(1)
                pe.wait_ge(w_loaded, 16 * KD)
                pe.wait_ge(S["weights_loaded"], N_WEIGHTS)
                for tile in tile_pairs(pe):
                    i, n, hT = tile.t, tile.n, hTs[:, tile.b]

                    def tokens(out, c, width, name):
                        for k in range(KD):
                            last = mm(out, hT[:, k, :], w[:, k, c:c + width], start=(k == 0), stop=(k == KD - 1))
                        last.then_inc(S[name], 1)

                    def channels(bank, c, name):
                        for m in range(4):
                            for k in range(KD):
                                last = mm(bank[:, m * P:(m + 1) * P], w[:, k, c + m * P:c + (m + 1) * P], hT[:, k, :], start=(k == 0), stop=(k == KD - 1))
                        last.then_inc(S[name], 1)

                    def gate(bank, r, name):
                        for k in range(KD):
                            mm(bank[:, :], hT[:, k, :], w[:, k, C2_GATES + r * 512:C2_GATES + (r + 1) * 512], start=(k == 0), stop=False)
                        mm(bank[:, :], ones[32 * r:32 * r + 1, :], mb[32 * r:32 * r + 1, :], start=False, stop=True).then_inc(S[name], 1)

                    pe.wait_ge(S["hT_act"], n)
                    pe.wait_ge(S["hT_dve"], n)
                    pe.wait_ge(S["kT_taken"], i)
                    tokens(B[5][:, :], C2_ZA, 512, "za_proj")
                    pe.wait_ge(S["gates23_taken"], i)
                    tokens(B[2][:, :], C2_Q, 512, "q_proj")
                    tokens(B[3][:, :], C2_K, 512, "kv_proj")
                    pe.wait_ge(S["qT_taken"], i)
                    tokens(B[4][:, 0:40], C2_KI, 40, "ki_proj")
                    pe.wait_ge(S["bT_ready"], i)
                    channels(B[6], C2_U, "u_proj")
                    channels(B[7], C2_ZB, "zb_proj")
                    gate(B[0], 0, "gate0")
                    gate(B[1], 1, "gate1")
                    pe.wait_ge(S["qk_ready"], n)
                    pe.wait_ge(S["pr_taken"], n)
                    pr_qk = flat(qk[:, :, :])
                    for c in range(4):
                        last = tr(B[4][:, c * P:(c + 1) * P], pr_qk[:, c * P:(c + 1) * P], ident[:, :])
                    last.then_inc(S["q_turned"], 1)
                    pe.wait_ge(S["za_ready"], n)
                    tr(B[5][:, 0:P], pr_qk[:, 512:640], ident[:, :])
                    tr(B[5][:, P:2 * P], flat(ki4[:, :, :]), ident[:, :])
                    for c in range(2):
                        last = tr(B[5][:, (2 + c) * P:(3 + c) * P], pr[:, C2_QI + c * P:C2_QI + (c + 1) * P], ident[:, :])
                    last.then_inc(S["k_turned"], 1)
                    pe.wait_ge(S["pooled_ready"], n)
                    for g in range(POOL_GROUPS):
                        last = mm(B[6][:, g * P:(g + 1) * P], pw[:, g, :], w1[:, g, 0:P], start=True, stop=True)
                    last.then_inc(S["pool_mixed"], 1)
                    if tile.more:
                        pe.wait_ge(S["gates01_taken"], n)
                        turn_x(n + 1)
                    gate(B[2], 2, "gate2")
                    gate(B[3], 3, "gate3")

            @block.scalar
            def _(act):
                f = nc.scalar.activation
                act.wait_ge(S["setup_done"], 1)

                def norm_x(n, t):
                    act.wait_ge(S["x_loaded"], n * 16)
                    act.wait_ge(S["x_turned"], t)
                    f(xn[:, :], xt[:, :], ACT.Square, accum_out=stat[:, 0:1]).then_inc(S["x_squares"], 1)
                    act.wait_ge(S["x_rstd"], n)
                    f(xn[:, :], xt[:, :], ACT.Copy, scale=stat[:, 1:2]).then_inc(S["xn_ready"], 1)

                def take_h(n, hT):
                    act.wait_ge(S["x_turned"], n)
                    for k in range(4):
                        last = f(hT[:, k, :], B[0][:, k * P:(k + 1) * P], ACT.Copy, scale=g_ch[:, k:k + 1])
                    last.then_inc(S["hT_act"], 1)

                norm_x(1, 0)
                act.wait_ge(S["weights_loaded"], N_WEIGHTS)
                take_h(1, hTs[:, 0])
                for tile in tile_pairs(act):
                    i, n = tile.t, tile.n
                    if tile.more:
                        norm_x(n + 1, n)
                    act.wait_ge(S["stage_stored"], i * 16)
                    act.wait_ge(S["za_proj"], n)
                    f(st[:, T_ZA:T_ZA + 512], B[5][:, :], ACT.Sigmoid).then_inc(S["za_sigmoid"], 1)
                    act.wait_ge(S["q_proj"], n)
                    act.wait_ge(S["k_turned"], i)
                    f(pr[:, 0:512], B[2][:, :], ACT.Copy).then_inc(S["q_taken"], 1)
                    act.wait_ge(S["zb_proj"], n)
                    f(flat(zb[:, :, :]), B[7][:, :], ACT.Sigmoid).then_inc(S["zb_sigmoid"], 1)
                    for r in range(2):
                        act.wait_ge(S[f"gate{r}"], n)
                        last = f(st[:, T_G + 512 * r:T_G + 512 * (r + 1)], B[r][:, :], ACT.Sigmoid)
                    last.then_inc(S["gates01_taken"], 1)
                    act.wait_ge(S["q_turned"], n)
                    f(st[:, T_QT:T_QT + 512], B[4][:, :], ACT.Copy).then_inc(S["qT_taken"], 1)
                    if tile.more:
                        take_h(n + 1, hTs[:, 1 - tile.b])
                    for r in range(2, 4):
                        act.wait_ge(S[f"gate{r}"], n)
                        last = f(st[:, T_G + 512 * r:T_G + 512 * (r + 1)], B[r][:, :], ACT.Sigmoid)
                    last.then_inc(S["gates23_taken"], 1)

            @block.vector
            def _(dve):
                ch = Chain(dve, S["dve_step"])
                v = nc.vector
                tt, ts, stt = v.tensor_tensor, v.tensor_scalar, v.scalar_tensor_tensor
                dve.wait_ge(S["weights_loaded"], N_WEIGHTS)
                dve.wait_ge(S["setup_done"], 1)

                def rotate(vectors, cos, sin, half):
                    heads = vectors.shape[1]
                    a, b = vectors[:, :, 0:half], vectors[:, :, half:2 * half]
                    c, s_ = spread(cos.unsqueeze(1), [P, heads, half]), spread(sin.unsqueeze(1), [P, heads, half])
                    t = [r4[:, e, 0:heads, 0:half] for e in range(4)]
                    tt(t[0], a, c, ALU.mult)
                    tt(t[1], b, s_, ALU.mult)
                    tt(t[2], a, s_, ALU.mult)
                    ch.link(tt(t[3], b, c, ALU.mult))
                    tt(a, t[0], t[1], ALU.subtract)
                    return tt(b, t[2], t[3], ALU.add)

                def take_h(n, hT):
                    dve.wait_ge(S["x_turned"], n)
                    for k in range(4, 8):
                        last = ts(hT[:, k, :], B[1][:, (k - 4) * P:(k - 3) * P], g_ch[:, k:k + 1], None, ALU.mult)
                    last.then_inc(S["hT_dve"], 1)

                take_h(1, hTs[:, 0])
                for tile in tile_pairs(dve):
                    i, n = tile.t, tile.n
                    v.tensor_copy(cs[:, :, :], tables[:, bass.ds(i, 1), :, :].rearrange("p a b c -> p (a b) c"))
                    dve.wait_ge(S["kv_proj"], n)
                    dve.wait_ge(S["k_turned"], i)
                    v.tensor_copy(pr[:, 512:1024], B[3][:, :])
                    dve.wait_ge(S["ki_proj"], n)
                    v.tensor_copy(pr[:, 1024:1064], B[4][:, 0:40]).then_inc(S["pr_taken"], 1)
                    dve.wait_ge(S["q_taken"], n)
                    dve.wait_ge(S["pr_taken"], n)
                    ch.link(tt(flat(qk[:, :, :]), pr[:, 0:640], pr[:, 0:640], ALU.mult))
                    v.tensor_reduce(ssq[:, :], qk[:, :, :], AX.X, ALU.add).then_inc(S["qk_squares"], 1)
                    ch.link(rotate(pr[:, C2_QI:C2_QI + 9 * IDX_DIM].rearrange("p (h d) -> p h d", d=IDX_DIM), cs[:, 0, ROT:], cs[:, 1, ROT:], IDX_ROT))
                    v.tensor_copy(ki4[:, :, :], spread(pr[:, C2_KI:C2_KI + IDX_DIM].unsqueeze(1), [P, 4, IDX_DIM]))
                    dve.wait_ge(S["stage_stored"], i * 16)
                    v.tensor_copy(st[:, T_V:T_V + P], pr[:, C2_V:C2_V + P])
                    wi, mag, sgn = pr[:, 1056:1064], st[:, T_W:T_W + 8], st[:, T_W + 8:T_W + 16]
                    ch.link(stt(mag, wi, -1.0, wi, ALU.mult, ALU.max))
                    ch.link(ts(mag, mag, 1.0 / 16.0, None, ALU.mult))
                    ch.link(ts(sgn, wi, 0.0, 2.0, ALU.is_ge, ALU.mult))
                    ch.link(ts(sgn, sgn, -1.0, None, ALU.add))
                    dve.wait_ge(S["qk_rstd"], n)
                    q_in = pr[:, 0:512].rearrange("p (g c d) -> p g c d", g=2, c=4)
                    q_out = flat(qk[:, 0:8, :]).rearrange("p (c g d) -> p g c d", g=2, c=4)
                    for g in range(2):
                        tt(q_out[:, g], q_in[:, g], spread(rsq[:, 4 * g:4 * g + 4].unsqueeze(2), [P, 4, HEAD]), ALU.mult)
                    ch.link(tt(qk[:, 8:10, :], pr[:, 512:640].rearrange("p (h d) -> p h d", d=HEAD), spread(rsq[:, 8:10].unsqueeze(2), [P, 2, HEAD]), ALU.mult))
                    ch.link(tt(flat(qk[:, :, :]), flat(qk[:, :, :]), flat(qk_g[:, :, :]), ALU.mult))
                    rotate(qk[:, :, :], cs[:, 0, 0:ROT], cs[:, 1, 0:ROT], ROT).then_inc(S["qk_ready"], 1)
                    dve.wait_ge(S["u_proj"], n)
                    dve.wait_ge(S["pool_mixed"], i)
                    ch.link(v.tensor_copy(u[:, :, HIST:], B[6][:, :].rearrange("p (g t) -> p g t", t=P)))
                    E = HIST + P
                    ch.link(tt(w1[:, :, 1:E], u[:, :, 1:E], u[:, :, 0:E - 1], ALU.add))
                    ch.link(tt(w2[:, 1:4, 3:E], w1[:, 1:4, 3:E], w1[:, 1:4, 1:E - 2], ALU.add))
                    ch.link(tt(w1[:, 2:4, 7:E], w2[:, 2:4, 7:E], w2[:, 2:4, 3:E - 4], ALU.add))
                    ch.link(tt(w2[:, 3:4, 15:E], w1[:, 3:4, 15:E], w1[:, 3:4, 7:E - 8], ALU.add))
                    for g, full in enumerate((w1, w2, w1, w2)):
                        last = tt(w2[:, g, HIST:], full[:, g, HIST:], inv[:, g, :], ALU.mult)
                    last.then_inc(S["inv_used"], 1)
                    dve.wait_ge(S["inv_used"], n)
                    tt(w1[:, :, 0:P], w2[:, :, HIST:], u[:, :, HIST:], ALU.subtract).then_inc(S["pooled_ready"], 1)
                    dve.wait_ge(S["pooled_ready"], n)
                    ch.link(v.tensor_copy(u[:, :, 0:HIST], u[:, :, P:P + HIST]))
                    dve.wait_ge(S["zb_sigmoid"], n)
                    ch.link(tt(flat(zb[:, :, :]), B[7][:, :], flat(zb[:, :, :]), ALU.mult))
                    dve.wait_ge(S["za_sigmoid"], n)
                    tt(st[:, T_ZA:T_ZA + 512], B[5][:, :], st[:, T_ZA:T_ZA + 512], ALU.mult).then_inc(S["za_ready"], 1)
                    dve.wait_ge(S["k_turned"], n)
                    v.tensor_copy(st[:, T_KT:T_KT + 2 * P], B[5][:, 0:2 * P])
                    v.tensor_copy(st[:, T_QI:T_QI + 256], B[5][:, 256:512]).then_inc(S["kT_taken"], 1)
                    dve.wait_ge(S["pool_mixed"], n)
                    for g in range(POOL_GROUPS):
                        last = stt(st[:, T_BT + g * P:T_BT + (g + 1) * P], B[6][:, g * P:(g + 1) * P], pscale[:, g:g + 1], zb[:, g, :], ALU.mult, ALU.mult)
                    last.then_inc(S["bT_ready"], 1)
                    if tile.more:
                        take_h(n + 1, hTs[:, 1 - tile.b])
                    dve.wait_ge(S["inv_ready"], 16)
                    ch.start_over()
        S.close()
BLK = 512
GROUP = BLK // P
HALVINGS = 25
BIG = 8.0e30
LEAST = 1.0e-30
WHOLE = TOPK // P


class Turn:

    def __init__(self, blocks, a, b, in_group, units_a, units_b, late):
        self.late = late
        fixed = isinstance(a, int)
        self.search = a is not None and not (fixed and a < WHOLE)
        self.first_search = fixed and a == WHOLE
        self.blocks, self.a, self.b, self.in_group = blocks, a, b, in_group
        self.units_a, self.units_b = units_a, units_b
        self.width = blocks * BLK


def turns(eng):
    yield Turn(1, 0, None, 0, 0, 0, False)
    for a in range(1, GROUP):
        yield Turn(1, a, a - 1, a, 8 * max(a - WHOLE, 0), 8 * (a - 1), a >= 2)
    units_a, units_b = 8 * (GROUP - WHOLE), 8 * (GROUP - 1)
    for g in range(1, TILES // GROUP):
        per = 8 * (g + 1)
        with eng.Fori(0, GROUP) as i:
            yield Turn(g + 1, eng.snap(i + g * GROUP), eng.snap(i + (g * GROUP - 1)), i + 0,
                       i * per + units_a, i * per + units_b, True)
        units_a, units_b = units_a + GROUP * per, units_b + GROUP * per
    yield Turn(TILES // GROUP, None, TILES - 1, 0, 0, units_b, True)


def attention(nc, A, x1, stage, out, const):
    ident = const["ident"]
    with ExitStack() as ctx:
        sb = lambda n, s: ctx.enter_context(nc.sbuf_tensor("at_" + n, s, F32))
        S = Signals(nc, "at")
        B = [ctx.enter_context(nc.psum_tensor(f"at_bank{i}", [P, 512], F32)) for i in range(8)]
        LOGIT, SCORE, TURNED, OUT = B[0:2], (B[2], B[3], B[7]), B[4:6], B[6]
        READY = len(SCORE)
        KT, KI, VC = sb("KT", [P, SEQ]), sb("KI", [P, SEQ]), sb("VC", [P, TILES, P])
        wa, wb, wo = sb("wa", [P, 4, D]), sb("wb", [P, 4, D]), sb("wo", [P, KD, D])
        halves, allowed = sb("halves", [P, HALVINGS]), sb("allowed", [P, BLK + 3 * P])
        ones = sb("ones", [P, 1])
        qi, qT = sb("qi", [P, IDX_HEADS, P]), sb("qT", [P, A2_HEADS, P])
        wi = sb("wi", [P, 16])
        rest = sb("rest", [P, T_KT - T_ZA])
        x = sb("x", [P, D])
        r = sb("r", [P, 4, BLK])
        acc, bias = sb("acc", [P, SEQ]), sb("bias", [P, SEQ])
        tie, run = sb("tie", [P, SEQ]), sb("run", [P, SEQ])
        over = bias
        mid, cnt, width = sb("mid", [P, 4]), sb("cnt", [P, 4]), sb("width", [P, HALVINGS])
        s = sb("s", [P, 2, SEQ])
        pT = sb("pT", [P, 2, TILES, P])
        mx, nm, den = sb("mx", [P, 2, 4]), sb("nm", [P, 8]), sb("den", [P, 8])
        at, aT = sb("a", [P, 512]), sb("aT", [P, 4, P])
        y, yT, o = sb("y", [P, D]), sb("yT", [P, KD, P]), sb("o", [P, D])
        za, bT = rest[:, 0:512], rest[:, T_BT - T_ZA:T_G - T_ZA]
        gates = rest[:, T_G - T_ZA:T_KT - T_ZA]
        flat = lambda ap: ap.rearrange("p a b -> p (a b)")
        rows_of = lambda t: bass.ds(t * P, P)
        FIRST_STEPS = 1
        LATE_STEP = 6
        SEARCH_STEPS = 8 - FIRST_STEPS
        tests = [0] * FIRST_STEPS + [HALVINGS * (e + 1) // SEARCH_STEPS - HALVINGS * e // SEARCH_STEPS for e in range(SEARCH_STEPS)]

        with nc.Block() as block:
            @block.sync
            def _(sp):
                load = lambda name, dst, src: sp.dma_start(dst, src).then_inc(S[name], 16)
                by_tile = stage.rearrange("(t p) c -> p t c", p=P)

                def fetch_queries(t):
                    if not t.first_search:
                        sp.wait_ge(S["index_done"], t.a - WHOLE)
                    src = stage[rows_of(t.a), :]
                    for q in range(4):
                        sp.dma_start(qi[32 * q:32 * q + 32, q::4, :], src[32 * q:32 * q + 32, T_QI:T_W].rearrange("p (h t) -> p h t", t=P)).then_inc(S["qi_loaded"], 16)
                    sp.dma_start(wi[:, :], src[:, T_W:T_ZA]).then_inc(S["qi_loaded"], 16)

                sp.wait_ge(S["queries_cleared"], 1)
                for t in turns(sp):
                    if t.b is None:
                        load("search_loaded", allowed[:, :], A["k_allowed"])
                        load("search_loaded", halves[:, :], row(A["k_halves"]))
                        load("KT_loaded", KT[:, :].rearrange("p (t c) -> p t c", c=P), by_tile[:, :, T_KT:T_KT + P])
                        load("V_loaded", VC[:, :, :], by_tile[:, :, T_V:T_V + P])
                        load("KI_loaded", KI[:, :].rearrange("p (t c) -> p t c", c=P), by_tile[:, :, T_KI:T_KI + P])
                    if t.search:
                        fetch_queries(t)
                    if t.b is not None:
                        if t.late:
                            sp.wait_ge(S["pv_done"], t.b * 8)
                        src = stage[rows_of(t.b), :]
                        for g in range(A2_KV):
                            sp.dma_start(qT[64 * g:64 * g + 64, 4 * g:4 * g + 4, :], src[64 * g:64 * g + 64, T_QT:T_QI].rearrange("p (h t) -> p h t", t=P)).then_inc(S["qT_loaded"], 16)
                        if t.late:
                            sp.wait_ge(S["y_ready"], t.b)
                        sp.dma_start(rest[:, :], stage[rows_of(t.b), T_ZA:T_KT]).then_inc(S["rest_loaded"], 16)
                        if t.late:
                            sp.wait_ge(S["out_ready"], t.b)
                        sp.dma_start(x[:, :], x1[rows_of(t.b), :]).then_inc(S["x_loaded"], 16)
                        if not t.late:
                            for name, dst in (("w_branch_b_2", wb), ("w_branch_a_2", wa), ("w_out_2", wo)):
                                load(name, dst[:, :, :], A[name][0].rearrange("(k p) n -> p k n", p=P))

            @block.gpsimd
            def _(pool):
                ch = Chain(pool, S["pool_step"])
                nc.gpsimd.memset(qi[:, :, :], 0.0)
                nc.gpsimd.memset(qT[:, :, :], 0.0).then_inc(S["queries_cleared"], 1)
                nc.gpsimd.memset(bias[:, :], -BIG)
                ch.link(nc.gpsimd.memset(mid[:, :], 0.0))
                nc.gpsimd.memset(ones[:, :], 1.0).then_inc(S["setup_done"], 1)
                for t in turns(pool):
                    if t.late:
                        pool.wait_ge(S["out_ready"], t.b)
                        pool.dma_start(out[rows_of(t.b - 1), :], o[:, :]).then_inc(S["out_stored"], 16)
                pool.wait_ge(S["out_ready"], TILES)
                pool.dma_start(out[rows_of(TILES - 1), :], o[:, :]).then_inc(S["out_stored"], 16)
                pool.wait_ge(S["out_stored"], 16 * TILES)

            @block.tensor
            def _(pe):
                mm, tr = nc.tensor.matmul, nc.tensor.transpose
                for t in turns(pe):
                    n = t.blocks
                    if t.b is None:
                        continue
                    if t.first_search:
                        pe.wait_ge(S["KI_loaded"], 16)
                    if not t.late:
                        pe.wait_ge(S["KT_loaded"], 16)

                    def project(quarter):
                        half, first = quarter // 2, quarter % 2 * KD // 2
                        for k in range(first, first + KD // 2):
                            last = mm(LOGIT[half][:, :], yT[:, k, :], wo[:, k, half * 512:(half + 1) * 512], start=(k == 0), stop=(k == KD - 1))
                        if quarter == 3:
                            last.then_inc(S["projected"], 1)

                    def index_products(h):
                        for kb in range(n):
                            j = h * n + kb
                            if not (isinstance(t.units_a, int) and t.units_a + j < 2):
                                pe.wait_ge(S["relu_done"], t.units_a + (j - 1))
                            mm(LOGIT[j % 2][:, :], qi[:, h, :], KI[:, kb * BLK:(kb + 1) * BLK],
                               start=True, stop=True).then_inc(S["logits"], 1)

                    def score_products(h, blocks):
                        for kb in blocks:
                            j = h * n + kb
                            pe.wait_ge(S["masked"], t.units_b + (j + 1))
                            mm(SCORE[j % READY][:, :], qT[:, h, :], KT[:, kb * BLK:(kb + 1) * BLK], start=True, stop=True).then_inc(S["scores"], 1)

                    def turn_probabilities(h):
                        pe.wait_ge(S["probs"], t.b * 8 + (h + 1))
                        for kb in range(n):
                            j = h * n + kb
                            pe.wait_ge(S["pT_taken"], t.units_b + (j + 1))
                            for e in range(GROUP):
                                last = tr(TURNED[j % 2][:, e * P:(e + 1) * P], s[:, h % 2, kb * BLK + e * P:kb * BLK + (e + 1) * P], ident[:, :])
                            last.then_inc(S["probs_turned"], 1)

                    def values(h):
                        if not t.late:
                            pe.wait_ge(S["V_loaded"], 16)
                        pe.wait_ge(S["pT_taken"], t.units_b + ((h + 1) * n + 2))
                        for kt in range(GROUP * n):
                            last = mm(OUT[:, h * 64:(h + 1) * 64], pT[:, h % 2, kt, :], VC[:, kt, 64 * (h // 4):64 * (h // 4) + 64],
                                      start=(kt == 0), stop=(kt == GROUP * n - 1))
                        last.then_inc(S["pv_done"], 1)

                    if t.search:
                        pe.wait_ge(S["qi_loaded"], (t.a - WHOLE) * 80 + 80)
                    if t.b is not None:
                        pe.wait_ge(S["qT_loaded"], t.b * 32 + 32)
                        if t.late:
                            pe.wait_ge(S["yT_ready"], t.b)
                        score_products(0, range(n))
                    for h in range(8):
                        if t.search and h < FIRST_STEPS:
                            for e in range(h * 8 // FIRST_STEPS, (h + 1) * 8 // FIRST_STEPS):
                                index_products(e)
                        if t.b is None:
                            continue
                        if h == LATE_STEP + 1:
                            pe.wait_ge(S["rest_loaded"], t.b * 16 + 16)
                            if t.late:
                                pe.wait_ge(S["out_ready"], t.b)
                            else:
                                pe.wait_ge(S["w_branch_b_2"], 16)
                            for half in range(2):
                                for k in range(4):
                                    mm(LOGIT[half][:, :], bT[:, k * P:(k + 1) * P], wb[:, k, half * 512:(half + 1) * 512], start=(k == 0), stop=(k == 3))
                        if t.late and LATE_STEP - 4 <= h < LATE_STEP:
                            if t.search and h == LATE_STEP - 4:
                                pe.wait_ge(S["relu_done"], t.units_a + 8 * n)
                            project(h - (LATE_STEP - 4))
                        if h < 7:
                            score_products(h + 1, range(n)[:READY])
                        turn_probabilities(h)
                        if h > 0:
                            values(h - 1)
                        if h < 7:
                            score_products(h + 1, range(n)[READY:])
                    if t.b is None:
                        continue
                    values(7)
                    pe.wait_ge(S["a_ready"], t.b + 1)
                    for c in range(4):
                        last = tr(TURNED[0][:, c * P:(c + 1) * P], at[:, c * P:(c + 1) * P], ident[:, :])
                    last.then_inc(S["a_turned"], 1)
                    if not t.late:
                        pe.wait_ge(S["w_branch_a_2"], 16)
                        pe.wait_ge(S["w_out_2"], 16)
                    pe.wait_ge(S["aT_ready"], t.b + 1)
                    for half in range(2):
                        for k in range(4):
                            last = mm(SCORE[half][:, :], aT[:, k, :], wa[:, k, half * 512:(half + 1) * 512], start=(k == 0), stop=(k == 3))
                    last.then_inc(S["branches_done"], 1)
                    pe.wait_ge(S["y_ready"], t.b + 1)
                    for k in range(KD):
                        last = tr(SCORE[k // 4][:, (k % 4) * P:(k % 4 + 1) * P], y[:, k * P:(k + 1) * P], ident[:, :])
                    last.then_inc(S["y_turned"], 1)
                    if t.a is None:
                        pe.wait_ge(S["yT_ready"], t.b + 1)
                        for quarter in range(4):
                            project(quarter)

            @block.scalar
            def _(act):
                f = nc.scalar.activation
                act.sem_inc(S["pT_taken"], 2)
                for t in turns(act):
                    n = t.blocks
                    if t.search:
                        act.wait_ge(S["qi_loaded"], (t.a - WHOLE) * 80 + 80)

                    def index_relu(h):
                        for kb in range(n):
                            j = h * n + kb
                            act.wait_ge(S["logits"], t.units_a + (j + 1))
                            if not (isinstance(t.units_a, int) and t.units_a + j < 4):
                                act.wait_ge(S["summed"], t.units_a + (j - 3))
                            f(r[:, j % 4, :], LOGIT[j % 2][:, :], ACT.Relu, scale=wi[:, h:h + 1]).then_inc(S["relu_done"], 1)

                    for h in range(8):
                        if t.b is not None:
                            act.wait_ge(S["row_max"], t.b * 8 + (h + 1))
                            f(s[:, h % 2, 0:t.width], s[:, h % 2, 0:t.width], ACT.Exp, bias=nm[:, h:h + 1], accum_out=den[:, h:h + 1]).then_inc(S["probs"], 1)
                        if t.search and h < FIRST_STEPS:
                            for e in range(h * 8 // FIRST_STEPS, (h + 1) * 8 // FIRST_STEPS):
                                index_relu(e)
                        if t.b is not None:
                            if h >= 2:
                                act.wait_ge(S["pv_done"], t.b * 8 + (h - 1))
                            for kb in range(n):
                                j = h * n + kb
                                act.wait_ge(S["probs_turned"], t.units_b + (j + 1))
                                f(flat(pT[:, h % 2, kb * GROUP:(kb + 1) * GROUP, :]), TURNED[j % 2][:, :], ACT.Copy).then_inc(S["pT_taken"], 1)
                    if t.b is not None:
                        act.wait_ge(S["a_turned"], t.b + 1)
                        f(flat(aT[:, :, :]), TURNED[0][:, :], ACT.Copy).then_inc(S["aT_ready"], 1)
                        act.wait_ge(S["y_turned"], t.b + 1)
                        f(flat(yT[:, 0:4, :]), SCORE[0][:, :], ACT.Copy)
                        f(flat(yT[:, 4:8, :]), SCORE[1][:, :], ACT.Copy).then_inc(S["yT_ready"], 1)

            @block.vector
            def _(dve):
                ch = Chain(dve, S["dve_step"])
                v = nc.vector
                tt, ts, stt = v.tensor_tensor, v.tensor_scalar, v.scalar_tensor_tensor
                dve.sem_inc(S["masked"], READY)
                dve.wait_ge(S["search_loaded"], 32)
                dve.wait_ge(S["setup_done"], 1)
                for t in turns(dve):
                    n, L = t.blocks, t.width

                    def index_sum(h):
                        sgn = wi[:, 8 + h:9 + h]
                        for kb in range(n):
                            j = h * n + kb
                            dve.wait_ge(S["relu_done"], t.units_a + (j + 1))
                            part = acc[:, kb * BLK:(kb + 1) * BLK]
                            if h == 0:
                                last = ts(part, r[:, j % 4, :], sgn, None, ALU.mult)
                            else:
                                dve.wait_ge(S["summed"], t.units_a + (j - n + 1))
                                last = stt(part, r[:, j % 4, :], sgn, part, ALU.mult, ALU.add)
                            last.then_inc(S["summed"], 1)

                    def search_range():
                        dve.wait_ge(S["summed"], t.units_a + 8 * n)
                        ch.link(v.tensor_reduce(cnt[:, 1:2], acc[:, 0:L], AX.X, ALU.max, apply_absolute_value=True))
                        ch.link(ts(cnt[:, 1:2].bitcast(I32), cnt[:, 1:2].bitcast(I32), 0x7f800000, None, ALU.bitwise_and))
                        ch.link(ts(cnt[:, 1:2], cnt[:, 1:2], 2.0, LEAST, ALU.mult, ALU.max))
                        ts(width[:, :], halves[:, :], cnt[:, 1:2], None, ALU.mult)
                        v.memset(mid[:, 0:1], 0.0)
                        start = t.in_group * (-P) + 3 * P
                        last_block = acc[:, L - BLK:L]
                        tt(last_block, last_block, allowed[:, bass.ds(start, BLK)], ALU.add).then_inc(S["index_done"], 1)
                        dve.wait_ge(S["index_done"], t.a - (WHOLE - 1))

                    def halve(k):
                        ch.link(ts(run[:, 0:L], acc[:, 0:L], mid[:, 0:1], 0.0, ALU.is_ge, ALU.add, accum_out=cnt[:, 0:1]))
                        if k < HALVINGS - 1:
                            ch.link(ts(cnt[:, 2:3], cnt[:, 0:1], TOPK - 0.5, -0.5, ALU.is_ge, ALU.add))
                            ch.link(stt(mid[:, 0:1], cnt[:, 2:3], width[:, k:k + 1], mid[:, 0:1], ALU.mult, ALU.add))
                        else:
                            ch.link(ts(cnt[:, 2:3], cnt[:, 0:1], TOPK - 0.5, -1.0, ALU.is_ge, ALU.add))
                            ch.link(stt(mid[:, 1:2], cnt[:, 2:3], width[:, k:k + 1], mid[:, 0:1], ALU.mult, ALU.add))
                            ch.link(tt(mid[:, 2:3], mid[:, 1:2], width[:, k:k + 1], ALU.add))

                    def candidates():
                        lo, hi = mid[:, 1:2], mid[:, 2:3]
                        ts(tie[:, 0:L], acc[:, 0:L], lo, None, ALU.is_ge)
                        ch.link(ts(over[:, 0:L], acc[:, 0:L], hi, 0.0, ALU.is_ge, ALU.add, accum_out=cnt[:, 0:1]))
                        ch.link(tt(tie[:, 0:L], tie[:, 0:L], over[:, 0:L], ALU.subtract))
                        ch.link(ts(cnt[:, 3:4], cnt[:, 0:1], -1.0, float(TOPK), ALU.mult, ALU.add))

                    def select():
                        ch.link(v.tensor_tensor_scan(run[:, 0:L], spread(ones[:, :], [P, L]), tie[:, 0:L], 0.0, ALU.mult, ALU.add))
                        ch.link(stt(tie[:, 0:L], run[:, 0:L], cnt[:, 3:4], tie[:, 0:L], ALU.is_le, ALU.mult))
                        ch.link(tt(tie[:, 0:L], tie[:, 0:L], over[:, 0:L], ALU.add))
                        ch.link(ts(bias[:, 0:L], tie[:, 0:L], BIG, -BIG, ALU.mult, ALU.add))

                    def mask(h):
                        if h >= 2:
                            dve.wait_ge(S["probs_turned"], t.units_b + (h - 1) * n)
                        for kb in range(n):
                            j = h * n + kb
                            c = slice(kb * BLK, (kb + 1) * BLK)
                            dve.wait_ge(S["scores"], t.units_b + (j + 1))
                            dve.sem_inc(S["score_seen"], 1)
                            v.tensor_tensor_reduce(out=s[:, h % 2, c], in0=SCORE[j % READY][:, :], in1=bias[:, c], scale=HEAD ** -0.5, scalar=-3.0e38,
                                                   op0=ALU.add, op1=ALU.max, accum_out=mx[:, h % 2, kb:kb + 1]).then_inc(S["masked"], 1)
                        dve.wait_ge(S["masked"], t.units_b + ((h + 1) * n + READY))
                        ch.link(v.tensor_reduce(nm[:, h:h + 1], mx[:, h % 2, 0:n], AX.X, ALU.max))
                        ts(nm[:, h:h + 1], nm[:, h:h + 1], -1.0, None, ALU.mult).then_inc(S["row_max"], 1)

                    if t.search:
                        dve.wait_ge(S["qi_loaded"], (t.a - WHOLE) * 80 + 80)

                    def finish(n):
                        dve.wait_ge(S["projected"], n)
                        dve.wait_ge(S["x_loaded"], n * 16)
                        for half in range(2):
                            c = slice(half * 512, (half + 1) * 512)
                            last = tt(o[:, c], LOGIT[half][:, :], x[:, c], ALU.add)
                        last.then_inc(S["out_ready"], 1)

                    done = 0
                    for h in range(8):
                        if t.b is not None:
                            mask(h)
                        if t.search:
                            if h < FIRST_STEPS:
                                for e in range(h * 8 // FIRST_STEPS, (h + 1) * 8 // FIRST_STEPS):
                                    index_sum(e)
                            if h == FIRST_STEPS:
                                search_range()
                        if t.late and h == LATE_STEP:
                            finish(t.b)
                        if t.search:
                            for _k in range(tests[h]):
                                halve(done)
                                done += 1
                    if t.b is not None:
                        dve.wait_ge(S["pv_done"], t.b * 8 + 8)
                        ch.link(v.reciprocal(den[:, :], den[:, :]))
                        hd = lambda ap: ap.rearrange("p (h d) -> p h d", d=HEAD)
                        ch.link(tt(hd(at[:, :]), hd(OUT[:, :]), spread(den[:, :].unsqueeze(2), [P, 8, HEAD]), ALU.mult))
                        dve.wait_ge(S["rest_loaded"], t.b * 16 + 16)
                        tt(at[:, :], at[:, :], za, ALU.mult).then_inc(S["a_ready"], 1)
                    if t.search:
                        candidates()
                    if t.b is not None:
                        dve.wait_ge(S["branches_done"], t.b + 1)
                        if t.late:
                            dve.wait_ge(S["out_stored"], t.b * 16)
                        for half in range(2):
                            c = slice(half * 512, (half + 1) * 512)
                            tt(y[:, c], SCORE[half][:, :], gates[:, half * 512:(half + 1) * 512], ALU.mult)
                            last = tt(o[:, c], LOGIT[half][:, :], gates[:, 1024 + half * 512:1024 + (half + 1) * 512], ALU.mult)
                        ch.link(last)
                        tt(y[:, :], y[:, :], o[:, :], ALU.add).then_inc(S["y_ready"], 1)
                        dve.wait_ge(S["y_ready"], t.b + 1)
                    if t.search:
                        select()
                    elif t.a is not None:
                        start = 3 * P - t.in_group * P
                        ts(bias[:, 0:BLK], allowed[:, start:start + BLK], -BIG / NEG, None, ALU.mult).then_inc(S["reach_taken"], 1)
                        dve.wait_ge(S["reach_taken"], t.a + 1)
                    if t.a is None:
                        finish(t.b + 1)
                    ch.start_over()
        S.close()


def build(nc, A, out):
    with ExitStack() as ctx:
        sb = lambda n, s: ctx.enter_context(nc.sbuf_tensor(n, s, F32))
        dram = lambda n, s: nc.dram_tensor(n, s, F32, kind="Internal").ap()
        const = dict(ident=sb("ident", [P, P]))
        keep = dict(scale_ch=sb("scale_ch", [P, KD]), shift_ch=sb("shift_ch", [P, KD]), gate_row=dram("gate_row", (P, D)))
        stage1, mixed = dram("stage1", (SEQ, M_END)), dram("mixed", (SEQ, D))
        x1, stage = dram("x1", (SEQ, D)), dram("stage", (SEQ, T_END))
        identity_loaded, w_in_loaded, w_in_2_loaded = map(nc.alloc_semaphore, ("identity_loaded", "w_in_loaded", "w_in_2_loaded"))
        with nc.Block() as block:
            @block.sync
            def _(sp):
                sp.dma_start(const["ident"][:, :], A["k_ident"]).then_inc(identity_loaded, 16)
                sp.wait_ge(identity_loaded, 16)
        with nc.sbuf_tensor("tables", [P, TILES, 2, ROT + IDX_ROT], F32) as tables:
            with nc.sbuf_tensor("w_in", [P, KD, IN1], F32) as w_in:
                adaptive_norm(nc, A, w_in, w_in_loaded, keep, const)
                rotary_tables(nc, A, tables)
                mixer_projections(nc, A, w_in, w_in_loaded, stage1, keep, const)
            mixers(nc, A, stage1, mixed, const)
            with nc.sbuf_tensor("w_in_2", [P, KD, IN2], F32) as w_in_2:
                output_and_residual(nc, A, mixed, x1, w_in_2, w_in_2_loaded, keep, const)
                projections(nc, A, x1, w_in_2, w_in_2_loaded, stage, tables, const)
        attention(nc, A, x1, stage, out, const)


def shape_constants():
    s, t = np.arange(P)[:, None], np.arange(P)[None]
    masks = np.zeros((P, LEVELS, P), np.float32)
    for level in range(LEVELS):
        half = 1 << level
        masks[:, level] = (s // (2 * half) == t // (2 * half)) & (t // half % 2 == 1) & (s // half % 2 == 0)
    one_chunk = s // R_CHUNK == t // R_CHUNK
    tri = np.stack([(s < t) & one_chunk, (s <= t) & one_chunk], axis=1).astype(np.float32)
    quad = (s // G_KEY == np.arange(R_W)[None] // G_VAL).astype(np.float32)
    chunk_of = (s // R_CHUNK == np.arange(2)[None]).astype(np.float32)
    dist = np.arange(P)[:, None] - np.arange(2 * P)[None] + P
    slopes = (2.0 ** -np.arange(1, A_HEADS + 1)).astype(np.float32)
    alibi = np.where(((dist >= 0) & (dist < P))[:, None, :], -slopes[None, :, None] * dist[:, None, :].astype(np.float32), NEG)
    freq8 = ["0x1p+0", "0x1.8d275ep-3", "0x1.34119p-5", "0x1.ddee9cp-8", "0x1.72ba44p-10", "0x1.1f91fp-12", "0x1.be2188p-15", "0x1.5a0f4ep-17"]
    freq = np.array([[float.fromhex(f) for f in freq8 + freq8[::2]]], np.float32)
    inv = np.zeros((2, P, POOL_GROUPS, P), np.float32)
    for g, w in enumerate((2, 4, 8, 16)):
        inv[0, :, g], inv[1, :, g] = 1.0 / np.minimum(np.arange(P) + 1, w), 1.0 / w
    reach = np.arange(BLK + 3 * P)[None] - 3 * P
    allowed = np.where(reach < 64 * (np.arange(P)[:, None] >= 64) + 64, 0.0, NEG)
    return {
        "k_ident": np.eye(P, dtype=np.float32), "k_masks": masks, "k_tri": tri,
        "k_pair": (s // HEAD == t // HEAD).astype(np.float32), "k_quad": quad, "k_chunk_of": chunk_of,
        "k_alibi": alibi.astype(np.float32), "k_freq": freq, "k_inv": inv, "k_allowed": allowed.astype(np.float32),
        "k_halves": (2.0 ** -np.arange(HALVINGS))[None].astype(np.float32),
    }


def kernel(**inputs):
    import concourse.bacc as bacc
    from concourse.bass_utils import run_bass_kernel_spmd as run

    nc = bacc.Bacc("TRN2", target_bir_lowering=False, num_devices=1)
    arrays = {}
    by_column = ("c", "ada_b", "norm_pre", "gla_gk_b", "rwkv_mu_w", "rwkv_mu_a", "rwkv_mu_rkv", "norm_g_2", "pool_scale_2", "positions_2")
    only_so = ("c", "norm_pre", "gla_gk_b", "rwkv_mu_w", "rwkv_mu_a", "rwkv_mu_rkv", "norm_g_2", "pool_scale_2", "positions_2")
    for name, value in inputs.items():
        a = np.ascontiguousarray(value)
        if name in by_column:
            arrays[name + "_ch"] = np.ascontiguousarray(a.reshape(-1, P).T)
        if name not in only_so:
            arrays[name] = a
    arrays.update(shape_constants())
    A, fed = {}, {}
    for name, a in arrays.items():
        fed["in_" + name] = a
        A[name] = nc.dram_tensor("in_" + name, a.shape, mybir.dt.from_np(a.dtype), kind="ExternalInput").ap()
    out = nc.dram_tensor("out", (1, SEQ, D), F32, kind="ExternalOutput").ap()
    build(nc, A, out[0])
    return run(nc, [fed], core_ids=[0]).results[0]["out"]
```
